# Optimizing a Trainium2 kernel written in Bass

```python
import jax, jax.numpy as jnp
from jax import lax
import numpy as np

D_MODEL = 1024
BATCH = 1
SEQ = 256
DEPTH = 2

HEAD_DIM = 64
A_HEADS = 8
A_KV = 2
B_HEADS = 8
B_KV = 2
C_HEADS = 16
D_FF = 2816
GRID_W = 64
Q_BLOCK = 128
WINDOW = 128
NA_KH = 8
NA_KW = 16
ROPE_THETA = 10000.0
EPS = 1e-6
EVEN_IN = (A_HEADS + 2 * A_KV + B_HEADS + 2 * B_KV) * HEAD_DIM
EVEN_OUT = (A_HEADS + B_HEADS) * HEAD_DIM
ODD_IN = 3 * C_HEADS * HEAD_DIM
ODD_OUT = C_HEADS * HEAD_DIM
NEG_INF = -1e30


def rms_norm(x, g):
    xf = x.astype(jnp.float32)
    y = xf * lax.rsqrt(jnp.mean(xf * xf, axis=-1, keepdims=True) + EPS)
    return (y * g.astype(jnp.float32)).astype(x.dtype)

def swiglu(h, w_gate, w_up, w_down):
    return (jax.nn.silu(h @ w_gate) * (h @ w_up)) @ w_down

def rope_cos_sin(pos, dim):
    inv = ROPE_THETA ** (-jnp.arange(0, dim, 2, dtype=jnp.float32) / dim)
    ang = pos.astype(jnp.float32)[:, None] * inv[None, :]
    return jnp.cos(ang), jnp.sin(ang)

def apply_rope(x, cos, sin):
    half = x.shape[-1] // 2
    c = cos[None, :, None, :].astype(x.dtype)
    s = sin[None, :, None, :].astype(x.dtype)
    x1, x2 = x[..., :half], x[..., half:]
    return jnp.concatenate([x1 * c - x2 * s, x1 * s + x2 * c], axis=-1)

def apply_axial_rope(x, cos_r, sin_r, cos_c, sin_c):
    half = x.shape[-1] // 2
    return jnp.concatenate([apply_rope(x[..., :half], cos_r, sin_r),
                            apply_rope(x[..., half:], cos_c, sin_c)], axis=-1)

def global_gqa(q, k, v):
    bsz, s_len, h, d = q.shape
    kv = k.shape[2]
    g = h // kv
    nb = s_len // Q_BLOCK
    scale = HEAD_DIM ** -0.5
    qb = q.reshape(bsz, nb, Q_BLOCK, kv, g, d).transpose(1, 0, 2, 3, 4, 5)

    def block(qi):
        s = jnp.einsum('bqkgd,bskd->bkgqs', qi, k, preferred_element_type=jnp.float32) * scale
        p = jax.nn.softmax(s, axis=-1).astype(v.dtype)
        return jnp.einsum('bkgqs,bskd->bqkgd', p, v)

    o = lax.map(block, qb)
    return o.transpose(1, 0, 2, 3, 4, 5).reshape(bsz, s_len, h * d)

def windowed_gqa_sink(q, k, v, sink):
    bsz, s_len, h, d = q.shape
    kv = k.shape[2]
    g = h // kv
    nb = s_len // Q_BLOCK
    scale = HEAD_DIM ** -0.5
    qb = q.reshape(bsz, nb, Q_BLOCK, kv, g, d)
    pad = ((0, 0), (Q_BLOCK, Q_BLOCK), (0, 0), (0, 0))
    kb = jnp.pad(k, pad).reshape(bsz, nb + 2, Q_BLOCK, kv, d)
    vb = jnp.pad(v, pad).reshape(bsz, nb + 2, Q_BLOCK, kv, d)
    k_slab = jnp.concatenate([kb[:, :-2], kb[:, 1:-1], kb[:, 2:]], axis=2)
    v_slab = jnp.concatenate([vb[:, :-2], vb[:, 1:-1], vb[:, 2:]], axis=2)
    s = jnp.einsum('bnqkgd,bnskd->bnkgqs', qb, k_slab, preferred_element_type=jnp.float32) * scale
    blk = jnp.arange(nb)[:, None, None] * Q_BLOCK
    qpos = blk + jnp.arange(Q_BLOCK)[None, :, None]
    kpos = blk - Q_BLOCK + jnp.arange(3 * Q_BLOCK)[None, None, :]
    valid = (jnp.abs(qpos - kpos) <= WINDOW) & (kpos >= 0) & (kpos < s_len)
    s = jnp.where(valid[None, :, None, None], s, NEG_INF)
    sk = sink.astype(jnp.float32).reshape(kv, g)[None, None, :, :, None]
    m = jnp.maximum(jnp.max(s, axis=-1), sk)
    p = jnp.exp(s - m[..., None])
    denom = jnp.sum(p, axis=-1) + jnp.exp(sk - m)
    p = (p / denom[..., None]).astype(v.dtype)
    o = jnp.einsum('bnkgqs,bnskd->bnqkgd', p, v_slab)
    return o.reshape(bsz, s_len, h * d)

def neighbourhood_attention(q, k, v, rel_bias, rows):
    bsz, s_len, h, d = q.shape
    kh = min(NA_KH, rows)
    kw = NA_KW
    scale = HEAD_DIM ** -0.5
    qg = q.reshape(bsz, rows, GRID_W, h, d)
    kg = k.reshape(bsz, rows, GRID_W, h, d)
    vg = v.reshape(bsz, rows, GRID_W, h, d)
    cols = jnp.arange(GRID_W)
    col_start = jnp.clip(cols - kw // 2, 0, GRID_W - kw)
    col_idx = col_start[:, None] + jnp.arange(kw)[None, :]
    col_bias_idx = col_idx - cols[:, None] + (NA_KW - 1)

    def row_fn(args):
        q_r, r = args
        rs = jnp.clip(r - kh // 2, 0, rows - kh)
        k_rows = lax.dynamic_slice_in_dim(kg, rs, kh, axis=1)
        v_rows = lax.dynamic_slice_in_dim(vg, rs, kh, axis=1)
        k_win = k_rows[:, :, col_idx]
        v_win = v_rows[:, :, col_idx]
        row_bias_idx = rs + jnp.arange(kh) - r + (NA_KH - 1)
        bias = rel_bias[:, row_bias_idx[:, None, None], col_bias_idx[None, :, :]]
        s = jnp.einsum('bchd,bacwhd->bhcaw', q_r, k_win, preferred_element_type=jnp.float32) * scale
        s = s + bias.transpose(0, 2, 1, 3)[None].astype(jnp.float32)
        p = jax.nn.softmax(s.reshape(bsz, h, GRID_W, kh * kw), axis=-1)
        p = p.reshape(s.shape).astype(v.dtype)
        return jnp.einsum('bhcaw,bacwhd->bchd', p, v_win)

    o = lax.map(row_fn, (qg.transpose(1, 0, 2, 3, 4), jnp.arange(rows)))
    return o.transpose(1, 0, 2, 3, 4).reshape(bsz, s_len, h * d)

def even_mixer(h, w_in, q_gain, k_gain, sink, w_out, rope1, rope_axial):
    bsz, s_len, _ = h.shape
    proj = h @ w_in
    sizes = [A_HEADS * HEAD_DIM, A_KV * HEAD_DIM, A_KV * HEAD_DIM,
             B_HEADS * HEAD_DIM, B_KV * HEAD_DIM, B_KV * HEAD_DIM]
    cuts = list(np.cumsum(sizes)[:-1])
    qa, ka, va, qb, kb, vb = jnp.split(proj, cuts, axis=-1)
    hd = lambda t: t.reshape(bsz, s_len, -1, HEAD_DIM)
    qa, ka, va, qb, kb, vb = map(hd, (qa, ka, va, qb, kb, vb))
    qa = apply_axial_rope(rms_norm(qa, q_gain), *rope_axial)
    ka = apply_axial_rope(rms_norm(ka, k_gain), *rope_axial)
    oa = global_gqa(qa, ka, va)
    qb = apply_rope(qb, *rope1)
    kb = apply_rope(kb, *rope1)
    ob = windowed_gqa_sink(qb, kb, vb, sink)
    return jnp.concatenate([oa, ob], axis=-1) @ w_out

def odd_mixer(h, w_qkv, rel_bias, w_out, rows):
    bsz, s_len, _ = h.shape
    q, k, v = jnp.split(h @ w_qkv, 3, axis=-1)
    q = q.reshape(bsz, s_len, C_HEADS, HEAD_DIM)
    k = k.reshape(bsz, s_len, C_HEADS, HEAD_DIM)
    v = v.reshape(bsz, s_len, C_HEADS, HEAD_DIM)
    return neighbourhood_attention(q, k, v, rel_bias, rows) @ w_out

def first_inputs(seed: int = 0) -> dict:
    key = jax.random.key(seed)
    ks = iter(jax.random.split(key, 32))
    f32 = jnp.float32
    n_even = (DEPTH + 1) // 2
    n_odd = DEPTH // 2

    def w(shape, fan_in):
        return jax.random.normal(next(ks), shape, f32) * (fan_in ** -0.5)

    def gain(shape):
        return 1.0 + 0.1 * jax.random.normal(next(ks), shape, f32)

    return {
        "x": jax.random.normal(next(ks), (BATCH, SEQ, D_MODEL), f32),
        "ffn1_norm": gain((DEPTH, D_MODEL)),
        "ffn1_w_gate": w((DEPTH, D_MODEL, D_FF), D_MODEL),
        "ffn1_w_up": w((DEPTH, D_MODEL, D_FF), D_MODEL),
        "ffn1_w_down": w((DEPTH, D_FF, D_MODEL), D_FF),
        "mix_norm": gain((DEPTH, D_MODEL)),
        "ffn2_norm": gain((DEPTH, D_MODEL)),
        "ffn2_w_gate": w((DEPTH, D_MODEL, D_FF), D_MODEL),
        "ffn2_w_up": w((DEPTH, D_MODEL, D_FF), D_MODEL),
        "ffn2_w_down": w((DEPTH, D_FF, D_MODEL), D_FF),
        "even_w_in": w((n_even, D_MODEL, EVEN_IN), D_MODEL),
        "a_q_norm": gain((n_even, HEAD_DIM)),
        "a_k_norm": gain((n_even, HEAD_DIM)),
        "b_sink": 0.5 * jax.random.normal(next(ks), (n_even, B_HEADS), f32),
        "even_w_out": w((n_even, EVEN_OUT, D_MODEL), EVEN_OUT),
        "odd_w_qkv": w((n_odd, D_MODEL, ODD_IN), D_MODEL),
        "c_rel_bias": 0.1 * jax.random.normal(next(ks), (n_odd, C_HEADS, 2 * NA_KH - 1, 2 * NA_KW - 1), f32),
        "odd_w_out": w((n_odd, ODD_OUT, D_MODEL), ODD_OUT),
        "final_norm": gain((D_MODEL,)),
    }

def first_block(x, ffn1_norm, ffn1_w_gate, ffn1_w_up, ffn1_w_down, mix_norm,
              ffn2_norm, ffn2_w_gate, ffn2_w_up, ffn2_w_down,
              even_w_in, a_q_norm, a_k_norm, b_sink, even_w_out,
              odd_w_qkv, c_rel_bias, odd_w_out, final_norm):
    s_len = x.shape[1]
    rows = s_len // GRID_W
    pos = jnp.arange(s_len)
    rope1 = rope_cos_sin(pos, HEAD_DIM)
    cos_r, sin_r = rope_cos_sin(pos // GRID_W, HEAD_DIM // 2)
    cos_c, sin_c = rope_cos_sin(pos % GRID_W, HEAD_DIM // 2)
    rope_axial = (cos_r, sin_r, cos_c, sin_c)
    for layer in range(DEPTH):
        i = layer // 2
        h = rms_norm(x, ffn1_norm[layer])
        x = x + 0.5 * swiglu(h, ffn1_w_gate[layer], ffn1_w_up[layer], ffn1_w_down[layer])
        h = rms_norm(x, mix_norm[layer])
        if layer % 2 == 0:
            x = x + even_mixer(h, even_w_in[i], a_q_norm[i], a_k_norm[i], b_sink[i],
                               even_w_out[i], rope1, rope_axial)
        else:
            x = x + odd_mixer(h, odd_w_qkv[i], c_rel_bias[i], odd_w_out[i], rows)
        h = rms_norm(x, ffn2_norm[layer])
        x = x + 0.5 * swiglu(h, ffn2_w_gate[layer], ffn2_w_up[layer], ffn2_w_down[layer])
    return rms_norm(x, final_norm)


DEPTH_2 = 1

N_ATTN_HEADS = 8
ATTN_HEAD_DIM = 64
ATTN_WIDTH = N_ATTN_HEADS * ATTN_HEAD_DIM
N_REC_HEADS = 4
REC_HEAD_DIM = 128
REC_WIDTH = N_REC_HEADS * REC_HEAD_DIM
D_MIX = ATTN_WIDTH + REC_WIDTH
IN_COLS = 3 * ATTN_WIDTH + N_ATTN_HEADS + 4 * REC_WIDTH
SPLIT_POINTS = (ATTN_WIDTH, 2 * ATTN_WIDTH, 3 * ATTN_WIDTH,
                3 * ATTN_WIDTH + N_ATTN_HEADS,
                3 * ATTN_WIDTH + N_ATTN_HEADS + REC_WIDTH,
                3 * ATTN_WIDTH + N_ATTN_HEADS + 2 * REC_WIDTH,
                3 * ATTN_WIDTH + N_ATTN_HEADS + 3 * REC_WIDTH)
CONV_WIDTH = 3
FOX_BLOCK = 128
HGRN_CHUNK = 64
LN_EPS = 1e-5
RMS_EPS = 1e-6
DEEPNORM_ALPHA = (2.0 * DEPTH_2) ** 0.25
DEEPNORM_BETA = (8.0 * DEPTH_2) ** -0.25


def _layer_norm(x, g, b):
    xf = x.astype(jnp.float32)
    mu = jnp.mean(xf, axis=-1, keepdims=True)
    var = jnp.mean(jnp.square(xf - mu), axis=-1, keepdims=True)
    y = (xf - mu) * lax.rsqrt(var + LN_EPS)
    return (y * g.astype(jnp.float32) + b.astype(jnp.float32)).astype(x.dtype)

def _rms_norm_heads(x, g):
    xf = x.astype(jnp.float32)
    y = xf * lax.rsqrt(jnp.mean(jnp.square(xf), axis=-1, keepdims=True) + RMS_EPS)
    return y * g.astype(jnp.float32)

def _fox_attention(q, k, v, logf):
    B, H, S, D = q.shape
    n_blocks = S // FOX_BLOCK
    c = jnp.cumsum(logf.astype(jnp.float32), axis=-1)
    qf = q.astype(jnp.float32) * (D ** -0.5)
    kf = k.astype(jnp.float32)
    vf = v.astype(jnp.float32)
    q_blocks = qf.reshape(B, H, n_blocks, FOX_BLOCK, D).transpose(2, 0, 1, 3, 4)
    c_blocks = c.reshape(B, H, n_blocks, FOX_BLOCK).transpose(2, 0, 1, 3)
    key_pos = jnp.arange(S)

    def block(args):
        q_i, c_i, i = args
        s = jnp.einsum('bhqd,bhkd->bhqk', q_i, kf) + c_i[..., :, None] - c[..., None, :]
        q_pos = i * FOX_BLOCK + jnp.arange(FOX_BLOCK)
        s = jnp.where(key_pos[None, :] <= q_pos[:, None], s, -jnp.inf)
        p = jax.nn.softmax(s, axis=-1)
        return jnp.einsum('bhqk,bhkd->bhqd', p, vf)

    o = lax.map(block, (q_blocks, c_blocks, jnp.arange(n_blocks)))
    return o.transpose(1, 2, 0, 3, 4).reshape(B, H, S, D)

def _hgrn2_chunked(q, k, v, logf):
    B, H, S, DK = q.shape
    DV = v.shape[-1]
    C = HGRN_CHUNK
    n_chunks = S // C

    def to_chunks(t):
        return t.astype(jnp.float32).reshape(B, H, n_chunks, C, t.shape[-1]).transpose(2, 0, 1, 3, 4)

    qc, kc, vc, gc = to_chunks(q), to_chunks(k), to_chunks(v), to_chunks(logf)
    b = jnp.cumsum(gc, axis=-2)
    causal = jnp.tril(jnp.ones((C, C), dtype=bool))

    def step(state, inp):
        q_i, k_i, v_i, b_i = inp
        diff = b_i[..., :, None, :] - b_i[..., None, :, :]
        decay = jnp.where(causal[:, :, None], jnp.exp(jnp.minimum(diff, 0.0)), 0.0)
        scores = jnp.einsum('bhtd,bhsd,bhtsd->bhts', q_i, k_i, decay)
        o = jnp.einsum('bhts,bhse->bhte', scores, v_i) \
            + jnp.einsum('bhtd,bhde->bhte', q_i * jnp.exp(b_i), state)
        b_last = b_i[..., -1:, :]
        state = jnp.exp(b_last[..., 0, :])[..., None] * state \
            + jnp.einsum('bhsd,bhse->bhde', k_i * jnp.exp(b_last - b_i), v_i)
        return state, o

    state0 = jnp.zeros((B, H, DK, DV), jnp.float32)
    _, o = lax.scan(step, state0, (qc, kc, vc, b))
    return o.transpose(1, 2, 0, 3, 4).reshape(B, H, S, DV)

def _causal_depthwise_conv(h, w, bias):
    S = h.shape[1]
    hp = jnp.pad(h, ((0, 0), (CONV_WIDTH - 1, 0), (0, 0)))
    y = bias
    for j in range(CONV_WIDTH):
        y = y + w[j] * hp[:, j:j + S, :]
    return y

def second_inputs(seed: int = 0) -> dict:
    key = jax.random.key(seed)
    ks = jax.random.split(key, 17)

    def nrm(k, shape, scale):
        return jax.random.normal(k, shape, jnp.float32) * scale

    col_scale = jnp.concatenate([
        jnp.ones((2 * ATTN_WIDTH,), jnp.float32),
        jnp.full((ATTN_WIDTH,), DEEPNORM_BETA, jnp.float32),
        jnp.ones((N_ATTN_HEADS + 2 * REC_WIDTH,), jnp.float32),
        jnp.full((REC_WIDTH,), DEEPNORM_BETA, jnp.float32),
        jnp.ones((REC_WIDTH,), jnp.float32)])

    return {
        'x': nrm(ks[0], (BATCH, SEQ, D_MODEL), 1.0),
        'ln_emb_g': 1.0 + nrm(ks[1], (D_MODEL,), 0.05),
        'ln_emb_b': nrm(ks[2], (D_MODEL,), 0.02),
        'w_in': nrm(ks[3], (DEPTH_2, D_MODEL, IN_COLS), D_MODEL ** -0.5) * col_scale,
        'fox_f_bias': 1.0 + nrm(ks[4], (DEPTH_2, N_ATTN_HEADS), 0.1),
        'fox_norm_g': 1.0 + nrm(ks[5], (DEPTH_2, ATTN_WIDTH), 0.05),
        'hgrn_lower_bounds': nrm(ks[6], (DEPTH_2, REC_WIDTH), 0.1),
        'hgrn_norm_g': 1.0 + nrm(ks[7], (DEPTH_2, REC_WIDTH), 0.05),
        'w_o': nrm(ks[8], (DEPTH_2, D_MIX, D_MODEL), D_MIX ** -0.5 * DEEPNORM_BETA),
        'ln_mix_g': 1.0 + nrm(ks[9], (DEPTH_2, D_MODEL), 0.05),
        'ln_mix_b': nrm(ks[10], (DEPTH_2, D_MODEL), 0.02),
        'w_up': nrm(ks[11], (DEPTH_2, D_MODEL, 2 * D_FF), D_MODEL ** -0.5 * DEEPNORM_BETA),
        'conv_w': nrm(ks[12], (DEPTH_2, CONV_WIDTH, 2 * D_FF), CONV_WIDTH ** -0.5),
        'conv_b': nrm(ks[13], (DEPTH_2, 2 * D_FF), 0.02),
        'w_down': nrm(ks[14], (DEPTH_2, D_FF, D_MODEL), D_FF ** -0.5 * DEEPNORM_BETA),
        'ln_ffn_g': 1.0 + nrm(ks[15], (DEPTH_2, D_MODEL), 0.05),
        'ln_ffn_b': nrm(ks[16], (DEPTH_2, D_MODEL), 0.02),
    }

def second_block(x, ln_emb_g, ln_emb_b, w_in, fox_f_bias, fox_norm_g, hgrn_lower_bounds,
              hgrn_norm_g, w_o, ln_mix_g, ln_mix_b, w_up, conv_w, conv_b, w_down,
              ln_ffn_g, ln_ffn_b):
    B, S, _ = x.shape
    dtype = x.dtype

    lb_sm = jax.nn.softmax(hgrn_lower_bounds.astype(jnp.float32), axis=0)
    lb_cum = jnp.cumsum(lb_sm, axis=0)
    lower_bounds = lb_cum - lb_cum[0:1]

    def heads(t, n_heads):
        return t.reshape(B, S, n_heads, -1).transpose(0, 2, 1, 3)

    x = _layer_norm(x, ln_emb_g, ln_emb_b)

    for l in range(DEPTH_2):
        proj = x @ w_in[l]
        q_a, k_a, v_a, f_a, q_r, f_r, i_r, g_r = jnp.split(proj, SPLIT_POINTS, axis=-1)

        logf_a = jax.nn.log_sigmoid((f_a + fox_f_bias[l]).astype(jnp.float32)).transpose(0, 2, 1)
        o_a = _fox_attention(heads(q_a, N_ATTN_HEADS), heads(k_a, N_ATTN_HEADS),
                             heads(v_a, N_ATTN_HEADS), logf_a)
        o_a = _rms_norm_heads(o_a.transpose(0, 2, 1, 3),
                              fox_norm_g[l].reshape(N_ATTN_HEADS, ATTN_HEAD_DIM))
        o_a = o_a.reshape(B, S, ATTN_WIDTH)

        lb = lower_bounds[l]
        logf_r = jnp.logaddexp(jnp.log(lb),
                               jnp.log1p(-lb) + jax.nn.log_sigmoid(f_r.astype(jnp.float32)))
        k_r = -jnp.expm1(logf_r)
        o_r = _hgrn2_chunked(heads(jax.nn.silu(q_r), N_REC_HEADS), heads(k_r, N_REC_HEADS),
                             heads(i_r, N_REC_HEADS), heads(logf_r, N_REC_HEADS))
        o_r = _rms_norm_heads(o_r.transpose(0, 2, 1, 3),
                              hgrn_norm_g[l].reshape(N_REC_HEADS, REC_HEAD_DIM))
        o_r = o_r.reshape(B, S, REC_WIDTH) * jax.nn.silu(g_r.astype(jnp.float32))

        mix = jnp.concatenate([o_a, o_r], axis=-1).astype(dtype) @ w_o[l]
        x = _layer_norm(DEEPNORM_ALPHA * x + mix, ln_mix_g[l], ln_mix_b[l])

        h = _causal_depthwise_conv(x @ w_up[l], conv_w[l], conv_b[l])
        a, u = jnp.split(h, 2, axis=-1)
        ffn = (jax.nn.gelu(a, approximate=False) * u) @ w_down[l]
        x = _layer_norm(DEEPNORM_ALPHA * x + ffn, ln_ffn_g[l], ln_ffn_b[l])

    return x


def setup_inputs(seed=0):
    out = dict(first_inputs(seed))
    for name, value in second_inputs(seed + 1).items():
        if name != "x":
            out[name + "_2"] = value
    return out


def reference(
    x, ffn1_norm, ffn1_w_gate, ffn1_w_up, ffn1_w_down, mix_norm, ffn2_norm, ffn2_w_gate,
    ffn2_w_up, ffn2_w_down, even_w_in, a_q_norm, a_k_norm, b_sink, even_w_out, odd_w_qkv,
    c_rel_bias, odd_w_out, final_norm, ln_emb_g_2, ln_emb_b_2, w_in_2, fox_f_bias_2,
    fox_norm_g_2, hgrn_lower_bounds_2, hgrn_norm_g_2, w_o_2, ln_mix_g_2, ln_mix_b_2, w_up_2,
    conv_w_2, conv_b_2, w_down_2, ln_ffn_g_2, ln_ffn_b_2,
):
    x = first_block(
        x, ffn1_norm, ffn1_w_gate, ffn1_w_up, ffn1_w_down, mix_norm, ffn2_norm, ffn2_w_gate,
        ffn2_w_up, ffn2_w_down, even_w_in, a_q_norm, a_k_norm, b_sink, even_w_out, odd_w_qkv,
        c_rel_bias, odd_w_out, final_norm,
    )
    return second_block(
        x, ln_emb_g_2, ln_emb_b_2, w_in_2, fox_f_bias_2, fox_norm_g_2, hgrn_lower_bounds_2,
        hgrn_norm_g_2, w_o_2, ln_mix_g_2, ln_mix_b_2, w_up_2, conv_w_2, conv_b_2, w_down_2,
        ln_ffn_g_2, ln_ffn_b_2,
    )


_drawn_inputs = setup_inputs


def setup_inputs(seed=0):
    import zlib

    import numpy as np

    out = dict(_drawn_inputs(seed))
    spreads = {}
    factors = {'a_q_norm': 6.509,
     'a_k_norm': 7.196,
     'b_sink': 8.0,
     'c_rel_bias': 3.087,
     'fox_f_bias_2': 4.666,
     'fox_norm_g_2': 3.433,
     'hgrn_norm_g_2': 6.089,
     'ln_mix_b_2': 2.846,
     'conv_b_2': 8.0,
     'ln_ffn_b_2': 2.737}
    for name, (base, spread) in spreads.items():
        noise = np.random.default_rng([zlib.crc32(name.encode()), seed]).standard_normal(out[name].shape)
        drawn = base * np.exp(spread * noise) if base else spread * noise
        out[name] = __import__('jax').numpy.asarray(drawn.astype(out[name].dtype))
    for name, factor in factors.items():
        out[name] = (out[name] * factor).astype(out[name].dtype)
    return out
```

```python
from contextlib import ExitStack

import numpy as np

import concourse.bass as bass
from concourse import mybir

F32 = mybir.dt.float32
F32R = mybir.dt.float32r
I32 = mybir.dt.int32
U32 = mybir.dt.uint32
ACT = mybir.ActivationFunctionType
ALU = mybir.AluOpType
AX_X = mybir.AxisListType.X

P = 128
S = 256
TB = S // P
DM = 1024
KC = DM // P
FF = 2816
UNIT = 2048
RING = 3
LOOKAHEAD = 2
FF_STEPS = FF // 256
EPS_RMS = 1e-6
EPS_LN = 1e-5
ALPHA = 2.0 ** 0.25
NEG = -1e30
HD = 64
SCALE = HD ** -0.5
GRID_W = 64
NA_KW = 16
REL_W = 2 * NA_KW - 1
REL_H = 15
LEVELS = (32, 16, 8, 4, 2, 1)
RSQRT_MAGIC = 1597463007.0

C_IDENT = 0
C_ROPE = C_IDENT + P
C_WIN = C_ROPE + 4 * TB * HD
C_NB = C_WIN + TB * S
C_CAUSAL = C_NB + S
C_LEVEL = C_CAUSAL + TB * S
C_ZERO = C_LEVEL + 64 * len(LEVELS)
C_SEL = C_ZERO + 64
C_N = C_SEL + 8 * P


def constant_table():
    t = np.zeros((P, C_N), np.float32)
    t[:, C_IDENT:C_IDENT + P] = np.eye(P, dtype=np.float32)
    pos = np.arange(S)

    def angles(at, dim):
        inv = (np.float32(10000.0) ** (-np.arange(0, dim, 2, dtype=np.float32) / np.float32(dim))).astype(np.float32)
        a = (at.astype(np.float32)[:, None] * inv[None, :]).astype(np.float32).astype(np.float64)
        return np.cos(a).astype(np.float32), np.sin(a).astype(np.float32)

    cr, sr = angles(pos // GRID_W, HD // 2)
    cc, sc = angles(pos % GRID_W, HD // 2)
    c1, s1 = angles(pos, HD)
    rope = [np.concatenate([cr, cr, cc, cc], 1), np.concatenate([-sr, sr, -sc, sc], 1),
            np.concatenate([c1, c1], 1), np.concatenate([-s1, s1], 1)]
    for n, r in enumerate(rope):
        for tb in range(TB):
            at = C_ROPE + (n * TB + tb) * HD
            t[:, at:at + HD] = r[tb * P:(tb + 1) * P]
    key = np.arange(S)[None, :]
    for tb in range(TB):
        q = tb * P + np.arange(P)[:, None]
        t[:, C_WIN + tb * S:C_WIN + (tb + 1) * S] = np.where(np.abs(q - key) <= 128, 0, 8 * NEG)
        t[:, C_CAUSAL + tb * S:C_CAUSAL + (tb + 1) * S] = np.where(key <= q, 0, 8 * NEG)
    c = np.arange(P)[:, None] % GRID_W
    first = np.clip(c - NA_KW // 2, 0, GRID_W - NA_KW)
    kc = key % GRID_W
    kc = GRID_W - 1 - kc
    t[:, C_NB:C_NB + S] = np.where((kc >= first) & (kc < first + NA_KW), 0, 8 * NEG)
    s = np.arange(P)[:, None]
    for n, m in enumerate(LEVELS):
        late = np.array([x for x in range(P) if x % (2 * m) >= m])[None, :]
        ok = (s // (2 * m) == late // (2 * m)) & (s % (2 * m) < m)
        t[:, C_LEVEL + 64 * n:C_LEVEL + 64 * (n + 1)] = ok
    for h in range(8):
        t[h, C_SEL + h * P:C_SEL + (h + 1) * P] = 1
    return t


def build(nc, io, out):
    ctx = ExitStack()
    with ctx:
        def sb(name, shape, dt=F32):
            return ctx.enter_context(nc.sbuf_tensor(name, shape, dt))

        def sem(name):
            return ctx.enter_context(nc.semaphore(name))

        raw = [sb(f"raw{n}", [P, UNIT]) for n in range(RING)]
        w_hi = [sb(f"w_hi{n}", [P, UNIT], F32R) for n in range(RING)]
        w_lo = [sb(f"w_lo{n}", [P, UNIT], F32R) for n in range(RING)]
        X = sb("x_tok", [P, TB, DM])
        XN = sb("xn_tok", [P, TB, DM])
        T = sb("t_feat", [P, KC, S])
        h_hi = sb("h_hi", [P, KC, S], F32R)
        h_lo = sb("h_lo", [P, KC, S], F32R)
        gu_hi = sb("gu_hi", [P, 2, S], F32R)
        gu_lo = sb("gu_lo", [P, 2, S], F32R)
        consts = sb("consts", [P, C_SEL])
        rowvec = sb("rowvec", [P, 2, DM])
        QKT = sb("qk_feat", [P, 16, S])
        V = sb("v_tok", [P, TB, DM])
        s_sb = sb("s_sb", [P, 2, 512])
        p_sb = sb("p_sb", [P, 2, 512])
        pt_sb = sb("pt_sb", [P, 2, 2, S])
        arena = sb("arena", [P, 8192])
        cols = sb("cols", [P, 56])
        convc = sb("convc", [P, 4, 44])
        ss = sb("ss", [P, 24])
        nt = sb("nt", [P, 4, 24])
        mx = sb("mx", [P, 16, 2])
        negm = sb("negm", [P, 16, 2])
        rsum = sb("rsum", [P, 16, 2])
        rinv = sb("rinv", [P, 16, 2])
        esink = sb("esink", [P, 8, 2])
        sink = sb("sink", [P, 8])
        fbias = sb("fbias", [8, 1])
        bn = sb("bn", [P, TB, 2, 6])
        mv = sb("mv", [P, TB, 2])
        cq = sb("cq", [P, TB, 8])
        PS = ctx.enter_context(nc.psum_tensor("ps", [P, 8, 512], F32))

        ident = consts[:, C_IDENT:C_IDENT + P]

        def rope_tab(n, tb):
            at = C_ROPE + (n * TB + tb) * HD
            return consts[:, at:at + HD]

        win_mask = consts[:, C_WIN:C_WIN + TB * S].rearrange("p (t k) -> p t k", t=TB)
        nb_mask = consts[:, C_NB:C_NB + S]
        causal_mask = consts[:, C_CAUSAL:C_CAUSAL + TB * S].rearrange("p (t k) -> p t k", t=TB)
        zeros = consts[:, C_ZERO:C_ZERO + 64]

        ffn_act = s_sb[:, 0, :]
        ffn_up = s_sb[:, 1, :]
        ffn_gu = p_sb[:, 0, :]
        PJ = arena[:, 0:3072].rearrange("p (t n) -> p t n", t=TB)
        R = arena[:, 3072:5632].rearrange("p (t n) -> p t n", t=TB)
        rope_t1 = arena[:, 5632:6912].rearrange("p (b n) -> p b n", b=2)
        rope_t2 = arena[:, 6912:8192].rearrange("p (b n) -> p b n", b=2)
        qk_gain = QKT[:, 10:13, :].rearrange("p a b -> p (a b)")[:, 0:640]
        bias = arena[:, :].rearrange("p (h t k) -> p h t k", h=16, t=TB)
        fox_bias = arena[:, 0:4096].rearrange("p (h t k) -> p h t k", h=8, t=TB)
        hg_b = arena[:, 4096:5120].rearrange("p (h t) -> p h t", h=4)
        hg_k = arena[:, 5120:6144].rearrange("p (h t) -> p h t", h=4)
        hg_d = arena[:, 6144:7168].rearrange("p (h t) -> p h t", h=4)
        hg_gate = arena[:, 7168:8192].rearrange("p (t n) -> p t n", t=TB)
        hg_e = arena[:, 0:1024].rearrange("p (h t) -> p h t", h=4)
        hg_kh = arena[:, 1024:2048].rearrange("p (h t) -> p h t", h=4)
        hg_qh = arena[:, 2048:3072].rearrange("p (h t) -> p h t", h=4)
        hg_st = arena[:, 3072:4096].rearrange("p (b t) -> p b t", b=8)
        hg_s2 = T[:, 0:2, :].rearrange("p a b -> p (a b)").rearrange("p (h t) -> p h t", h=4)
        hg_q = QKT[:, 8:12, :]
        hg_f = QKT[:, 12:16, :]
        wf = s_sb[:, 0, 0:64].rearrange("p (k n) -> p k n", k=KC)
        sel = V[0:8, 0, :].rearrange("p (h q) -> p h q", h=8)
        f_z = p_sb[0:8, 0, 0:256]
        f_a = p_sb[0:8, 0, 256:512]
        f_m = p_sb[0:8, 1, 0:256]
        f_c = p_sb[0:8, 1, 256:512]

        w_landed = [sem(f"w_landed{n}") for n in range(RING)]
        w_hi_ready = sem("w_hi_ready")
        w_lo_ready = sem("w_lo_ready")
        w_released = sem("w_released")
        FFN_UNITS = 3 * FF_STEPS
        sizes = [("ffn1_0", FFN_UNITS), ("even_in", 6), ("even_out", 4), ("ffn2_0", FFN_UNITS),
                 ("ffn1_1", FFN_UNITS), ("odd_in", 12), ("odd_out", 4), ("ffn2_1", FFN_UNITS),
                 ("rec_in", 14), ("rec_out", 4), ("conv_ffn", FFN_UNITS)]
        first_unit, total = {}, 0
        for name, n in sizes:
            first_unit[name] = total
            total += n
        TOTAL_UNITS = total

        def split_hi(act, n, i=0):
            if isinstance(i, int) and n + 3 * i >= TOTAL_UNITS:
                return
            slot = n % RING
            act.wait_ge(w_landed[slot], 16 * i + 16 * (n // RING + 1))
            if n >= RING:
                act.wait_ge(w_released, 3 * i + (n - RING + 1))
            act.activation(w_hi[slot][:, :], raw[slot][:, :], ACT.Copy).then_inc(w_hi_ready, 1)

        def split_lo(dve, n, i=0):
            if isinstance(i, int) and n + 3 * i >= TOTAL_UNITS:
                return
            slot = n % RING
            dve.wait_ge(w_hi_ready, 3 * i + (n + 1))
            dve.tensor_tensor(w_lo[slot][:, :], raw[slot][:, :], w_hi[slot][:, :].bitcast(F32),
                              ALU.subtract).then_inc(w_lo_ready, 1)

        def load_unit(sp, n, src, view, i=0):
            slot = n % RING
            if n >= RING:
                sp.wait_ge(w_lo_ready, 3 * i + (n - RING + 1))
            sp.dma_start(view(raw[slot]), src).then_inc(w_landed[slot], 16)

        def feat_view(w):
            return w[:, :].rearrange("p (k n) -> p k n", k=KC)

        def tok_view(w):
            return w[:, :].rearrange("p (k n) -> p k n", k=4)

        def down_view(w):
            return w[:, :].rearrange("p (k n) -> p k n", k=2)

        def feat_src(w, col):
            return w[:, bass.ds(col, 256)].rearrange("(k p) n -> p k n", p=P)

        def tok_src(w, half, col):
            return w[half * 512:(half + 1) * 512, col:col + 512].rearrange("(k p) n -> p k n", p=P)

        def down_src(w, row):
            return w[bass.ds(row, 256), :].rearrange("(k p) n -> p k n", p=P)

        def three(mm, o, ahi, alo, bhi, blo, first, last):
            mm(o, ahi, bhi, start=first, stop=False)
            mm(o, alo, bhi, start=False, stop=False)
            return mm(o, ahi, blo, start=False, stop=last)

        def feat_unit(pe, n, bank, i=0):
            slot = n % RING
            pe.wait_ge(w_lo_ready, 3 * i + (n + 1))
            for t in range(2):
                for k in range(KC):
                    a, b = feat_view(w_hi[slot]), feat_view(w_lo[slot])
                    last = three(pe.matmul, PS[:, bank, t * S:(t + 1) * S],
                                 a[:, k, t * P:(t + 1) * P], b[:, k, t * P:(t + 1) * P],
                                 h_hi[:, k, :], h_lo[:, k, :], k == 0, k == KC - 1)
            last.then_inc(w_released, 1)

        def tok_unit(pe, n, half, banks):
            slot = n % RING
            pe.wait_ge(w_lo_ready, n + 1)
            a, b = tok_view(w_hi[slot]), tok_view(w_lo[slot])
            for tb in range(TB):
                for k in range(4):
                    kk = 4 * half + k
                    last = three(pe.matmul, PS[:, banks[tb], :],
                                 h_hi[:, kk, tb * P:(tb + 1) * P], h_lo[:, kk, tb * P:(tb + 1) * P],
                                 a[:, k, :], b[:, k, :], kk == 0, kk == KC - 1)
            last.then_inc(w_released, 1)

        def down_unit(pe, n, first, last_unit, i=0):
            slot = n % RING
            pe.wait_ge(w_lo_ready, 3 * i + (n + 1))
            a, b = down_view(w_hi[slot]), down_view(w_lo[slot])
            for k in range(2):
                for tb in range(TB):
                    for half in range(2):
                        last = three(pe.matmul, PS[:, 4 + 2 * tb + half, :],
                                     gu_hi[:, k, tb * P:(tb + 1) * P], gu_lo[:, k, tb * P:(tb + 1) * P],
                                     a[:, k, half * 512:(half + 1) * 512], b[:, k, half * 512:(half + 1) * 512],
                                     first and k == 0, last_unit and k == 1)
            return last.then_inc(w_released, 1)

        def chain(name):
            step, count = sem(name), [0]

            def link(eng, ins):
                count[0] += 1
                ins.then_inc(step, 1)
                eng.wait_ge(step, count[0])
            return link

        dlink = chain("dve_step")
        alink = chain("act_step")
        plink = chain("pool_step")

        def rsqrt(dve, x, n):
            y, t, u = nt[:, 0, 0:n], nt[:, 1, 0:n], nt[:, 2, 0:n]
            dlink(dve, dve.tensor_scalar(y.bitcast(I32), x.bitcast(I32), -0.5, RSQRT_MAGIC, ALU.mult, ALU.add))
            for step in range(3):
                dlink(dve, dve.tensor_tensor(t, y, y, ALU.mult))
                dlink(dve, dve.scalar_tensor_tensor(u, t, -0.5, x, ALU.mult, ALU.mult))
                o = x if step == 2 else y
                dlink(dve, dve.scalar_tensor_tensor(o, u, 1.5, y, ALU.add, ALU.mult))

        class Norm:

            x_ready = sem("norm_x_ready")
            square = sem("norm_square")
            normed = sem("norm_normed")
            turned = sem("norm_turned")
            t_dve = sem("norm_t_dve")
            t_act = sem("norm_t_act")
            hi = sem("norm_hi")
            lo = sem("norm_lo")

            def __init__(self, at, gain=None, src=None):
                self.at, self.gain, self.rms = at, gain, src is None
                self.src = XN if src is None else src

            def pe(self, pe):
                for tb in range(TB):
                    pe.wait_ge(self.normed, self.at * TB + tb + 1)
                    for k in range(KC):
                        m = pe.transpose(PS[:, k // 2, (k % 2) * S + tb * P:(k % 2) * S + (tb + 1) * P],
                                         self.src[:, tb, k * P:(k + 1) * P], ident)
                        if tb == TB - 1 and k % 2:
                            m.then_inc(self.turned, 1)

            def ready(self, pe):
                pe.wait_ge(self.lo, self.at * 4 + 4)

            def stage(self, eng, j, done):
                eng.wait_ge(self.turned, self.at * 4 + j + 1)
                for kk in range(2):
                    k = 2 * j + kk
                    src = PS[:, j, kk * S:(kk + 1) * S]
                    g = 1.0 if self.gain is None else cols[:, self.gain + k:self.gain + k + 1]
                    if done is self.t_act:
                        m = eng.activation(T[:, k, :], src, ACT.Copy, scale=g)
                    else:
                        m = eng.tensor_scalar(T[:, k, :], src, g, None, ALU.mult)
                m.then_inc(done, 1)

            def act(self, act):
                if self.rms:
                    act.wait_ge(self.x_ready, self.at + 1)
                    act.activation(XN[:, 0, :], X[:, 0, :], ACT.Square, scale=1.0 / 32.0,
                                   accum_out=ss[:, 0:1]).then_inc(self.square, 1)
                for j in range(4):
                    if j % 2:
                        self.stage(act, j, self.t_act)
                        act.wait_ge(self.t_act, self.at * 2 + j // 2 + 1)
                    else:
                        act.wait_ge(self.t_dve, self.at * 2 + j // 2 + 1)
                    act.activation(h_hi[:, 2 * j:2 * j + 2, :], T[:, 2 * j:2 * j + 2, :], ACT.Copy).then_inc(self.hi, 1)

            def dve(self, dve):
                if self.rms:
                    dve.wait_ge(self.x_ready, self.at + 1)
                    dlink(dve, dve.tensor_tensor_reduce(XN[:, 1, :], X[:, 1, :], X[:, 1, :], 1.0 / DM, 0.0,
                                                        ALU.mult, ALU.add, ss[:, 1:2]))
                    dve.wait_ge(self.square, self.at + 1)
                    dlink(dve, dve.tensor_scalar(ss[:, 0:2], ss[:, 0:2], EPS_RMS, None, ALU.add))
                    rsqrt(dve, ss[:, 0:2], 2)
                    for tb in range(TB):
                        dve.tensor_scalar(XN[:, tb, :], X[:, tb, :], ss[:, tb:tb + 1], None,
                                          ALU.mult).then_inc(self.normed, 1)
                for j in range(0, 4, 2):
                    self.stage(dve, j, self.t_dve)
                for j in range(4):
                    dve.wait_ge(self.hi, self.at * 4 + j + 1)
                    dve.tensor_tensor(h_lo[:, 2 * j:2 * j + 2, :], T[:, 2 * j:2 * j + 2, :],
                                      h_hi[:, 2 * j:2 * j + 2, :].bitcast(F32), ALU.subtract).then_inc(self.lo, 1)

        class Ffn:

            act_done = sem("ffn_act_done")
            gu_done = sem("ffn_gu_done")
            guhi_done = sem("ffn_guhi_done")
            gulo_done = sem("ffn_gulo_done")

            def __init__(self, at, name, wg, wu, wd, norm, after, conv=False):
                self.u0, self.b = first_unit[name], at * FF_STEPS
                self.wg, self.wu, self.wd, self.norm, self.after, self.conv = wg, wu, wd, norm, after, conv
                if conv:
                    self.tap2 = sem(name + "_tap2")
                    self.tap1 = sem(name + "_tap1")
                    self.a_conv = sem(name + "_a_conv")
                    self.u_conv = sem(name + "_u_conv")

            def sp(self, sp):
                u = self.u0
                load_unit(sp, u, feat_src(self.wg, 0), feat_view)
                load_unit(sp, u + 1, feat_src(self.wu, 0), feat_view)
                load_unit(sp, u + 2, feat_src(self.wg, 256), feat_view)
                load_unit(sp, u + 3, feat_src(self.wu, 256), feat_view)
                load_unit(sp, u + 4, down_src(self.wd, 0), down_view)
                with sp.Fori(0, FF_STEPS - 2) as i:
                    load_unit(sp, u + 5, feat_src(self.wg, i * 256 + 512), feat_view, i)
                    load_unit(sp, u + 6, feat_src(self.wu, i * 256 + 512), feat_view, i)
                    load_unit(sp, u + 7, down_src(self.wd, i * 256 + 256), down_view, i)
                load_unit(sp, u + 3 * FF_STEPS - 1, down_src(self.wd, FF - 256), down_view)

            def pe(self, pe):
                u = self.u0
                self.norm.ready(pe)
                self.up(pe, u, 0, 0, None)
                self.up(pe, u + 1, 1, 0, None)
                self.up(pe, u + 2, 0, 0, 1)
                self.up(pe, u + 3, 1, 0, 1)
                pe.wait_ge(self.gulo_done, self.b + 1)
                down_unit(pe, u + 4, True, False)
                with pe.Fori(0, FF_STEPS - 2) as i:
                    self.up(pe, u + 5, 0, i, i + 2)
                    self.up(pe, u + 6, 1, i, i + 2)
                    pe.wait_ge(self.gulo_done, i + (self.b + 2))
                    down_unit(pe, u + 7, False, False, i)
                pe.wait_ge(self.gulo_done, self.b + FF_STEPS)
                down_unit(pe, u + 3 * FF_STEPS - 1, False, True)

            def up(self, pe, n, which, i, free):
                if free is not None:
                    if self.conv:
                        pe.wait_ge(self.a_conv if which == 0 else self.u_conv, free)
                    else:
                        pe.wait_ge(self.act_done if which == 0 else self.gu_done, free + self.b)
                feat_unit(pe, n, which, i)

            def conv_tap2(self, act, which, i, at):
                act.wait_ge(w_released, self.u0 + 1 + which + at)
                dst = ffn_act if which == 0 else ffn_up
                for t in range(2):
                    tile = i * 2 + (22 * which + t)
                    m = act.activation(dst[:, t * S:(t + 1) * S], PS[:, which, t * S:(t + 1) * S], ACT.Identity,
                                       bias=convc[:, 3, bass.ds(tile, 1)], scale=convc[:, 2, bass.ds(tile, 1)])
                m.then_inc(self.tap2, 1)

            def conv_taps(self, dve, which, i):
                dve.wait_ge(self.tap2, 2 * i + (which + 1))
                dst = ffn_act if which == 0 else ffn_up
                for t in range(2):
                    tile = i * 2 + (22 * which + t)
                    y = dst[:, t * S + 1:(t + 1) * S]
                    m = dve.scalar_tensor_tensor(y, PS[:, which, t * S:(t + 1) * S - 1],
                                                 convc[:, 1, bass.ds(tile, 1)], y, ALU.mult, ALU.add)
                m.then_inc(self.tap1, 1)
                dve.wait_ge(self.tap1, 2 * i + (which + 1))
                for t in range(2):
                    tile = i * 2 + (22 * which + t)
                    y = dst[:, t * S + 2:(t + 1) * S]
                    m = dve.scalar_tensor_tensor(y, PS[:, which, t * S:(t + 1) * S - 2],
                                                 convc[:, 0, bass.ds(tile, 1)], y, ALU.mult, ALU.add)
                m.then_inc(self.a_conv if which == 0 else self.u_conv, 1)

            def act_step(self, act, i, first):
                u, r = self.u0, (0 if first else i - 1)
                if first:
                    at_g, at_u = 0, 0
                    split_hi(act, u + 2)
                else:
                    at_g = 3 * r + 2
                    at_u = 3 * r + 2
                    split_hi(act, u + 4, i=r)
                if self.conv:
                    self.conv_tap2(act, 0, i, at_g)
                split_hi(act, u + 3 if first else u + 5, i=r)
                if self.conv:
                    self.conv_tap2(act, 1, i, at_u)
                    act.wait_ge(self.a_conv, i + 1)
                    act.activation(ffn_act, ffn_act, ACT.Gelu).then_inc(self.act_done, 1)
                else:
                    act.wait_ge(w_released, u + 1 + at_g)
                    act.activation(ffn_act, PS[:, 0, :], ACT.Silu).then_inc(self.act_done, 1)
                if not first:
                    split_hi(act, u + 6, i=r)
                act.wait_ge(self.gu_done, i + (self.b + 1))
                if not first:
                    act.wait_ge(w_released, u + 3 * r + 5)
                act.activation(gu_hi[:, :, :], ffn_gu.rearrange("p (t s) -> p t s", t=2), ACT.Copy)\
                   .then_inc(self.guhi_done, 1)

            def act(self, act):
                self.act_step(act, 0, True)
                self.act_step(act, 1, False)
                end = FF_STEPS - 2 if self.conv else FF_STEPS - 1
                with act.Fori(1, end) as i:
                    self.act_step(act, i + 1, False)
                if self.conv:
                    self.act_step(act, FF_STEPS - 1, False)
                split_hi(act, self.u0 + 3 * FF_STEPS + 1)

            def dve_step(self, dve, i, first):
                u, r = self.u0, (0 if first else i - 1)
                split_lo(dve, u + 2 if first else u + 4, i=r)
                if self.conv:
                    self.conv_taps(dve, 0, i)
                split_lo(dve, u + 3 if first else u + 5, i=r)
                if self.conv:
                    self.conv_taps(dve, 1, i)
                    dve.wait_ge(self.u_conv, i + 1)
                    dve.wait_ge(self.act_done, i + (self.b + 1))
                    if not first:
                        dve.wait_ge(self.gulo_done, i + self.b)
                    dve.tensor_tensor(ffn_gu, ffn_act, ffn_up, ALU.mult).then_inc(self.gu_done, 1)
                else:
                    dve.wait_ge(w_released, u + 2 if first else u + 3 * r + 4)
                    dve.wait_ge(self.act_done, i + (self.b + 1))
                    if not first:
                        dve.wait_ge(self.gulo_done, i + self.b)
                    dve.tensor_tensor(ffn_gu, PS[:, 1, :], ffn_act, ALU.mult).then_inc(self.gu_done, 1)
                if not first:
                    split_lo(dve, u + 6, i=r)
                dve.wait_ge(self.guhi_done, i + (self.b + 1))
                dve.tensor_tensor(gu_lo[:, :, :], ffn_gu.rearrange("p (t s) -> p t s", t=2),
                                  gu_hi[:, :, :].bitcast(F32), ALU.subtract).then_inc(self.gulo_done, 1)

            def dve(self, dve):
                self.dve_step(dve, 0, True)
                end = FF_STEPS - 2 if self.conv else FF_STEPS - 1
                with dve.Fori(0, end) as i:
                    self.dve_step(dve, i + 1, False)
                if self.conv:
                    self.dve_step(dve, FF_STEPS - 1, False)
                split_lo(dve, self.u0 + 3 * FF_STEPS + 1)
                dve.wait_ge(w_released, self.u0 + 3 * FF_STEPS)
                for tb in range(TB):
                    for half in range(2):
                        x = X[:, tb, half * 512:(half + 1) * 512]
                        y = PS[:, 4 + 2 * tb + half, :]
                        if self.conv:
                            m = dve.scalar_tensor_tensor(x, x, ALPHA, y, ALU.mult, ALU.add)
                        else:
                            m = dve.scalar_tensor_tensor(x, y, 0.5, x, ALU.mult, ALU.add)
                m.then_inc(self.after, 1)

        class OutProj:
            def __init__(self, name, w, ready, after, alpha=None):
                self.u0, self.w, self.ready, self.after, self.alpha = first_unit[name], w, ready, after, alpha

            def sp(self, sp):
                for c in range(2):
                    for half in range(2):
                        load_unit(sp, self.u0 + 2 * c + half, tok_src(self.w, half, c * 512), tok_view)

            def pe(self, pe):
                self.ready(pe)
                for c in range(2):
                    for half in range(2):
                        tok_unit(pe, self.u0 + 2 * c + half, half, (2 * c, 2 * c + 1))

            def act(self, act):
                for j in range(4):
                    split_hi(act, self.u0 + j + LOOKAHEAD)

            def dve(self, dve):
                for c in range(2):
                    for half in range(2):
                        split_lo(dve, self.u0 + 2 * c + half + LOOKAHEAD)
                    dve.wait_ge(w_released, self.u0 + 2 * c + 2)
                    for tb in range(TB):
                        x = X[:, tb, c * 512:(c + 1) * 512]
                        y = PS[:, 2 * c + tb, :]
                        if self.alpha is None:
                            m = dve.tensor_tensor(x, y, x, ALU.add)
                        else:
                            m = dve.scalar_tensor_tensor(x, x, self.alpha, y, ALU.mult, ALU.add)
                m.then_inc(self.after, 1)

        class Attention:

            def __init__(self, name, heads, q, k, v, bias, sink_of=None, token_out=False, rows_reversed=False):
                self.n, self.q, self.k, self.v, self.bias = heads, q, k, v, bias
                self.sink_of, self.token_out, self.rows_reversed = sink_of, token_out, rows_reversed
                self.scores = sem(name + "_scores")
                self.max_ready = sem(name + "_max")
                self.exp_done = sem(name + "_exp")
                self.p_ready = sem(name + "_p")
                self.turned = sem(name + "_turned")
                self.pt_ready = sem(name + "_pt")
                self.out_ready = sem(name + "_out")
                self.hi = sem(name + "_hi")
                self.lo = sem(name + "_lo")
                self.start = sem(name + "_start")

            def pe_scores(self, pe, g):
                if g == 0:
                    pe.wait_ge(self.start, 2)
                if g >= 2:
                    pe.wait_ge(self.exp_done, g - 1)
                for tb in range(TB):
                    m = pe.matmul(PS[:, g % 2, tb * S:(tb + 1) * S], self.q(g, tb), self.k(g), start=True, stop=True)
                m.then_inc(self.scores, 1)

            def pe_turn(self, pe, g):
                pe.wait_ge(self.p_ready, g + 1)
                if g >= 2:
                    pe.wait_ge(self.pt_ready, g - 1)
                for kb in range(2):
                    for tb in range(TB):
                        m = pe.transpose(PS[:, 2 + g % 2, kb * S + tb * P:kb * S + (tb + 1) * P],
                                         p_sb[:, g % 2, tb * S + kb * P:tb * S + (kb + 1) * P], ident)
                m.then_inc(self.turned, 1)

            def pe_values(self, pe, g):
                pe.wait_ge(self.pt_ready, g + 1)
                if self.token_out:
                    for tb in range(TB):
                        for kb in range(tb + 1):
                            m = pe.matmul(PS[:, 4 + tb, g * HD:(g + 1) * HD], pt_sb[:, g % 2, kb, tb * P:(tb + 1) * P],
                                          self.v(g, kb), start=kb == 0, stop=kb == tb)
                else:
                    if g % 2 == 0 and g >= 4:
                        pe.wait_ge(self.lo, g // 2 - 1)
                    o = PS[(g % 2) * HD:(g % 2) * HD + HD, 4 + (g // 2) % 2, 0:S]
                    for kb in range(2):
                        m = pe.matmul(o, self.v(g, kb), pt_sb[:, g % 2, kb, :], start=kb == 0, stop=kb == 1)
                m.then_inc(self.out_ready, 1)

            def pe(self, pe):
                for s in range(self.n + 2):
                    if s < self.n:
                        self.pe_scores(pe, s)
                    if 1 <= s <= self.n:
                        self.pe_turn(pe, s - 1)
                    if s >= 2:
                        self.pe_values(pe, s - 2)

            def dve_max(self, dve, g):
                dve.wait_ge(self.scores, g + 1)
                b = self.bias(g)
                if b is None:
                    dlink(dve, dve.tensor_reduce(mx[:, g, :], PS[:, g % 2, :].rearrange("p (t k) -> p t k", t=TB),
                                                 AX_X, ALU.max))
                    dve.tensor_scalar(negm[:, g, :], mx[:, g, :], -SCALE, None, ALU.mult).then_inc(self.max_ready, 1)
                    return
                for tb in range(TB):
                    o, i, bb = s_sb[:, g % 2, tb * S:(tb + 1) * S], PS[:, g % 2, tb * S:(tb + 1) * S], b[:, tb, :]
                    if self.rows_reversed:
                        bb = bass.AP(tensor=bb.tensor, offset=bb.offset + GRID_W - 1,
                                     ap=[list(bb.ap[0]), [GRID_W, 4], [-1, GRID_W]])
                        o, i = (z.rearrange("p (a k) -> p a k", k=GRID_W) for z in (o, i))
                    m = dve.tensor_tensor_reduce(o, i, bb, SCALE, -3e38, ALU.add, ALU.max, mx[:, g, tb:tb + 1])
                dlink(dve, m)
                if self.sink_of is not None and self.sink_of(g) is not None:
                    s = self.sink_of(g)
                    dve.tensor_scalar(negm[:, g, :], mx[:, g, :], s, -1.0, ALU.max, ALU.mult).then_inc(self.max_ready, 1)
                else:
                    dve.tensor_scalar(negm[:, g, :], mx[:, g, :], -1.0, None, ALU.mult).then_inc(self.max_ready, 1)

            def act_exp(self, act, g):
                act.wait_ge(self.max_ready, g + 1)
                if g >= 2:
                    act.wait_ge(self.turned, g - 1)
                raw_scores = self.bias(g) is None
                if self.sink_of is not None and self.sink_of(g) is not None:
                    act.activation(esink[:, g % 8, :], negm[:, g, :], ACT.Exp, bias=self.sink_of(g))
                for tb in range(TB):
                    src = PS[:, g % 2, tb * S:(tb + 1) * S] if raw_scores else s_sb[:, g % 2, tb * S:(tb + 1) * S]
                    m = act.activation(p_sb[:, g % 2, tb * S:(tb + 1) * S], src, ACT.Exp, bias=negm[:, g, tb:tb + 1],
                                       scale=SCALE if raw_scores else 1.0, accum_out=rsum[:, g, tb:tb + 1])
                m.then_inc(self.exp_done, 1)

            def dve_scale(self, dve, g):
                dve.wait_ge(self.exp_done, g + 1)
                if self.sink_of is not None and self.sink_of(g) is not None:
                    dlink(dve, dve.tensor_tensor(rsum[:, g, :], rsum[:, g, :], esink[:, g % 8, :], ALU.add))
                if self.token_out:
                    dve.reciprocal(rinv[:, g, :], rsum[:, g, :]).then_inc(self.p_ready, 1)
                    return
                dlink(dve, dve.reciprocal(rinv[:, g, :], rsum[:, g, :]))
                for tb in range(TB):
                    p = p_sb[:, g % 2, tb * S:(tb + 1) * S]
                    m = dve.tensor_scalar(p, p, rinv[:, g, tb:tb + 1], None, ALU.mult)
                m.then_inc(self.p_ready, 1)

            def act_turned(self, act, g):
                act.wait_ge(self.turned, g + 1)
                if g >= 2:
                    act.wait_ge(self.out_ready, g - 1)
                act.activation(pt_sb[:, g % 2, :, :], PS[:, 2 + g % 2, :].rearrange("p (k q) -> p k q", k=2),
                               ACT.Copy).then_inc(self.pt_ready, 1)

            def act(self, act):
                for s in range(self.n + 3):
                    if s < self.n:
                        self.act_exp(act, s)
                    if 1 <= s <= self.n:
                        self.act_turned(act, s - 1)
                    if not self.token_out and s >= 3 and s % 2 == 0:
                        pair = (s - 4) // 2
                        act.wait_ge(self.out_ready, 2 * pair + 2)
                        act.activation(h_hi[:, pair, :], PS[:, 4 + pair % 2, 0:S], ACT.Copy).then_inc(self.hi, 1)

            def dve(self, dve):
                for s in range(self.n + 3):
                    if s < self.n:
                        self.dve_max(dve, s)
                    if 1 <= s <= self.n:
                        self.dve_scale(dve, s - 1)
                    if not self.token_out and s >= 3 and s % 2 == 0:
                        pair = (s - 4) // 2
                        dve.wait_ge(self.hi, pair + 1)
                        dve.tensor_tensor(h_lo[:, pair, :], PS[:, 4 + pair % 2, 0:S], h_hi[:, pair, :].bitcast(F32),
                                          ALU.subtract).then_inc(self.lo, 1)

            def ready(self, pe):
                pe.wait_ge(self.lo, self.n // 2)

        class EvenIn:
            def __init__(self, norm, att):
                self.u0, self.norm, self.att = first_unit["even_in"], norm, att
                self.pj_act = sem("even_pj_act")
                self.pj_dve = sem("even_pj_dve")
                self.rope = [sem("even_rope_a"), sem("even_rope_b")]
                self.turned = sem("even_turned")
                self.const = sem("even_const")

            def sp(self, sp, w):
                for c in range(3):
                    for half in range(2):
                        load_unit(sp, self.u0 + 2 * c + half, tok_src(w, half, c * 512), tok_view)

            def pe(self, pe):
                self.norm.ready(pe)
                for c in range(3):
                    if c == 2:
                        pe.wait_ge(self.pj_act, 1)
                        pe.wait_ge(self.pj_dve, 1)
                    for half in range(2):
                        tok_unit(pe, self.u0 + 2 * c + half, half, (2 * (c % 2), 2 * (c % 2) + 1))
                for br in range(2):
                    pe.wait_ge(self.rope[br], TB)
                    for slot in range(5):
                        bank = ((4, 5, 6), (7, 2, 3))[br][slot // 2]
                        for tb in range(TB):
                            m = pe.transpose(PS[:, bank, (slot % 2) * S + tb * P:(slot % 2) * S + (tb + 1) * P],
                                             R[:, tb, br * 640 + slot * P:br * 640 + (slot + 1) * P], ident)
                        if slot % 2 or slot == 4:
                            m.then_inc(self.turned, 1)

            def evac(self, eng, n):
                br, j = divmod(n, 3)
                bank = ((4, 5, 6), (7, 2, 3))[br][j]
                w = 2 if j < 2 else 1
                src = PS[:, bank, 0:w * S].rearrange("p (a s) -> p a s", a=w)
                dst = QKT[:, 5 * br + 2 * j:5 * br + 2 * j + w, :]
                eng.wait_ge(self.turned, n + 1)
                return dst, src

            def act(self, act):
                for c in range(3):
                    for half in range(2):
                        split_hi(act, self.u0 + 2 * c + half + LOOKAHEAD)
                    act.wait_ge(w_released, self.u0 + 2 * c + 2)
                    act.activation(PJ[:, 0, c * 512:(c + 1) * 512], PS[:, 2 * (c % 2), :], ACT.Copy)\
                       .then_inc(self.pj_act, 1)
                for n in (0, 2, 3, 5):
                    dst, src = self.evac(act, n)
                    m = act.activation(dst, src, ACT.Copy)
                m.then_inc(self.att.start, 1)

            def rotate(self, eng, link, br, tb):
                x0 = 768 * br
                if tb:
                    eng.wait_ge(self.rope[br], tb)
                x = PJ[:, tb, x0:x0 + 640]
                t1, t2 = rope_t1[:, br, :], rope_t2[:, br, :]
                C, Sn = rope_tab(2 * br, tb), rope_tab(2 * br + 1, tb)
                eng.tensor_tensor(t1.rearrange("p (h d) -> p h d", d=HD), x.rearrange("p (h d) -> p h d", d=HD),
                                  C.unsqueeze(1).to_broadcast([P, 10, HD]), ALU.mult)
                w = 16 if br == 0 else 32
                groups = HD // (2 * w)
                for half in range(2):
                    o = t2.rearrange("p (h g a w) -> p h g a w", g=groups, a=2, w=w)[:, :, :, half, :]
                    i = x.rearrange("p (h g a w) -> p h g a w", g=groups, a=2, w=w)[:, :, :, 1 - half, :]
                    s = Sn.rearrange("p (g a w) -> p g a w", a=2, w=w)[:, :, half, :].unsqueeze(1)\
                        .to_broadcast([P, 10, groups, w])
                    m = eng.tensor_tensor(o, i, s, ALU.mult)
                link(eng, m)
                r = R[:, tb, br * 640:(br + 1) * 640]
                qi = "p (b s d) -> p b s d"
                eng.tensor_tensor(r[:, 0:512].rearrange("p (s b d) -> p b s d", b=2, d=HD),
                                  t1[:, 0:512].rearrange(qi, b=2, d=HD), t2[:, 0:512].rearrange(qi, b=2, d=HD), ALU.add)
                eng.tensor_tensor(r[:, 512:640], t1[:, 512:640], t2[:, 512:640], ALU.add).then_inc(self.rope[br], 1)

            def dve(self, dve):
                for c in range(3):
                    for half in range(2):
                        split_lo(dve, self.u0 + 2 * c + half + LOOKAHEAD)
                    dve.wait_ge(w_released, self.u0 + 2 * c + 2)
                    dve.tensor_copy(PJ[:, 1, c * 512:(c + 1) * 512], PS[:, 2 * (c % 2) + 1, :]).then_inc(self.pj_dve, 1)
                dve.wait_ge(self.pj_act, 2)
                dve.wait_ge(self.pj_dve, 3)
                dve.wait_ge(self.const, 32)
                xa = PJ[:, :, 0:640]
                sq = R[:, :, 0:640]
                dlink(dve, dve.tensor_tensor(sq, xa, xa, ALU.mult))
                for tb in range(TB):
                    m = dve.tensor_reduce(ss[:, tb * 10:(tb + 1) * 10], sq[:, tb, :].rearrange("p (h d) -> p h d", d=HD),
                                          AX_X, ALU.add)
                dlink(dve, m)
                dlink(dve, dve.tensor_scalar(ss[:, 0:20], ss[:, 0:20], 1.0 / HD, EPS_RMS, ALU.mult, ALU.add))
                rsqrt(dve, ss[:, 0:20], 20)
                for tb in range(TB):
                    x = PJ[:, tb, 0:640].rearrange("p (h d) -> p h d", d=HD)
                    dlink(dve, dve.tensor_tensor(x, x, ss[:, tb * 10:(tb + 1) * 10].unsqueeze(2).to_broadcast([P, 10, HD]),
                                                 ALU.mult))
                    dlink(dve, dve.tensor_tensor(PJ[:, tb, 0:640], PJ[:, tb, 0:640], qk_gain, ALU.mult))
                    self.rotate(dve, dlink, 0, tb)
                for n in (1, 4):
                    dst, src = self.evac(dve, n)
                    m = dve.tensor_copy(dst, src)
                m.then_inc(self.att.start, 1)

            def pool(self, pool):
                pool.wait_ge(self.pj_act, 3)
                pool.wait_ge(self.pj_dve, 3)
                for tb in range(TB):
                    self.rotate(pool, plink, 1, tb)

        class OddIn:
            def __init__(self, norm, att):
                self.u0, self.norm, self.att = first_unit["odd_in"], norm, att
                self.act_out = sem("odd_act_out")
                self.dve_out = sem("odd_dve_out")

            def sp(self, sp, w):
                for j in range(8):
                    load_unit(sp, self.u0 + j, feat_src(w, j * 256), feat_view)
                for c in range(2):
                    for half in range(2):
                        load_unit(sp, self.u0 + 8 + 2 * c + half, tok_src(w, half, 2048 + c * 512), tok_view)

            def pe(self, pe):
                self.norm.ready(pe)
                for j in range(8):
                    if j >= 4:
                        pe.wait_ge(self.dve_out if j % 2 else self.act_out, (j - 4) // 2 + 1)
                    feat_unit(pe, self.u0 + j, j % 4)
                for c in range(2):
                    for half in range(2):
                        tok_unit(pe, self.u0 + 8 + 2 * c + half, half, (4 + 2 * c, 5 + 2 * c))

            def take(self, eng, mine, split, copy, out):
                for j in range(8):
                    split(eng, self.u0 + j + LOOKAHEAD)
                    if j % 2 == mine:
                        eng.wait_ge(w_released, self.u0 + j + 1)
                        m = copy(QKT[:, 2 * j:2 * j + 2, :], PS[:, j % 4, :].rearrange("p (a s) -> p a s", a=2))
                        m.then_inc(out, 1)
                for c in range(2):
                    for half in range(2):
                        split(eng, self.u0 + 8 + 2 * c + half + LOOKAHEAD)
                    eng.wait_ge(w_released, self.u0 + 8 + 2 * c + 2)
                    m = copy(V[:, mine, c * 512:(c + 1) * 512], PS[:, 4 + 2 * c + mine, :])
                m.then_inc(self.att.start, 1)

            def act(self, act):
                self.take(act, 0, split_hi, lambda o, i: act.activation(o, i, ACT.Copy), self.act_out)

            def dve(self, dve):
                self.take(dve, 1, split_lo, lambda o, i: dve.tensor_copy(o, i), self.dve_out)

        def layer_norm(dve, g, b, done):
            for tb in range(TB):
                for half in range(2):
                    m = dve.bn_stats(bn[:, tb, half, :], X[:, tb, half * 512:(half + 1) * 512])
            dlink(dve, m)
            for tb in range(TB):
                m = dve.bn_aggr(mv[:, tb, :], bn[:, tb, :, :].rearrange("p a b -> p (a b)"))
            dlink(dve, m)
            dlink(dve, dve.tensor_scalar(ss[:, 0:2], mv[:, :, 1], EPS_LN, None, ALU.add))
            rsqrt(dve, ss[:, 0:2], 2)
            for tb in range(TB):
                x = X[:, tb, :]
                dlink(dve, dve.tensor_scalar(x, x, mv[:, tb, 0:1], ss[:, tb:tb + 1], ALU.subtract, ALU.mult))
                dlink(dve, dve.tensor_tensor(x, x, g, ALU.mult))
                m = dve.tensor_tensor(x, x, b, ALU.add)
                if tb == 0:
                    dlink(dve, m) if done is None else m.then_inc(done, 1)
                else:
                    m.then_inc(done, 1)

        QA, KA, VA, FA = 0, 512, 1024, 1536
        QR, FR, IR, GR = 1544, 2056, 2568, 3080

        class RecIn:
            PLAN = [("f", QA, 0), ("f", KA, 4), ("t", VA, 0), ("f", QR, 8), ("t", GR, 1), ("f", FR, 12), ("t", IR, 2)]

            def __init__(self, norm, att):
                self.u0, self.norm, self.att = first_unit["rec_in"], norm, att
                self.wf_in = sem("rec_wf_in")
                self.f_done = sem("rec_f_done")
                self.f_chain = sem("rec_f_chain")
                self.c_ready = sem("rec_c_ready")
                self.c_turned = sem("rec_c_turned")
                self.cq_ready = sem("rec_cq_ready")
                self.c_wide = sem("rec_c_wide")
                self.bias_done = sem("rec_bias_done")
                self.sel_free = sem("rec_sel_free")
                self.act_out = sem("rec_act_out")
                self.dve_out = sem("rec_dve_out")

            def sp(self, sp, w):
                n = self.u0
                for kind, col, _ in self.PLAN:
                    for j in range(2):
                        if kind == "f":
                            load_unit(sp, n, feat_src(w, col + 256 * j), feat_view)
                        else:
                            load_unit(sp, n, tok_src(w, j, col), tok_view)
                        n += 1

            def banks(self, group):
                return (0, 1) if group % 2 == 0 else (2, 3)

            def pe(self, pe):
                self.norm.ready(pe)
                pe.wait_ge(self.wf_in, 32)
                for k in range(KC):
                    m = pe.matmul(PS[0:8, 6, 0:S], wf[:, k, :], T[:, k, :], start=k == 0, stop=k == KC - 1)
                m.then_inc(self.f_done, 1)
                n = self.u0
                for group, (kind, _, _) in enumerate(self.PLAN):
                    b = self.banks(group)
                    if group >= 2:
                        pe.wait_ge(self.act_out, group - 1)
                        pe.wait_ge(self.dve_out, group - 1)
                    for j in range(2):
                        if kind == "f":
                            feat_unit(pe, n, b[j])
                        else:
                            tok_unit(pe, n, j, b)
                        n += 1
                    if group == 0:
                        pe.wait_ge(self.c_ready, 1)
                        for tb in range(TB):
                            m = pe.transpose(PS[:, 6, tb * 8:(tb + 1) * 8], f_c[:, tb * P:(tb + 1) * P],
                                             consts[0:8, C_IDENT:C_IDENT + 8])
                        m.then_inc(self.c_turned, 1)
                    if group == 1:
                        for pair in range(4):
                            bank = 4 + pair % 2
                            if pair >= 2:
                                pe.wait_ge(self.bias_done, pair - 1)
                            for a in range(2):
                                m = pe.matmul(PS[:, bank, a * S:(a + 1) * S], sel[:, 2 * pair + a, :], f_m,
                                              start=True, stop=True)
                            m.then_inc(self.c_wide, 1)

            def take(self, eng, mine, split, copy, out, extra):
                n = self.u0
                for group, (kind, _, dst) in enumerate(self.PLAN):
                    b = self.banks(group)[mine]
                    for j in range(2):
                        split(eng, n + LOOKAHEAD)
                        n += 1
                        if kind == "f" and j == mine:
                            eng.wait_ge(w_released, n)
                            copy(QKT[:, dst + 2 * j:dst + 2 * j + 2, :],
                                 PS[:, b, :].rearrange("p (a s) -> p a s", a=2), group).then_inc(out, 1)
                    if kind == "t":
                        eng.wait_ge(w_released, n)
                        if dst == 0:
                            eng.wait_ge(self.c_wide, 4)
                        o = (V[:, mine, 0:512], hg_gate[:, mine, :], V[:, mine, 512:1024])[dst]
                        copy(o, PS[:, b, :], group).then_inc(out, 1)
                    extra(group)

            def act(self, act):
                act.wait_ge(self.f_done, 1)
                alink(act, act.activation(f_z, PS[0:8, 6, 0:S], ACT.Identity, bias=fbias[:, 0:1]))
                alink(act, act.activation(f_a, f_z, ACT.Abs))
                alink(act, act.activation(f_a, f_a, ACT.Exp, scale=-1.0))
                act.activation(f_a, f_a, ACT.Ln, bias=1.0).then_inc(self.f_chain, 1)

                def extra(group):
                    if group == 6:
                        act.wait_ge(self.dve_out, 6)
                        act.wait_ge(self.act_out, 6)
                        alink(act, act.activation(hg_d[:, :, :], hg_f, ACT.Abs))
                        alink(act, act.activation(hg_d[:, :, :], hg_d[:, :, :], ACT.Exp, scale=-1.0))
                        act.activation(hg_d[:, :, :], hg_d[:, :, :], ACT.Ln, bias=1.0).then_inc(self.att.start, 1)

                def copy(o, i, group):
                    return act.activation(o, i, ACT.Copy)

                self.take(act, 0, split_hi, copy, self.act_out, extra)

            def dve(self, dve):
                dve.wait_ge(self.f_chain, 1)
                dlink(dve, dve.tensor_scalar(f_m, f_z, 0.0, None, ALU.min))
                dlink(dve, dve.tensor_tensor(f_m, f_m, f_a, ALU.subtract))
                for c in range(4):
                    dlink(dve, dve.tensor_tensor_scan(f_c[:, c * 64:(c + 1) * 64], f_m[:, c * 64:(c + 1) * 64],
                                                      zeros[0:8, :], 0.0 if c == 0 else f_c[:, c * 64 - 1:c * 64],
                                                      ALU.add, ALU.add))
                dlink(dve, dve.tensor_scalar(f_m, f_c, -8.0, None, ALU.mult))
                dve.tensor_scalar(f_c, f_c, 8.0, None, ALU.mult).then_inc(self.c_ready, 1)

                def extra(group):
                    if group == 0:
                        dve.wait_ge(self.c_turned, 1)
                        dlink(dve, dve.tensor_copy(cq[:, :, :], PS[:, 6, 0:16].rearrange("p (t h) -> p t h", t=TB)))
                    if group == 1:
                        for pair in range(4):
                            dve.wait_ge(self.c_wide, pair + 1)
                            for a in range(2):
                                h = 2 * pair + a
                                for tb in range(TB):
                                    m = dve.scalar_tensor_tensor(
                                        fox_bias[:, h, tb, :], PS[:, 4 + pair % 2, a * S:(a + 1) * S],
                                        cq[:, tb, h:h + 1], causal_mask[:, tb, :], ALU.add, ALU.add)
                            m.then_inc(self.bias_done, 1)

                def copy(o, i, group):
                    return dve.tensor_copy(o, i)

                self.take(dve, 1, split_lo, copy, self.dve_out, extra)
                dve.wait_ge(self.bias_done, 4)
                dve.tensor_copy(cq[:, :, :], cq[:, :, :]).then_inc(self.att.start, 1)

        class Recurrence:

            def __init__(self, att):
                self.att = att
                self.k_arg = sem("hg_k_arg")
                self.k_ready = sem("hg_k_ready")
                self.b_ready = sem("hg_b_ready")
                self.d_ready = sem("hg_d_ready")
                self.e_ready = sem("hg_e_ready")
                self.kq_ready = sem("hg_kq_ready")
                self.st_zero = sem("hg_st_zero")
                self.mm_done = sem("hg_mm_done")
                self.read_done = sem("hg_read_done")
                self.o_done = sem("hg_o_done")
                self.q_ready = sem("hg_q_ready")
                self.gate_ready = sem("hg_gate_ready")

            def pool(self, pool):
                pool.wait_ge(self.att.out_ready, 8)
                pool.memset(hg_st[:, :, :], 0.0).then_inc(self.st_zero, 1)
                pool.wait_ge(self.b_ready, 1)
                for n, m in enumerate((64,) + LEVELS):
                    b = hg_b.rearrange("p h t -> p (h t)")
                    d = hg_d.rearrange("p h t -> p (h t)")
                    if n == 0:
                        w = 64
                        ref = b.rearrange("p (c w) -> p c w", w=w)[:, :, w - 1:w]
                    else:
                        w = 2 * m
                        ref = b.rearrange("p (c w) -> p c w", w=w)[:, :, m - 1:m]
                        pool.wait_ge(self.e_ready, n)
                    pool.tensor_tensor(d.rearrange("p (c w) -> p c w", w=w), b.rearrange("p (c w) -> p c w", w=w),
                                       ref.to_broadcast([P, 1024 // w, w]), ALU.subtract).then_inc(self.d_ready, 1)

            def act(self, act):
                act.wait_ge(self.k_arg, 1)
                act.activation(hg_k, hg_k, ACT.Exp).then_inc(self.k_ready, 1)
                act.wait_ge(self.d_ready, 1)
                act.wait_ge(self.st_zero, 1)
                act.activation(hg_f, hg_b, ACT.Exp)
                act.activation(hg_e, hg_d, ACT.Exp, scale=-1.0).then_inc(self.e_ready, 1)
                for n, m in enumerate(LEVELS):
                    act.wait_ge(self.d_ready, n + 2)
                    act.wait_ge(self.kq_ready, n + 2 if n else 1)
                    d = hg_d.rearrange("p h t -> p (h t)").rearrange("p (c w) -> p c w", w=2 * m)
                    e = hg_e.rearrange("p h t -> p (h t)").rearrange("p (c w) -> p c w", w=2 * m)
                    act.activation(e[:, :, 0:m], d[:, :, 0:m], ACT.Exp, scale=-1.0)
                    act.activation(e[:, :, m:2 * m], d[:, :, m:2 * m], ACT.Exp).then_inc(self.e_ready, 1)

            def act_silu(self, act):
                act.activation(hg_q, hg_q, ACT.Silu).then_inc(self.q_ready, 1)
                act.activation(hg_gate, hg_gate, ACT.Silu).then_inc(self.gate_ready, 1)

            def pe(self, pe):
                pe.wait_ge(self.k_ready, 1)
                pe.wait_ge(self.q_ready, 1)
                for tb in range(TB):
                    for h in range(4):
                        m = pe.matmul(PS[:, 6 + tb, h * P:(h + 1) * P], hg_k[:, h, tb * P:(tb + 1) * P],
                                      hg_q[:, h, tb * P:(tb + 1) * P], start=True, stop=True)
                m.then_inc(self.mm_done, 1)
                pe.wait_ge(self.kq_ready, 1)
                for h in range(4):
                    for tb in range(TB):
                        m = pe.matmul(PS[:, 0, (2 * h + tb) * 64:(2 * h + tb + 1) * 64],
                                      hg_kh[:, h, tb * P:(tb + 1) * P], hg_qh[:, h, tb * P + 64:(tb + 1) * P],
                                      start=True, stop=True)
                m.then_inc(self.mm_done, 1)
                pe.wait_ge(self.kq_ready, 2)
                for h in range(4):
                    m = pe.matmul(PS[:, 1, h * P:(h + 1) * P], hg_kh[:, h, 0:P], hg_qh[:, h, P:S], start=True, stop=True)
                m.then_inc(self.mm_done, 1)
                for n, mm in enumerate(LEVELS):
                    pe.wait_ge(self.kq_ready, n + 3)
                    bank = n % 2
                    pe.wait_ge(self.read_done, n + 2)
                    for h in range(4):
                        for tb in range(TB):
                            q = hg_qh[:, h, tb * P:(tb + 1) * P].rearrange("p (c w) -> p c w", w=2 * mm)[:, :, mm:2 * mm]
                            o = PS[:, bank, (2 * h + tb) * 64:(2 * h + tb + 1) * 64].rearrange("p (c w) -> p c w", w=mm)
                            m = pe.matmul(o, hg_kh[:, h, tb * P:(tb + 1) * P], q, start=True, stop=True)
                    m.then_inc(self.mm_done, 1)
                pe.wait_ge(self.read_done, 3 + len(LEVELS))
                for tb in range(TB):
                    for h in range(4):
                        o = PS[:, 2 + tb, h * P:(h + 1) * P]
                        m = pe.matmul(o, hg_st[:, 2 * h + tb, :], V[:, tb, 512 + h * P:512 + (h + 1) * P],
                                      start=True, stop=tb == 0)
                        if tb:
                            m = pe.matmul(o, hg_s2[:, h, :], V[:, 0, 512 + h * P:512 + (h + 1) * P],
                                          start=False, stop=True)
                m.then_inc(self.o_done, 1)

            def dve_gates(self, dve):
                dve.wait_ge(self.att.start, 2)
                dve.tensor_scalar(hg_b, hg_f, 0.0, None, ALU.min)
                dlink(dve, dve.tensor_scalar(hg_k, hg_f, 0.0, -1.0, ALU.max, ALU.mult))
                dve.tensor_tensor(hg_k, hg_k, hg_d, ALU.subtract).then_inc(self.k_arg, 1)
                dlink(dve, dve.tensor_tensor(hg_b, hg_b, hg_d, ALU.subtract))
                b = hg_b.rearrange("p h t -> p (h t)")
                for c in range(16):
                    m = dve.tensor_tensor_scan(b[:, c * 64:(c + 1) * 64], b[:, c * 64:(c + 1) * 64], zeros, 0.0,
                                               ALU.add, ALU.add)
                m.then_inc(self.b_ready, 1)

            def dve(self, dve):
                dve.wait_ge(self.e_ready, 1)
                dve.wait_ge(self.k_ready, 1)
                dve.wait_ge(self.q_ready, 1)
                dve.tensor_tensor(hg_kh, hg_k, hg_e, ALU.mult)
                dve.tensor_tensor(hg_qh, hg_q, hg_f, ALU.mult).then_inc(self.kq_ready, 1)
                dve.wait_ge(self.mm_done, 1)
                eye = ident.unsqueeze(1).to_broadcast([P, 4, P]).bitcast(U32)
                st = hg_st.rearrange("p (h t) x -> p t h x", t=TB)
                dve.wait_ge(self.st_zero, 1)
                for tb in range(TB):
                    m = dve.copy_predicated(st[:, tb], eye, PS[:, 6 + tb, :].rearrange("p (h x) -> p h x", h=4))
                m.then_inc(self.read_done, 1)
                dve.wait_ge(self.mm_done, 2)
                dve.wait_ge(self.read_done, 1)
                dve.tensor_copy(hg_st[0:64, :, 64:128], PS[0:64, 0, :].rearrange("p (b x) -> p b x", b=8))\
                   .then_inc(self.read_done, 1)
                dve.wait_ge(self.kq_ready, 1)
                dve.tensor_tensor(hg_kh[:, :, 0:64], hg_kh[:, :, 0:64], hg_f[:, :, 127:128].to_broadcast([P, 4, 64]),
                                  ALU.mult)
                dve.tensor_tensor(hg_qh[:, :, 192:256], hg_qh[:, :, 192:256],
                                  hg_f[:, :, 191:192].to_broadcast([P, 4, 64]), ALU.mult).then_inc(self.kq_ready, 1)
                dve.wait_ge(self.mm_done, 3)
                dve.tensor_copy(hg_s2, PS[:, 1, :].rearrange("p (h x) -> p h x", h=4)).then_inc(self.read_done, 1)

                def operands(n):
                    m = LEVELS[n]

                    def cut(x):
                        return x.rearrange("p h t -> p (h t)").rearrange("p (c w) -> p c w", w=2 * m)
                    dve.wait_ge(self.e_ready, n + 2)
                    dve.wait_ge(self.kq_ready, n + 2)
                    dve.tensor_tensor(cut(hg_kh)[:, :, 0:m], cut(hg_k)[:, :, 0:m], cut(hg_e)[:, :, 0:m], ALU.mult)
                    dve.tensor_tensor(cut(hg_qh)[:, :, m:2 * m], cut(hg_q)[:, :, m:2 * m], cut(hg_e)[:, :, m:2 * m],
                                      ALU.mult).then_inc(self.kq_ready, 1)

                for n, m in enumerate(LEVELS):
                    operands(n)
                    dve.wait_ge(self.mm_done, n + 4)
                    dve.wait_ge(self.read_done, n + 3)
                    mask = consts[:, C_LEVEL + 64 * n:C_LEVEL + 64 * (n + 1)].bitcast(U32)\
                        .rearrange("p (c w) -> p c w", w=m).unsqueeze(1).to_broadcast([P, 8, 64 // m, m])
                    o = hg_st.rearrange("p b (c w) -> p b c w", w=2 * m)[:, :, :, m:2 * m]
                    src = PS[:, n % 2, :].rearrange("p (b c w) -> p b c w", b=8, w=m)
                    dve.copy_predicated(o, mask, src).then_inc(self.read_done, 1)

        class RecOut:

            def __init__(self, att, rec, norm):
                self.att, self.rec, self.norm = att, rec, norm
                self.fox_read = sem("mix_fox_read")

            def dve_fox(self, dve):
                dve.wait_ge(self.att.out_ready, 8)
                for tb in range(TB):
                    dve.tensor_tensor(XN[:, tb, 0:512].rearrange("p (h d) -> p h d", d=HD),
                                      PS[:, 4 + tb, :].rearrange("p (h d) -> p h d", d=HD),
                                      rinv[:, 0:8, tb:tb + 1].to_broadcast([P, 8, HD]), ALU.mult)\
                       .then_inc(self.fox_read, 1)

            def dve(self, dve):
                dve.wait_ge(self.rec.o_done, 1)
                dve.wait_ge(self.fox_read, 2)
                for tb in range(TB):
                    m = dve.tensor_copy(XN[:, tb, 512:1024], PS[:, 2 + tb, :])
                dlink(dve, m)
                sq = arena[:, 4096:6144].rearrange("p (t n) -> p t n", t=TB)
                dlink(dve, dve.tensor_tensor(sq, XN[:, :, :], XN[:, :, :], ALU.mult))
                for tb in range(TB):
                    dve.tensor_reduce(ss[:, tb * 12:tb * 12 + 8], sq[:, tb, 0:512].rearrange("p (h d) -> p h d", d=HD),
                                      AX_X, ALU.add)
                    m = dve.tensor_reduce(ss[:, tb * 12 + 8:tb * 12 + 12],
                                          sq[:, tb, 512:1024].rearrange("p (h d) -> p h d", d=P), AX_X, ALU.add)
                dlink(dve, m)
                s3 = ss[:, 0:24].rearrange("p (t h) -> p t h", t=TB)
                dve.tensor_scalar(s3[:, :, 0:8], s3[:, :, 0:8], 1.0 / HD, EPS_RMS, ALU.mult, ALU.add)
                dlink(dve, dve.tensor_scalar(s3[:, :, 8:12], s3[:, :, 8:12], 1.0 / P, EPS_RMS, ALU.mult, ALU.add))
                rsqrt(dve, ss[:, 0:24], 24)
                dve.wait_ge(self.rec.gate_ready, 1)
                for tb in range(TB):
                    x = XN[:, tb, 512:1024]
                    dlink(dve, dve.tensor_tensor(x.rearrange("p (h d) -> p h d", d=P),
                                                 x.rearrange("p (h d) -> p h d", d=P),
                                                 ss[:, tb * 12 + 8:tb * 12 + 12].unsqueeze(2).to_broadcast([P, 4, P]),
                                                 ALU.mult))
                    dve.tensor_tensor(x, x, hg_gate[:, tb, :], ALU.mult)
                    y = XN[:, tb, 0:512].rearrange("p (h d) -> p h d", d=HD)
                    dve.tensor_tensor(y, y, ss[:, tb * 12:tb * 12 + 8].unsqueeze(2).to_broadcast([P, 8, HD]), ALU.mult)\
                       .then_inc(self.norm.normed, 1)

        G_FFN1, G_MIX, G_FFN2, G_OUT = 0, 16, 32, 48
        n_ffn1_0 = Norm(0, G_FFN1)
        n_mix_0 = Norm(1, G_MIX)
        n_ffn2_0 = Norm(2, G_FFN2)
        n_ffn1_1 = Norm(3, G_FFN1 + 8)
        n_mix_1 = Norm(4, G_MIX + 8)
        n_ffn2_1 = Norm(5, G_FFN2 + 8)
        n_emb = Norm(6, None, X)
        n_gated = Norm(7, G_OUT, XN)
        n_conv = Norm(8, None, X)
        final_x = sem("final_x")
        mixed_x = sem("mixed_x")
        conv_x = sem("conv_x")
        out_x = sem("out_x")

        def even_q(g, tb):
            br, h = divmod(g, 8)
            base = (h // 4) * HD
            return QKT[base:base + HD, 5 * br + h % 4, tb * P:(tb + 1) * P]

        def even_k(g):
            br, h = divmod(g, 8)
            base = (h // 4) * HD
            return QKT[base:base + HD, 5 * br + 4, :]

        def even_v(g, kb):
            br, h = divmod(g, 8)
            at = 768 * br + 640 + (h // 4) * HD
            return PJ[:, kb, at:at + HD]

        att_even = Attention("att_even", 16, even_q, even_k, even_v, lambda g: None if g < 8 else win_mask,
                             lambda g: None if g < 8 else sink[:, g - 8:g - 7])
        att_odd = Attention("att_odd", 16,
                            lambda g, tb: QKT[(g % 2) * HD:(g % 2) * HD + HD, g // 2, tb * P:(tb + 1) * P],
                            lambda g: QKT[(g % 2) * HD:(g % 2) * HD + HD, 8 + g // 2, :],
                            lambda g, kb: V[:, kb, g * HD:(g + 1) * HD], lambda g: bias[:, g], rows_reversed=True)
        att_fox = Attention("att_fox", 8,
                            lambda g, tb: QKT[(g % 2) * HD:(g % 2) * HD + HD, g // 2, tb * P:(tb + 1) * P],
                            lambda g: QKT[(g % 2) * HD:(g % 2) * HD + HD, 4 + g // 2, :],
                            lambda g, kb: V[:, kb, g * HD:(g + 1) * HD], lambda g: fox_bias[:, g], token_out=True)
        even_in = EvenIn(n_mix_0, att_even)
        odd_in = OddIn(n_mix_1, att_odd)
        rec_in = RecIn(n_emb, att_fox)
        rec = Recurrence(att_fox)
        rec_out = RecOut(att_fox, rec, n_gated)
        ffn1_0 = Ffn(0, "ffn1_0", io["ffn1_w_gate"][0], io["ffn1_w_up"][0], io["ffn1_w_down"][0], n_ffn1_0, n_mix_0.x_ready)
        even_out = OutProj("even_out", io["even_w_out"][0], att_even.ready, n_ffn2_0.x_ready)
        ffn2_0 = Ffn(1, "ffn2_0", io["ffn2_w_gate"][0], io["ffn2_w_up"][0], io["ffn2_w_down"][0], n_ffn2_0, n_ffn1_1.x_ready)
        ffn1_1 = Ffn(2, "ffn1_1", io["ffn1_w_gate"][1], io["ffn1_w_up"][1], io["ffn1_w_down"][1], n_ffn1_1, n_mix_1.x_ready)
        odd_out = OutProj("odd_out", io["odd_w_out"][0], att_odd.ready, n_ffn2_1.x_ready)
        ffn2_1 = Ffn(3, "ffn2_1", io["ffn2_w_gate"][1], io["ffn2_w_up"][1], io["ffn2_w_down"][1], n_ffn2_1, final_x)
        rec_proj = OutProj("rec_out", io["w_o_2"][0], n_gated.ready, mixed_x, alpha=ALPHA)
        w_up = io["w_up_2"][0]
        conv_ffn = Ffn(4, "conv_ffn", w_up[:, 0:FF], w_up[:, FF:2 * FF], io["w_down_2"][0], n_conv, conv_x, conv=True)

        x_in = sem("x_in")
        consts_in = sem("consts_in")
        rows_in = sem("rows_in")
        rows_turned = sem("rows_turned")
        cols_ready = sem("cols_ready")
        sink_in = sem("sink_in")
        bias_in = sem("bias_in")
        bias_masked = sem("bias_masked")
        even_done = sem("even_done")
        vec_in = sem("vec_in")
        vec2_in = sem("vec2_in")
        vec3_in = sem("vec3_in")
        vec_used = sem("vec_used")
        out_stored = sem("out_stored")

        norm_rows = pt_sb[0:56, 0, 0, 0:P]
        conv_rows = s_sb[0:44, 0, :].rearrange("p (a n) -> p a n", a=4)

        block = ctx.enter_context(nc.Block())

        @block.sync
        def _(sp):
            sp.dma_start(consts[:, :], io["consts"][:, 0:C_SEL]).then_inc(consts_in, 16)
            ffn1_0.sp(sp)
            even_in.sp(sp, io["even_w_in"][0])
            even_out.sp(sp)
            ffn2_0.sp(sp)
            ffn1_1.sp(sp)
            odd_in.sp(sp, io["odd_w_qkv"][0])
            odd_out.sp(sp)
            ffn2_1.sp(sp)
            rec_in.sp(sp, io["w_in_2"][0])
            rec_proj.sp(sp)
            conv_ffn.sp(sp)
            for tb in range(TB):
                sp.wait_ge(out_x, tb + 1)
                sp.dma_start(out[0, tb * P:(tb + 1) * P, :], X[:, tb, :]).then_inc(out_stored, 16)
            sp.wait_ge(out_stored, 16 * TB)

        @block.gpsimd
        def _(pool):
            pool.dma_start(sink[:, :], io["b_sink"][0].partition_broadcast(P)).then_inc(sink_in, 16)
            pool.dma_start(fbias[:, :], io["fox_f_bias_2"][0].rearrange("(h a) -> h a", a=1)).then_inc(sink_in, 16)
            q = bass.AP(tensor=io["a_q_norm"].tensor, offset=0, ap=[[0, P], [0, 8], [1, HD]])
            k = bass.AP(tensor=io["a_k_norm"].tensor, offset=0, ap=[[0, P], [0, 2], [1, HD]])
            pool.dma_start(qk_gain[:, 0:512].rearrange("p (h d) -> p h d", d=HD), q).then_inc(even_in.const, 16)
            pool.dma_start(qk_gain[:, 512:640].rearrange("p (h d) -> p h d", d=HD), k).then_inc(even_in.const, 16)
            pool.wait_ge(consts_in, 16)
            even_in.pool(pool)
            pool.wait_ge(even_done, 1)
            table = io["c_rel_bias"].tensor
            for h in range(16):
                for r in range(4):
                    tb, base = divmod(r * GRID_W, P)
                    src = bass.AP(tensor=table, offset=h * REL_H * REL_W + (7 - r) * REL_W - 48,
                                  ap=[[1, GRID_W], [REL_W, 4], [1, GRID_W]])
                    pool.dma_start(bias[base:base + GRID_W, h, tb, :].rearrange("p (a k) -> p a k", a=4), src)\
                        .then_inc(bias_in, 16)
            pool.wait_ge(bias_in, 16 * 64)
            for h in range(16):
                for tb in range(TB):
                    plink(pool, pool.tensor_scalar(bias[:, h, tb, :], bias[:, h, tb, :], 8.0, None, ALU.mult))
                    pool.tensor_tensor(bias[:, h, tb, :], bias[:, h, tb, :], nb_mask, ALU.add).then_inc(bias_masked, 1)
            pool.dma_start(rowvec[:, 0, :], io["final_norm"].partition_broadcast(P)).then_inc(vec_in, 16)
            pool.dma_start(rowvec[:, 1, :], io["ln_emb_g_2"].partition_broadcast(P)).then_inc(vec_in, 16)
            pool.wait_ge(att_odd.lo, 8)
            pool.dma_start(V[:, 0, :], io["ln_emb_b_2"].partition_broadcast(P)).then_inc(vec_in, 16)
            pool.wait_ge(n_emb.normed, 7 * TB)
            pool.dma_start(wf, io["w_in_2"][0, :, FA:FA + 8].rearrange("(k p) n -> p k n", p=P)).then_inc(rec_in.wf_in, 16)
            pool.dma_start(sel, io["consts"][0:8, C_SEL:C_N].rearrange("p (h q) -> p h q", h=8)).then_inc(rec_in.wf_in, 16)
            pool.dma_start(rowvec[:, 0, :], io["ln_mix_g_2"][0].partition_broadcast(P)).then_inc(vec2_in, 16)
            pool.dma_start(rowvec[:, 1, :], io["ln_mix_b_2"][0].partition_broadcast(P)).then_inc(vec2_in, 16)
            rec.pool(pool)
            pool.wait_ge(n_conv.normed, 9 * TB)
            pool.dma_start(rowvec[:, 0, :], io["ln_ffn_g_2"][0].partition_broadcast(P)).then_inc(vec3_in, 16)
            pool.dma_start(rowvec[:, 1, :], io["ln_ffn_b_2"][0].partition_broadcast(P)).then_inc(vec3_in, 16)
            pool.wait_ge(vec3_in, 32)

        @block.scalar
        def _(act):
            act.dma_start(X[:, :, :], io["x"][0].rearrange("(t p) n -> p t n", p=P)).then_inc(x_in, 16)
            for n, name in enumerate(("ffn1_norm", "mix_norm", "ffn2_norm")):
                act.dma_start(norm_rows[16 * n:16 * n + 16, :], io[name].rearrange("l (k n) -> (l k) n", n=P))\
                   .then_inc(rows_in, 16)
            act.dma_start(norm_rows[48:52, :], io["fox_norm_g_2"].rearrange("l (k n) -> (l k) n", n=P)).then_inc(rows_in, 16)
            act.dma_start(norm_rows[52:56, :], io["hgrn_norm_g_2"].rearrange("l (k n) -> (l k) n", n=P)).then_inc(rows_in, 16)
            act.dma_start(conv_rows[:, 0:3, :], io["conv_w_2"][0].rearrange("a (k n) -> k a n", n=P)).then_inc(rows_in, 16)
            act.dma_start(conv_rows[:, 3, :], io["conv_b_2"][0].rearrange("(k n) -> k n", n=P)).then_inc(rows_in, 16)
            split_hi(act, 0)
            split_hi(act, 1)
            act.wait_ge(x_in, 16)
            act.wait_ge(cols_ready, 2)
            n_ffn1_0.act(act)
            ffn1_0.act(act)
            n_mix_0.act(act)
            even_in.act(act)
            act.wait_ge(sink_in, 32)
            att_even.act(act)
            even_out.act(act)
            n_ffn2_0.act(act)
            ffn2_0.act(act)
            n_ffn1_1.act(act)
            ffn1_1.act(act)
            n_mix_1.act(act)
            odd_in.act(act)
            att_odd.act(act)
            odd_out.act(act)
            n_ffn2_1.act(act)
            ffn2_1.act(act)
            n_emb.act(act)
            rec_in.act(act)
            rec.act_silu(act)
            att_fox.act(act)
            rec.act(act)
            n_gated.act(act)
            rec_proj.act(act)
            n_conv.act(act)
            conv_ffn.act(act)

        @block.vector
        def _(dve):
            split_lo(dve, 0)
            split_lo(dve, 1)
            dve.wait_ge(rows_turned, 1)
            dve.tensor_copy(cols[:, :], PS[:, 7, 0:56]).then_inc(cols_ready, 1)
            dve.tensor_copy(convc[:, :, :], PS[:, 7, 64:240].rearrange("p (a k) -> p a k", a=4)).then_inc(cols_ready, 1)
            dve.wait_ge(x_in, 16)
            dve.wait_ge(cols_ready, 2)
            dve.tensor_copy(ss[:, 20:21], cols[:, 0:1]).then_inc(n_ffn1_0.x_ready, 1)
            n_ffn1_0.dve(dve)
            ffn1_0.dve(dve)
            n_mix_0.dve(dve)
            even_in.dve(dve)
            dve.wait_ge(sink_in, 32)
            att_even.dve(dve)
            dve.tensor_copy(ss[:, 20:21], cols[:, 0:1]).then_inc(even_done, 1)
            even_out.dve(dve)
            n_ffn2_0.dve(dve)
            ffn2_0.dve(dve)
            n_ffn1_1.dve(dve)
            ffn1_1.dve(dve)
            n_mix_1.dve(dve)
            odd_in.dve(dve)
            dve.wait_ge(bias_masked, 32)
            att_odd.dve(dve)
            odd_out.dve(dve)
            n_ffn2_1.dve(dve)
            ffn2_1.dve(dve)
            dve.wait_ge(final_x, 1)
            for tb in range(TB):
                m = dve.tensor_tensor_reduce(XN[:, tb, :], X[:, tb, :], X[:, tb, :], 1.0 / DM, 0.0,
                                             ALU.mult, ALU.add, ss[:, tb:tb + 1])
            dlink(dve, m)
            dlink(dve, dve.tensor_scalar(ss[:, 0:2], ss[:, 0:2], EPS_RMS, None, ALU.add))
            rsqrt(dve, ss[:, 0:2], 2)
            dve.wait_ge(vec_in, 48)
            for tb in range(TB):
                m = dve.scalar_tensor_tensor(X[:, tb, :], X[:, tb, :], ss[:, tb:tb + 1], rowvec[:, 0, :],
                                             ALU.mult, ALU.mult)
            dlink(dve, m)
            layer_norm(dve, rowvec[:, 1, :], V[:, 0, :], n_emb.normed)
            n_emb.dve(dve)
            rec_in.dve(dve)
            rec.dve_gates(dve)
            att_fox.dve(dve)
            rec_out.dve_fox(dve)
            rec.dve(dve)
            rec_out.dve(dve)
            n_gated.dve(dve)
            rec_proj.dve(dve)
            dve.wait_ge(mixed_x, 1)
            dve.wait_ge(vec2_in, 32)
            layer_norm(dve, rowvec[:, 0, :], rowvec[:, 1, :], n_conv.normed)
            n_conv.dve(dve)
            conv_ffn.dve(dve)
            dve.wait_ge(conv_x, 1)
            dve.wait_ge(vec3_in, 32)
            layer_norm(dve, rowvec[:, 0, :], rowvec[:, 1, :], out_x)

        @block.tensor
        def _(pe):
            pe.wait_ge(consts_in, 16)
            pe.wait_ge(rows_in, 16 * 7)
            pe.transpose(PS[:, 7, 0:56], norm_rows, consts[0:56, C_IDENT:C_IDENT + 56])
            for a in range(4):
                m = pe.transpose(PS[:, 7, 64 + 44 * a:64 + 44 * (a + 1)], conv_rows[:, a, :],
                                 consts[0:44, C_IDENT:C_IDENT + 44])
            m.then_inc(rows_turned, 1)
            n_ffn1_0.pe(pe)
            ffn1_0.pe(pe)
            n_mix_0.pe(pe)
            even_in.pe(pe)
            att_even.pe(pe)
            even_out.pe(pe)
            n_ffn2_0.pe(pe)
            ffn2_0.pe(pe)
            n_ffn1_1.pe(pe)
            ffn1_1.pe(pe)
            n_mix_1.pe(pe)
            odd_in.pe(pe)
            att_odd.pe(pe)
            odd_out.pe(pe)
            n_ffn2_1.pe(pe)
            ffn2_1.pe(pe)
            n_emb.pe(pe)
            rec_in.pe(pe)
            att_fox.pe(pe)
            rec.pe(pe)
            n_gated.pe(pe)
            rec_proj.pe(pe)
            n_conv.pe(pe)
            conv_ffn.pe(pe)


_INS = ["x", "ffn1_norm", "ffn1_w_gate", "ffn1_w_up", "ffn1_w_down", "mix_norm", "ffn2_norm", "ffn2_w_gate",
        "ffn2_w_up", "ffn2_w_down", "even_w_in", "a_q_norm", "a_k_norm", "b_sink", "even_w_out", "odd_w_qkv",
        "c_rel_bias", "odd_w_out", "final_norm", "ln_emb_g_2", "ln_emb_b_2", "w_in_2", "fox_f_bias_2",
        "fox_norm_g_2", "hgrn_norm_g_2", "w_o_2", "ln_mix_g_2", "ln_mix_b_2", "w_up_2", "conv_w_2", "conv_b_2",
        "w_down_2", "ln_ffn_g_2", "ln_ffn_b_2"]


def kernel(**inputs):
    import numpy as _np
    import concourse.bacc as _bacc
    from concourse import mybir as _mybir
    from concourse.bass_utils import run_bass_kernel_spmd as _run

    nc = _bacc.Bacc("TRN2", target_bir_lowering=False, num_devices=1)
    arrays, io = {}, {}
    for name in _INS + ["consts"]:
        if name == "consts":
            a = constant_table()
        elif name == "c_rel_bias":
            a = _np.ascontiguousarray(inputs[name][..., ::-1])
        else:
            a = _np.ascontiguousarray(inputs[name])
        arrays[f"in_{name}_dram"] = a
        io[name] = nc.dram_tensor(f"in_{name}_dram", a.shape, _mybir.dt.from_np(a.dtype), kind="ExternalInput").ap()
    out = nc.dram_tensor("out_0_dram", (1, S, DM), F32, kind="ExternalOutput").ap()
    build(nc, io, out)
    r = _run(nc, [arrays], core_ids=[0])
    return r.results[0]["out_0_dram"]
```

```python
from contextlib import ExitStack

import numpy as np

import concourse.bass as bass
from concourse import mybir

F32 = mybir.dt.float32
F32R = mybir.dt.float32r
I32 = mybir.dt.int32
U32 = mybir.dt.uint32
ACT = mybir.ActivationFunctionType
ALU = mybir.AluOpType
AX_X = mybir.AxisListType.X

P = 128
S = 256
TB = S // P
DM = 1024
KC = DM // P
FF = 2816
UNIT = 2048
RING = 3
LOOKAHEAD = 2
FF_STEPS = FF // 256
EPS_RMS = 1e-6
EPS_LN = 1e-5
ALPHA = 2.0 ** 0.25
NEG = -1e30
HD = 64
SCALE = HD ** -0.5
GRID_W = 64
NA_KW = 16
REL_W = 2 * NA_KW - 1
REL_H = 15
LEVELS = (32, 16, 8, 4, 2, 1)
RSQRT_MAGIC = 1597463007.0

C_IDENT = 0
C_ROPE = C_IDENT + P
C_WIN = C_ROPE + 4 * TB * HD
C_NB = C_WIN + TB * S
C_CAUSAL = C_NB + S
C_LEVEL = C_CAUSAL + TB * S
C_ZERO = C_LEVEL + 64 * len(LEVELS)
C_SEL = C_ZERO + 64
C_N = C_SEL + 8 * P


def constant_table():
    t = np.zeros((P, C_N), np.float32)
    t[:, C_IDENT:C_IDENT + P] = np.eye(P, dtype=np.float32)
    pos = np.arange(S)

    def angles(at, dim):
        inv = (np.float32(10000.0) ** (-np.arange(0, dim, 2, dtype=np.float32) / np.float32(dim))).astype(np.float32)
        a = (at.astype(np.float32)[:, None] * inv[None, :]).astype(np.float32).astype(np.float64)
        return np.cos(a).astype(np.float32), np.sin(a).astype(np.float32)

    cr, sr = angles(pos // GRID_W, HD // 2)
    cc, sc = angles(pos % GRID_W, HD // 2)
    c1, s1 = angles(pos, HD)
    rope = [np.concatenate([cr, cr, cc, cc], 1), np.concatenate([-sr, sr, -sc, sc], 1),
            np.concatenate([c1, c1], 1), np.concatenate([-s1, s1], 1)]
    for n, r in enumerate(rope):
        for tb in range(TB):
            at = C_ROPE + (n * TB + tb) * HD
            t[:, at:at + HD] = r[tb * P:(tb + 1) * P]
    key = np.arange(S)[None, :]
    for tb in range(TB):
        q = tb * P + np.arange(P)[:, None]
        t[:, C_WIN + tb * S:C_WIN + (tb + 1) * S] = np.where(np.abs(q - key) <= 128, 0, 8 * NEG)
        t[:, C_CAUSAL + tb * S:C_CAUSAL + (tb + 1) * S] = np.where(key <= q, 0, 8 * NEG)
    c = np.arange(P)[:, None] % GRID_W
    first = np.clip(c - NA_KW // 2, 0, GRID_W - NA_KW)
    kc = key % GRID_W
    kc = GRID_W - 1 - kc
    t[:, C_NB:C_NB + S] = np.where((kc >= first) & (kc < first + NA_KW), 0, 8 * NEG)
    s = np.arange(P)[:, None]
    for n, m in enumerate(LEVELS):
        late = np.array([x for x in range(P) if x % (2 * m) >= m])[None, :]
        ok = (s // (2 * m) == late // (2 * m)) & (s % (2 * m) < m)
        t[:, C_LEVEL + 64 * n:C_LEVEL + 64 * (n + 1)] = ok
    for h in range(8):
        t[h, C_SEL + h * P:C_SEL + (h + 1) * P] = 1
    return t


def build(nc, io, out):
    ctx = ExitStack()
    with ctx:
        def sb(name, shape, dt=F32):
            return ctx.enter_context(nc.sbuf_tensor(name, shape, dt))

        def sem(name):
            return ctx.enter_context(nc.semaphore(name))

        raw = [sb(f"raw{n}", [P, UNIT]) for n in range(RING)]
        w_hi = [sb(f"w_hi{n}", [P, UNIT], F32R) for n in range(RING)]
        w_lo = [sb(f"w_lo{n}", [P, UNIT], F32R) for n in range(RING)]
        X = sb("x_tok", [P, TB, DM])
        XN = sb("xn_tok", [P, TB, DM])
        T = sb("t_feat", [P, KC, S])
        h_hi = sb("h_hi", [P, KC, S], F32R)
        h_lo = sb("h_lo", [P, KC, S], F32R)
        gu_hi = sb("gu_hi", [P, 2, S], F32R)
        gu_lo = sb("gu_lo", [P, 2, S], F32R)
        consts = sb("consts", [P, C_SEL])
        rowvec = sb("rowvec", [P, 2, DM])
        QKT = sb("qk_feat", [P, 16, S])
        V = sb("v_tok", [P, TB, DM])
        s_sb = sb("s_sb", [P, 2, 512])
        p_sb = sb("p_sb", [P, 2, 512])
        pt_sb = sb("pt_sb", [P, 2, 2, S])
        arena = sb("arena", [P, 8192])
        convc = sb("convc", [P, 4, 44])
        ss = sb("ss", [P, 24])
        nt = sb("nt", [P, 4, 24])
        mx = sb("mx", [P, 16, 2])
        negm = sb("negm", [P, 16, 2])
        rsum = sb("rsum", [P, 16, 2])
        rinv = sb("rinv", [P, 16, 2])
        esink = sb("esink", [P, 8, 2])
        sink = sb("sink", [P, 8])
        fbias = sb("fbias", [8, 1])
        bn = sb("bn", [P, TB, 2, 6])
        mv = sb("mv", [P, TB, 2])
        cq = sb("cq", [P, TB, 8])
        PS = ctx.enter_context(nc.psum_tensor("ps", [P, 8, 512], F32))

        ident = consts[:, C_IDENT:C_IDENT + P]

        def rope_tab(n, tb):
            at = C_ROPE + (n * TB + tb) * HD
            return consts[:, at:at + HD]

        win_mask = consts[:, C_WIN:C_WIN + TB * S].rearrange("p (t k) -> p t k", t=TB)
        nb_mask = consts[:, C_NB:C_NB + S]
        causal_mask = consts[:, C_CAUSAL:C_CAUSAL + TB * S].rearrange("p (t k) -> p t k", t=TB)
        zeros = consts[:, C_ZERO:C_ZERO + 64]

        ffn_act = s_sb[:, 0, :]
        ffn_up = s_sb[:, 1, :]
        ffn_gu = p_sb[:, 0, :]
        PJ = arena[:, 0:3072].rearrange("p (t n) -> p t n", t=TB)
        R = arena[:, 3072:5632].rearrange("p (t n) -> p t n", t=TB)
        rope_t1 = arena[:, 5632:6912].rearrange("p (b n) -> p b n", b=2)
        rope_t2 = arena[:, 6912:8192].rearrange("p (b n) -> p b n", b=2)
        qk_gain = QKT[:, 10:13, :].rearrange("p a b -> p (a b)")[:, 0:640]
        bias = arena[:, :].rearrange("p (h t k) -> p h t k", h=16, t=TB)
        fox_bias = arena[:, 0:4096].rearrange("p (h t k) -> p h t k", h=8, t=TB)
        hg_b = arena[:, 4096:5120].rearrange("p (h t) -> p h t", h=4)
        hg_k = arena[:, 5120:6144].rearrange("p (h t) -> p h t", h=4)
        hg_d = arena[:, 6144:7168].rearrange("p (h t) -> p h t", h=4)
        hg_gate = arena[:, 7168:8192].rearrange("p (t n) -> p t n", t=TB)
        hg_e = arena[:, 0:1024].rearrange("p (h t) -> p h t", h=4)
        hg_kh = arena[:, 1024:2048].rearrange("p (h t) -> p h t", h=4)
        hg_qh = arena[:, 2048:3072].rearrange("p (h t) -> p h t", h=4)
        hg_st = arena[:, 3072:4096].rearrange("p (b t) -> p b t", b=8)
        hg_s2 = T[:, 0:2, :].rearrange("p a b -> p (a b)").rearrange("p (h t) -> p h t", h=4)
        hg_q = QKT[:, 8:12, :]
        hg_f = QKT[:, 12:16, :]
        wf = s_sb[:, 0, 0:64].rearrange("p (k n) -> p k n", k=KC)
        sel = XN[0:8, 0, :].rearrange("p (h q) -> p h q", h=8)
        f_z = p_sb[0:8, 0, 0:256]
        f_a = p_sb[0:8, 0, 256:512]
        f_m = p_sb[0:8, 1, 0:256]
        f_c = p_sb[0:8, 1, 256:512]

        w_landed = [sem(f"w_landed{n}") for n in range(RING)]
        w_hi_ready = sem("w_hi_ready")
        w_lo_ready = sem("w_lo_ready")
        w_released = sem("w_released")
        bank_done = sem("bank_done")
        out_bank_done = sem("out_bank_done")
        gain_in = sem("gain_in")
        FFN_UNITS = 3 * FF_STEPS
        sizes = [("ffn1_0", FFN_UNITS), ("even_in", 6), ("even_out", 4), ("ffn2_0", FFN_UNITS),
                 ("ffn1_1", FFN_UNITS), ("odd_in", 12), ("odd_out", 4), ("ffn2_1", FFN_UNITS),
                 ("rec_in", 14), ("rec_out", 4), ("conv_ffn", FFN_UNITS)]
        first_unit, total = {}, 0
        for name, n in sizes:
            first_unit[name] = total
            total += n
        TOTAL_UNITS = total

        def split_hi(act, n, i=0):
            if isinstance(i, int) and n + 3 * i >= TOTAL_UNITS:
                return
            slot = n % RING
            act.wait_ge(w_landed[slot], 16 * i + 16 * (n // RING + 1))
            if n >= RING:
                act.wait_ge(w_released, 3 * i + (n - RING + 1))
            act.activation(w_hi[slot][:, :], raw[slot][:, :], ACT.Copy).then_inc(w_hi_ready, 1)

        def split_lo(dve, n, i=0):
            if isinstance(i, int) and n + 3 * i >= TOTAL_UNITS:
                return
            slot = n % RING
            dve.wait_ge(w_hi_ready, 3 * i + (n + 1))
            dve.tensor_tensor(w_lo[slot][:, :], raw[slot][:, :], w_hi[slot][:, :].bitcast(F32),
                              ALU.subtract).then_inc(w_lo_ready, 1)

        def load_unit(sp, n, src, view, i=0):
            slot = n % RING
            if n >= RING:
                sp.wait_ge(w_lo_ready, 3 * i + (n - RING + 1))
            sp.dma_start(view(raw[slot]), src).then_inc(w_landed[slot], 16)

        def feat_view(w):
            return w[:, :].rearrange("p (k n) -> p k n", k=KC)

        def tok_view(w):
            return w[:, :].rearrange("p (k n) -> p k n", k=4)

        def down_view(w):
            return w[:, :].rearrange("p (k n) -> p k n", k=2)

        def feat_src(w, col):
            return w[:, bass.ds(col, 256)].rearrange("(k p) n -> p k n", p=P)

        def tok_src(w, half, col):
            return w[half * 512:(half + 1) * 512, col:col + 512].rearrange("(k p) n -> p k n", p=P)

        def down_src(w, row):
            return w[bass.ds(row, 256), :].rearrange("(k p) n -> p k n", p=P)

        def three(mm, o, ahi, alo, bhi, blo, first, last):
            mm(o, ahi, bhi, start=first, stop=False)
            mm(o, alo, bhi, start=False, stop=False)
            return mm(o, ahi, blo, start=False, stop=last)

        def feat_unit(pe, n, bank, i=0, ready=None):
            slot = n % RING
            pe.wait_ge(w_lo_ready, 3 * i + (n + 1))
            for t in range(2):
                for k in range(KC):
                    if ready is not None and t == 0:
                        ready(pe, k)
                    a, b = feat_view(w_hi[slot]), feat_view(w_lo[slot])
                    last = three(pe.matmul, PS[:, bank, t * S:(t + 1) * S],
                                 a[:, k, t * P:(t + 1) * P], b[:, k, t * P:(t + 1) * P],
                                 h_hi[:, k, :], h_lo[:, k, :], k == 0, k == KC - 1)
            last.then_inc(w_released, 1)

        def tok_unit(pe, n, half, banks, ready=None, done=None):
            slot = n % RING
            pe.wait_ge(w_lo_ready, n + 1)
            a, b = tok_view(w_hi[slot]), tok_view(w_lo[slot])
            for tb in range(TB):
                for k in range(4):
                    kk = 4 * half + k
                    if ready is not None and tb == 0:
                        ready(pe, kk)
                    last = three(pe.matmul, PS[:, banks[tb], :],
                                 h_hi[:, kk, tb * P:(tb + 1) * P], h_lo[:, kk, tb * P:(tb + 1) * P],
                                 a[:, k, :], b[:, k, :], kk == 0, kk == KC - 1)
                if done is not None and tb == 0:
                    last.then_inc(done, 1)
            last.then_inc(w_released, 1)

        def down_unit(pe, n, first, last_unit, i=0):
            slot = n % RING
            pe.wait_ge(w_lo_ready, 3 * i + (n + 1))
            a, b = down_view(w_hi[slot]), down_view(w_lo[slot])
            for tb in range(TB):
                for half in range(2):
                    for k in range(2):
                        last = three(pe.matmul, PS[:, 4 + 2 * tb + half, :],
                                     gu_hi[:, k, tb * P:(tb + 1) * P], gu_lo[:, k, tb * P:(tb + 1) * P],
                                     a[:, k, half * 512:(half + 1) * 512], b[:, k, half * 512:(half + 1) * 512],
                                     first and k == 0, last_unit and k == 1)
                    if last_unit and (tb, half) != (1, 1):
                        last.then_inc(bank_done, 1)
            return last.then_inc(w_released, 1)

        def chain(name):
            step, count = sem(name), [0]

            def link(eng, ins):
                count[0] += 1
                ins.then_inc(step, 1)
                eng.wait_ge(step, count[0])
            return link

        dlink = chain("dve_step")
        alink = chain("act_step")
        plink = chain("pool_step")

        def rsqrt(dve, x, n):
            y, t, u = nt[:, 0, 0:n], nt[:, 1, 0:n], nt[:, 2, 0:n]
            dlink(dve, dve.tensor_scalar(y.bitcast(I32), x.bitcast(I32), -0.5, RSQRT_MAGIC, ALU.mult, ALU.add))
            for step in range(3):
                dlink(dve, dve.tensor_tensor(t, y, y, ALU.mult))
                dlink(dve, dve.scalar_tensor_tensor(u, t, -0.5, x, ALU.mult, ALU.mult))
                o = x if step == 2 else y
                dlink(dve, dve.scalar_tensor_tensor(o, u, 1.5, y, ALU.add, ALU.mult))

        QUARTERS = [(0, 0), (1, 0), (0, 1), (1, 1)]

        class Norm:

            x_ready = sem("norm_x_ready")
            square = sem("norm_square")
            normed = sem("norm_normed")
            turned = sem("norm_turned")
            hi = sem("norm_hi")
            lo = sem("norm_lo")

            def __init__(self, at, src=None):
                self.at, self.rms = at, src is None
                self.src = XN if src is None else src
                self.gain = rowvec[:, at % 2, :]

            def pe(self, pe):
                for q, (tb, half) in enumerate(QUARTERS):
                    pe.wait_ge(self.normed, self.at * 4 + q + 1)
                    for k in range(4):
                        kk = 4 * half + k
                        m = pe.transpose(PS[:, q, k * P:(k + 1) * P], self.src[:, tb, kk * P:(kk + 1) * P], ident)
                    m.then_inc(self.turned, 1)

            def ready(self, pe, k):
                if k in (0, 4):
                    pe.wait_ge(self.lo, self.at * 4 + (2 if k == 0 else 4))

            def act(self, act, first=False):
                if self.rms:
                    for q, (tb, half) in enumerate(self.order):
                        if not first:
                            act.wait_ge(self.x_ready, self.at * 4 - 4 + q + 1)
                        act.activation(XN[:, tb, half * 512:(half + 1) * 512], X[:, tb, half * 512:(half + 1) * 512],
                                       ACT.Square, scale=1.0 / 32.0, accum_out=ss[:, 2 * half + tb:2 * half + tb + 1])\
                           .then_inc(self.square, 1)
                if first:
                    split_hi(act, 0)
                    split_hi(act, 1)
                for q, (tb, half) in enumerate(QUARTERS):
                    act.wait_ge(self.turned, self.at * 4 + q + 1)
                    act.activation(h_hi[:, 4 * half:4 * half + 4, tb * P:(tb + 1) * P],
                                   PS[:, q, :].rearrange("p (k t) -> p k t", k=4), ACT.Copy).then_inc(self.hi, 1)

            def dve(self, dve, first=False):
                if self.rms:
                    dve.wait_ge(self.square, self.at * 4 + 4)
                    dlink(dve, dve.scalar_tensor_tensor(ss[:, 0:2], ss[:, 0:2], EPS_RMS, ss[:, 2:4], ALU.add, ALU.add))
                    rsqrt(dve, ss[:, 0:2], 2)
                    dve.wait_ge(gain_in, 16 * (self.at + 1))
                    for tb, half in QUARTERS:
                        f = slice(half * 512, (half + 1) * 512)
                        dve.scalar_tensor_tensor(XN[:, tb, f], X[:, tb, f], ss[:, tb:tb + 1], self.gain[:, f],
                                                 ALU.mult, ALU.mult).then_inc(self.normed, 1)
                if first:
                    split_lo(dve, 0)
                    split_lo(dve, 1)
                for q, (tb, half) in enumerate(QUARTERS):
                    dve.wait_ge(self.hi, self.at * 4 + q + 1)
                    o = h_lo[:, 4 * half:4 * half + 4, tb * P:(tb + 1) * P]
                    h = h_hi[:, 4 * half:4 * half + 4, tb * P:(tb + 1) * P].bitcast(F32)
                    dve.tensor_tensor(o, PS[:, q, :].rearrange("p (k t) -> p k t", k=4), h, ALU.subtract)\
                       .then_inc(self.lo, 1)

        class Ffn:

            act_done = sem("ffn_act_done")
            gu_done = sem("ffn_gu_done")
            guhi_done = sem("ffn_guhi_done")
            gulo_done = sem("ffn_gulo_done")

            def __init__(self, at, name, wg, wu, wd, norm, after, conv=False):
                self.u0, self.b = first_unit[name], at * FF_STEPS
                self.wg, self.wu, self.wd, self.norm, self.conv = wg, wu, wd, norm, conv
                self.after, self.banks_before = after, 3 * at
                if conv:
                    self.tap2 = sem(name + "_tap2")
                    self.tap1 = sem(name + "_tap1")
                    self.a_conv = sem(name + "_a_conv")
                    self.u_conv = sem(name + "_u_conv")

            def sp(self, sp):
                u = self.u0
                load_unit(sp, u, feat_src(self.wg, 0), feat_view)
                load_unit(sp, u + 1, feat_src(self.wu, 0), feat_view)
                load_unit(sp, u + 2, feat_src(self.wg, 256), feat_view)
                load_unit(sp, u + 3, feat_src(self.wu, 256), feat_view)
                load_unit(sp, u + 4, down_src(self.wd, 0), down_view)
                with sp.Fori(0, FF_STEPS - 2) as i:
                    load_unit(sp, u + 5, feat_src(self.wg, i * 256 + 512), feat_view, i)
                    load_unit(sp, u + 6, feat_src(self.wu, i * 256 + 512), feat_view, i)
                    load_unit(sp, u + 7, down_src(self.wd, i * 256 + 256), down_view, i)
                load_unit(sp, u + 3 * FF_STEPS - 1, down_src(self.wd, FF - 256), down_view)

            def pe(self, pe):
                u = self.u0
                feat_unit(pe, u, 0, ready=self.norm.ready)
                self.up(pe, u + 1, 1, 0, None)
                self.up(pe, u + 2, 0, 0, 1)
                self.up(pe, u + 3, 1, 0, 1)
                pe.wait_ge(self.gulo_done, self.b + 1)
                down_unit(pe, u + 4, True, False)
                with pe.Fori(0, FF_STEPS - 2) as i:
                    self.up(pe, u + 5, 0, i, i + 2)
                    self.up(pe, u + 6, 1, i, i + 2)
                    pe.wait_ge(self.gulo_done, i + (self.b + 2))
                    down_unit(pe, u + 7, False, False, i)
                pe.wait_ge(self.gulo_done, self.b + FF_STEPS)
                down_unit(pe, u + 3 * FF_STEPS - 1, False, True)

            def up(self, pe, n, which, i, free):
                if free is not None:
                    if self.conv:
                        pe.wait_ge(self.a_conv if which == 0 else self.u_conv, free)
                    else:
                        pe.wait_ge(self.act_done if which == 0 else self.gu_done, free + self.b)
                feat_unit(pe, n, which, i)

            def conv_tap2(self, act, which, i, at):
                act.wait_ge(w_released, self.u0 + 1 + which + at)
                dst = ffn_act if which == 0 else ffn_up
                for t in range(2):
                    tile = i * 2 + (22 * which + t)
                    m = act.activation(dst[:, t * S:(t + 1) * S], PS[:, which, t * S:(t + 1) * S], ACT.Identity,
                                       bias=convc[:, 3, bass.ds(tile, 1)], scale=convc[:, 2, bass.ds(tile, 1)])
                m.then_inc(self.tap2, 1)

            def conv_taps(self, dve, which, i):
                dve.wait_ge(self.tap2, 2 * i + (which + 1))
                dst = ffn_act if which == 0 else ffn_up
                for t in range(2):
                    tile = i * 2 + (22 * which + t)
                    y = dst[:, t * S + 1:(t + 1) * S]
                    m = dve.scalar_tensor_tensor(y, PS[:, which, t * S:(t + 1) * S - 1],
                                                 convc[:, 1, bass.ds(tile, 1)], y, ALU.mult, ALU.add)
                m.then_inc(self.tap1, 1)
                dve.wait_ge(self.tap1, 2 * i + (which + 1))
                for t in range(2):
                    tile = i * 2 + (22 * which + t)
                    y = dst[:, t * S + 2:(t + 1) * S]
                    m = dve.scalar_tensor_tensor(y, PS[:, which, t * S:(t + 1) * S - 2],
                                                 convc[:, 0, bass.ds(tile, 1)], y, ALU.mult, ALU.add)
                m.then_inc(self.a_conv if which == 0 else self.u_conv, 1)

            def act_step(self, act, i, first):
                u, r = self.u0, (0 if first else i - 1)
                if first:
                    at_g, at_u = 0, 0
                    split_hi(act, u + 2)
                else:
                    at_g = 3 * r + 2
                    at_u = 3 * r + 2
                    split_hi(act, u + 4, i=r)
                if self.conv:
                    self.conv_tap2(act, 0, i, at_g)
                split_hi(act, u + 3 if first else u + 5, i=r)
                if self.conv:
                    self.conv_tap2(act, 1, i, at_u)
                    act.wait_ge(self.a_conv, i + 1)
                    act.activation(ffn_act, ffn_act, ACT.Gelu).then_inc(self.act_done, 1)
                else:
                    act.wait_ge(w_released, u + 1 + at_g)
                    act.activation(ffn_act, PS[:, 0, :], ACT.Silu).then_inc(self.act_done, 1)
                if not first:
                    split_hi(act, u + 6, i=r)
                act.wait_ge(self.gu_done, i + (self.b + 1))
                if not first:
                    act.wait_ge(w_released, u + 3 * r + 5)
                act.activation(gu_hi[:, :, :], ffn_gu.rearrange("p (t s) -> p t s", t=2), ACT.Copy)\
                   .then_inc(self.guhi_done, 1)

            def act(self, act):
                self.act_step(act, 0, True)
                self.act_step(act, 1, False)
                end = FF_STEPS - 2 if self.conv else FF_STEPS - 1
                with act.Fori(1, end) as i:
                    self.act_step(act, i + 1, False)
                if self.conv:
                    self.act_step(act, FF_STEPS - 1, False)
                split_hi(act, self.u0 + 3 * FF_STEPS + 1)

            def dve_step(self, dve, i, first):
                u, r = self.u0, (0 if first else i - 1)
                split_lo(dve, u + 2 if first else u + 4, i=r)
                if self.conv:
                    self.conv_taps(dve, 0, i)
                split_lo(dve, u + 3 if first else u + 5, i=r)
                if self.conv:
                    self.conv_taps(dve, 1, i)
                    dve.wait_ge(self.u_conv, i + 1)
                    dve.wait_ge(self.act_done, i + (self.b + 1))
                    if not first:
                        dve.wait_ge(self.gulo_done, i + self.b)
                    dve.tensor_tensor(ffn_gu, ffn_act, ffn_up, ALU.mult).then_inc(self.gu_done, 1)
                else:
                    dve.wait_ge(w_released, u + 2 if first else u + 3 * r + 4)
                    dve.wait_ge(self.act_done, i + (self.b + 1))
                    if not first:
                        dve.wait_ge(self.gulo_done, i + self.b)
                    dve.tensor_tensor(ffn_gu, PS[:, 1, :], ffn_act, ALU.mult).then_inc(self.gu_done, 1)
                if not first:
                    split_lo(dve, u + 6, i=r)
                dve.wait_ge(self.guhi_done, i + (self.b + 1))
                dve.tensor_tensor(gu_lo[:, :, :], ffn_gu.rearrange("p (t s) -> p t s", t=2),
                                  gu_hi[:, :, :].bitcast(F32), ALU.subtract).then_inc(self.gulo_done, 1)

            def dve(self, dve):
                self.dve_step(dve, 0, True)
                end = FF_STEPS - 2 if self.conv else FF_STEPS - 1
                with dve.Fori(0, end) as i:
                    self.dve_step(dve, i + 1, False)
                if self.conv:
                    self.dve_step(dve, FF_STEPS - 1, False)
                split_lo(dve, self.u0 + 3 * FF_STEPS + 1)
                for tb in range(TB):
                    for half in range(2):
                        if (tb, half) == (1, 1):
                            dve.wait_ge(w_released, self.u0 + 3 * FF_STEPS)
                        else:
                            dve.wait_ge(bank_done, self.banks_before + 2 * tb + half + 1)
                        x = X[:, tb, half * 512:(half + 1) * 512]
                        y = PS[:, 4 + 2 * tb + half, :]
                        if self.conv:
                            m = dve.scalar_tensor_tensor(x, x, ALPHA, y, ALU.mult, ALU.add)
                        else:
                            m = dve.scalar_tensor_tensor(x, y, 0.5, x, ALU.mult, ALU.add)
                        m.then_inc(self.after, 1)

        class OutProj:

            def __init__(self, name, w, ready, after, at, alpha=None, bank=0):
                self.u0, self.w, self.ready, self.after, self.alpha = first_unit[name], w, ready, after, alpha
                self.done, self.done_before, self.bank = out_bank_done, 2 * at, bank

            def sp(self, sp):
                for half in range(2):
                    for c in range(2):
                        load_unit(sp, self.u0 + 2 * half + c, tok_src(self.w, half, c * 512), tok_view)

            def pe(self, pe):
                for half in range(2):
                    for c in range(2):
                        tok_unit(pe, self.u0 + 2 * half + c, half, (self.bank + 2 * c, self.bank + 2 * c + 1),
                                 ready=self.ready if c == 0 else None, done=self.done if half else None)

            def act(self, act):
                for j in range(4):
                    split_hi(act, self.u0 + j + LOOKAHEAD)

            def dve(self, dve):
                for j in range(4):
                    split_lo(dve, self.u0 + j + LOOKAHEAD)
                for c in range(2):
                    for tb in range(TB):
                        if tb == 0:
                            dve.wait_ge(self.done, self.done_before + c + 1)
                        else:
                            dve.wait_ge(w_released, self.u0 + 3 + c)
                        x = X[:, tb, c * 512:(c + 1) * 512]
                        y = PS[:, self.bank + 2 * c + tb, :]
                        if self.alpha is None:
                            m = dve.tensor_tensor(x, y, x, ALU.add)
                        else:
                            m = dve.scalar_tensor_tensor(x, x, self.alpha, y, ALU.mult, ALU.add)
                        m.then_inc(self.after, 1)

        class Attention:

            def __init__(self, name, heads, q, k, v, bias, sink_of=None, token_out=False, rows_reversed=False):
                self.n, self.q, self.k, self.v, self.bias = heads, q, k, v, bias
                self.sink_of, self.token_out, self.rows_reversed = sink_of, token_out, rows_reversed
                self.scores = sem(name + "_scores")
                self.max_ready = sem(name + "_max")
                self.exp_done = sem(name + "_exp")
                self.p_ready = sem(name + "_p")
                self.turned = sem(name + "_turned")
                self.pt_ready = sem(name + "_pt")
                self.out_ready = sem(name + "_out")
                self.hi = sem(name + "_hi")
                self.lo = sem(name + "_lo")
                self.start = sem(name + "_start")

            def pe_scores(self, pe, g):
                if g == 0:
                    pe.wait_ge(self.start, 2)
                if g >= 2:
                    pe.wait_ge(self.exp_done, g - 1)
                for tb in range(TB):
                    m = pe.matmul(PS[:, g % 2, tb * S:(tb + 1) * S], self.q(g, tb), self.k(g), start=True, stop=True)
                m.then_inc(self.scores, 1)

            def pe_turn(self, pe, g):
                pe.wait_ge(self.p_ready, g + 1)
                if g >= 2:
                    pe.wait_ge(self.pt_ready, g - 1)
                for kb in range(2):
                    for tb in range(TB):
                        m = pe.transpose(PS[:, 2 + g % 2, kb * S + tb * P:kb * S + (tb + 1) * P],
                                         p_sb[:, g % 2, tb * S + kb * P:tb * S + (kb + 1) * P], ident)
                m.then_inc(self.turned, 1)

            def pe_values(self, pe, g):
                pe.wait_ge(self.pt_ready, g + 1)
                if self.token_out:
                    for tb in range(TB):
                        for kb in range(tb + 1):
                            m = pe.matmul(PS[:, 4 + tb, g * HD:(g + 1) * HD], pt_sb[:, g % 2, kb, tb * P:(tb + 1) * P],
                                          self.v(g, kb), start=kb == 0, stop=kb == tb)
                else:
                    if g % 2 == 0 and g >= 4:
                        pe.wait_ge(self.lo, g // 2 - 1)
                    o = PS[(g % 2) * HD:(g % 2) * HD + HD, 4 + (g // 2) % 2, 0:S]
                    for kb in range(2):
                        m = pe.matmul(o, self.v(g, kb), pt_sb[:, g % 2, kb, :], start=kb == 0, stop=kb == 1)
                m.then_inc(self.out_ready, 1)

            def pe(self, pe):
                for s in range(self.n + 3):
                    if s < self.n:
                        self.pe_scores(pe, s)
                    if 2 <= s <= self.n + 1:
                        self.pe_turn(pe, s - 2)
                    if s >= 3:
                        self.pe_values(pe, s - 3)

            def dve_max(self, dve, g):
                dve.wait_ge(self.scores, g + 1)
                b = self.bias(g)
                if b is None:
                    dlink(dve, dve.tensor_reduce(mx[:, g, :], PS[:, g % 2, :].rearrange("p (t k) -> p t k", t=TB),
                                                 AX_X, ALU.max))
                    dve.tensor_scalar(negm[:, g, :], mx[:, g, :], -SCALE, None, ALU.mult).then_inc(self.max_ready, 1)
                    return
                for tb in range(TB):
                    o, i, bb = s_sb[:, g % 2, tb * S:(tb + 1) * S], PS[:, g % 2, tb * S:(tb + 1) * S], b[:, tb, :]
                    if self.rows_reversed:
                        bb = bass.AP(tensor=bb.tensor, offset=bb.offset + GRID_W - 1,
                                     ap=[list(bb.ap[0]), [GRID_W, 4], [-1, GRID_W]])
                        o, i = (z.rearrange("p (a k) -> p a k", k=GRID_W) for z in (o, i))
                    m = dve.tensor_tensor_reduce(o, i, bb, SCALE, -3e38, ALU.add, ALU.max, mx[:, g, tb:tb + 1])
                dlink(dve, m)
                if self.sink_of is not None and self.sink_of(g) is not None:
                    s = self.sink_of(g)
                    dve.tensor_scalar(negm[:, g, :], mx[:, g, :], s, -1.0, ALU.max, ALU.mult).then_inc(self.max_ready, 1)
                else:
                    dve.tensor_scalar(negm[:, g, :], mx[:, g, :], -1.0, None, ALU.mult).then_inc(self.max_ready, 1)

            def act_exp(self, act, g):
                act.wait_ge(self.max_ready, g + 1)
                if g >= 2:
                    act.wait_ge(self.turned, g - 1)
                raw_scores = self.bias(g) is None
                if self.sink_of is not None and self.sink_of(g) is not None:
                    act.activation(esink[:, g % 8, :], negm[:, g, :], ACT.Exp, bias=self.sink_of(g))
                for tb in range(TB):
                    src = PS[:, g % 2, tb * S:(tb + 1) * S] if raw_scores else s_sb[:, g % 2, tb * S:(tb + 1) * S]
                    m = act.activation(p_sb[:, g % 2, tb * S:(tb + 1) * S], src, ACT.Exp, bias=negm[:, g, tb:tb + 1],
                                       scale=SCALE if raw_scores else 1.0, accum_out=rsum[:, g, tb:tb + 1])
                m.then_inc(self.exp_done, 1)

            def dve_scale(self, dve, g):
                dve.wait_ge(self.exp_done, g + 1)
                if self.sink_of is not None and self.sink_of(g) is not None:
                    dlink(dve, dve.tensor_tensor(rsum[:, g, :], rsum[:, g, :], esink[:, g % 8, :], ALU.add))
                if self.token_out:
                    dve.reciprocal(rinv[:, g, :], rsum[:, g, :]).then_inc(self.p_ready, 1)
                    return
                dlink(dve, dve.reciprocal(rinv[:, g, :], rsum[:, g, :]))
                for tb in range(TB):
                    p = p_sb[:, g % 2, tb * S:(tb + 1) * S]
                    m = dve.tensor_scalar(p, p, rinv[:, g, tb:tb + 1], None, ALU.mult)
                m.then_inc(self.p_ready, 1)

            def act_turned(self, act, g):
                act.wait_ge(self.turned, g + 1)
                if g >= 2:
                    act.wait_ge(self.out_ready, g - 1)
                act.activation(pt_sb[:, g % 2, :, :], PS[:, 2 + g % 2, :].rearrange("p (k q) -> p k q", k=2),
                               ACT.Copy).then_inc(self.pt_ready, 1)

            def act(self, act):
                for s in range(self.n + 4):
                    if s < self.n:
                        self.act_exp(act, s)
                    if 2 <= s <= self.n + 1:
                        self.act_turned(act, s - 2)
                    if not self.token_out and s >= 5 and s % 2 == 1:
                        pair = (s - 5) // 2
                        act.wait_ge(self.out_ready, 2 * pair + 2)
                        act.activation(h_hi[:, pair, :], PS[:, 4 + pair % 2, 0:S], ACT.Copy).then_inc(self.hi, 1)

            def dve(self, dve):
                for s in range(self.n + 4):
                    if s < self.n:
                        self.dve_max(dve, s)
                    if 1 <= s <= self.n:
                        self.dve_scale(dve, s - 1)
                    if not self.token_out and s >= 5 and s % 2 == 1:
                        pair = (s - 5) // 2
                        dve.wait_ge(self.hi, pair + 1)
                        dve.tensor_tensor(h_lo[:, pair, :], PS[:, 4 + pair % 2, 0:S], h_hi[:, pair, :].bitcast(F32),
                                          ALU.subtract).then_inc(self.lo, 1)

            def ready(self, pe, k):
                pe.wait_ge(self.lo, k + 1)

        class EvenIn:
            def __init__(self, norm, att):
                self.u0, self.norm, self.att = first_unit["even_in"], norm, att
                self.pj_act = sem("even_pj_act")
                self.pj_dve = sem("even_pj_dve")
                self.rope = [sem("even_rope_a"), sem("even_rope_b")]
                self.turned = sem("even_turned")
                self.const = sem("even_const")

            def sp(self, sp, w):
                for c in range(3):
                    for half in range(2):
                        load_unit(sp, self.u0 + 2 * c + half, tok_src(w, half, c * 512), tok_view)

            def pe(self, pe):
                for c in range(3):
                    if c == 2:
                        pe.wait_ge(self.pj_act, 1)
                        pe.wait_ge(self.pj_dve, 1)
                    for half in range(2):
                        tok_unit(pe, self.u0 + 2 * c + half, half, (2 * (c % 2), 2 * (c % 2) + 1),
                                 ready=self.norm.ready if c == 0 else None)
                for br in range(2):
                    pe.wait_ge(self.rope[br], TB)
                    for slot in range(5):
                        bank = ((4, 5, 6), (7, 2, 3))[br][slot // 2]
                        for tb in range(TB):
                            m = pe.transpose(PS[:, bank, (slot % 2) * S + tb * P:(slot % 2) * S + (tb + 1) * P],
                                             R[:, tb, br * 640 + slot * P:br * 640 + (slot + 1) * P], ident)
                        if slot % 2 or slot == 4:
                            m.then_inc(self.turned, 1)

            def evac(self, eng, n):
                br, j = divmod(n, 3)
                bank = ((4, 5, 6), (7, 2, 3))[br][j]
                w = 2 if j < 2 else 1
                src = PS[:, bank, 0:w * S].rearrange("p (a s) -> p a s", a=w)
                dst = QKT[:, 5 * br + 2 * j:5 * br + 2 * j + w, :]
                eng.wait_ge(self.turned, n + 1)
                return dst, src

            def act(self, act):
                for c in range(3):
                    for half in range(2):
                        split_hi(act, self.u0 + 2 * c + half + LOOKAHEAD)
                    act.wait_ge(w_released, self.u0 + 2 * c + 2)
                    act.activation(PJ[:, 0, c * 512:(c + 1) * 512], PS[:, 2 * (c % 2), :], ACT.Copy)\
                       .then_inc(self.pj_act, 1)
                for n in (0, 2, 3, 5):
                    dst, src = self.evac(act, n)
                    m = act.activation(dst, src, ACT.Copy)
                m.then_inc(self.att.start, 1)

            def rotate(self, eng, link, br, tb):
                x0 = 768 * br
                if tb:
                    eng.wait_ge(self.rope[br], tb)
                x = PJ[:, tb, x0:x0 + 640]
                t1, t2 = rope_t1[:, br, :], rope_t2[:, br, :]
                C, Sn = rope_tab(2 * br, tb), rope_tab(2 * br + 1, tb)
                eng.tensor_tensor(t1.rearrange("p (h d) -> p h d", d=HD), x.rearrange("p (h d) -> p h d", d=HD),
                                  C.unsqueeze(1).to_broadcast([P, 10, HD]), ALU.mult)
                w = 16 if br == 0 else 32
                groups = HD // (2 * w)
                for half in range(2):
                    o = t2.rearrange("p (h g a w) -> p h g a w", g=groups, a=2, w=w)[:, :, :, half, :]
                    i = x.rearrange("p (h g a w) -> p h g a w", g=groups, a=2, w=w)[:, :, :, 1 - half, :]
                    s = Sn.rearrange("p (g a w) -> p g a w", a=2, w=w)[:, :, half, :].unsqueeze(1)\
                        .to_broadcast([P, 10, groups, w])
                    m = eng.tensor_tensor(o, i, s, ALU.mult)
                link(eng, m)
                r = R[:, tb, br * 640:(br + 1) * 640]
                qi = "p (b s d) -> p b s d"
                eng.tensor_tensor(r[:, 0:512].rearrange("p (s b d) -> p b s d", b=2, d=HD),
                                  t1[:, 0:512].rearrange(qi, b=2, d=HD), t2[:, 0:512].rearrange(qi, b=2, d=HD), ALU.add)
                eng.tensor_tensor(r[:, 512:640], t1[:, 512:640], t2[:, 512:640], ALU.add).then_inc(self.rope[br], 1)

            def dve(self, dve):
                for c in range(3):
                    for half in range(2):
                        split_lo(dve, self.u0 + 2 * c + half + LOOKAHEAD)
                    dve.wait_ge(w_released, self.u0 + 2 * c + 2)
                    dve.tensor_copy(PJ[:, 1, c * 512:(c + 1) * 512], PS[:, 2 * (c % 2) + 1, :]).then_inc(self.pj_dve, 1)
                dve.wait_ge(self.pj_act, 2)
                dve.wait_ge(self.pj_dve, 3)
                dve.wait_ge(self.const, 32)
                xa = PJ[:, :, 0:640]
                sq = R[:, :, 0:640]
                dlink(dve, dve.tensor_tensor(sq, xa, xa, ALU.mult))
                for tb in range(TB):
                    m = dve.tensor_reduce(ss[:, tb * 10:(tb + 1) * 10], sq[:, tb, :].rearrange("p (h d) -> p h d", d=HD),
                                          AX_X, ALU.add)
                dlink(dve, m)
                dlink(dve, dve.tensor_scalar(ss[:, 0:20], ss[:, 0:20], 1.0 / HD, EPS_RMS, ALU.mult, ALU.add))
                rsqrt(dve, ss[:, 0:20], 20)
                for tb in range(TB):
                    x = PJ[:, tb, 0:640].rearrange("p (h d) -> p h d", d=HD)
                    dlink(dve, dve.tensor_tensor(x, x, ss[:, tb * 10:(tb + 1) * 10].unsqueeze(2).to_broadcast([P, 10, HD]),
                                                 ALU.mult))
                    dlink(dve, dve.tensor_tensor(PJ[:, tb, 0:640], PJ[:, tb, 0:640], qk_gain, ALU.mult))
                    self.rotate(dve, dlink, 0, tb)
                for n in (1, 4):
                    dst, src = self.evac(dve, n)
                    m = dve.tensor_copy(dst, src)
                m.then_inc(self.att.start, 1)

            def pool(self, pool):
                pool.wait_ge(self.pj_act, 3)
                pool.wait_ge(self.pj_dve, 3)
                for tb in range(TB):
                    self.rotate(pool, plink, 1, tb)

        class OddIn:
            def __init__(self, norm, att):
                self.u0, self.norm, self.att = first_unit["odd_in"], norm, att
                self.act_out = sem("odd_act_out")
                self.dve_out = sem("odd_dve_out")

            def sp(self, sp, w):
                for j in range(8):
                    load_unit(sp, self.u0 + j, feat_src(w, j * 256), feat_view)
                for c in range(2):
                    for half in range(2):
                        load_unit(sp, self.u0 + 8 + 2 * c + half, tok_src(w, half, 2048 + c * 512), tok_view)

            def pe(self, pe):
                for j in range(8):
                    if j >= 4:
                        pe.wait_ge(self.dve_out if j % 2 else self.act_out, (j - 4) // 2 + 1)
                    feat_unit(pe, self.u0 + j, j % 4, ready=self.norm.ready if j == 0 else None)
                for c in range(2):
                    for half in range(2):
                        tok_unit(pe, self.u0 + 8 + 2 * c + half, half, (4 + 2 * c, 5 + 2 * c))

            def take(self, eng, mine, split, copy, out):
                for j in range(8):
                    split(eng, self.u0 + j + LOOKAHEAD)
                    if j % 2 == mine:
                        eng.wait_ge(w_released, self.u0 + j + 1)
                        m = copy(QKT[:, 2 * j:2 * j + 2, :], PS[:, j % 4, :].rearrange("p (a s) -> p a s", a=2))
                        m.then_inc(out, 1)
                for c in range(2):
                    for half in range(2):
                        split(eng, self.u0 + 8 + 2 * c + half + LOOKAHEAD)
                    eng.wait_ge(w_released, self.u0 + 8 + 2 * c + 2)
                    m = copy(V[:, mine, c * 512:(c + 1) * 512], PS[:, 4 + 2 * c + mine, :])
                m.then_inc(self.att.start, 1)

            def act(self, act):
                self.take(act, 0, split_hi, lambda o, i: act.activation(o, i, ACT.Copy), self.act_out)

            def dve(self, dve):
                self.take(dve, 1, split_lo, lambda o, i: dve.tensor_copy(o, i), self.dve_out)

        def layer_norm(dve, g, b, done):
            for tb in range(TB):
                for half in range(2):
                    m = dve.bn_stats(bn[:, tb, half, :], X[:, tb, half * 512:(half + 1) * 512])
            dlink(dve, m)
            for tb in range(TB):
                m = dve.bn_aggr(mv[:, tb, :], bn[:, tb, :, :].rearrange("p a b -> p (a b)"))
            dlink(dve, m)
            dlink(dve, dve.tensor_scalar(ss[:, 0:2], mv[:, :, 1], EPS_LN, None, ALU.add))
            rsqrt(dve, ss[:, 0:2], 2)
            for tb, half in QUARTERS:
                f = slice(half * 512, (half + 1) * 512)
                x = X[:, tb, f]
                dlink(dve, dve.scalar_tensor_tensor(x, x, mv[:, tb, 0:1], g[:, f], ALU.subtract, ALU.mult))
                dve.scalar_tensor_tensor(x, x, ss[:, tb:tb + 1], b[:, f], ALU.mult, ALU.add).then_inc(done, 1)

        QA, KA, VA, FA = 0, 512, 1024, 1536
        QR, FR, IR, GR = 1544, 2056, 2568, 3080

        class RecIn:
            PLAN = [("f", QA, 0), ("f", KA, 4), ("t", VA, 0), ("f", QR, 8), ("t", GR, 1), ("f", FR, 12), ("t", IR, 2)]

            def __init__(self, norm, att):
                self.u0, self.norm, self.att = first_unit["rec_in"], norm, att
                self.wf_in = sem("rec_wf_in")
                self.t_ready = sem("rec_t_ready")
                self.f_done = sem("rec_f_done")
                self.f_chain = sem("rec_f_chain")
                self.c_ready = sem("rec_c_ready")
                self.c_turned = sem("rec_c_turned")
                self.cq_ready = sem("rec_cq_ready")
                self.c_wide = sem("rec_c_wide")
                self.bias_done = sem("rec_bias_done")
                self.sel_free = sem("rec_sel_free")
                self.act_out = sem("rec_act_out")
                self.dve_out = sem("rec_dve_out")

            def sp(self, sp, w):
                n = self.u0
                for kind, col, _ in self.PLAN:
                    for j in range(2):
                        if kind == "f":
                            load_unit(sp, n, feat_src(w, col + 256 * j), feat_view)
                        else:
                            load_unit(sp, n, tok_src(w, j, col), tok_view)
                        n += 1

            def banks(self, group):
                return (0, 1) if group % 2 == 0 else (2, 3)

            def pe(self, pe):
                n = self.u0
                for group, (kind, _, _) in enumerate(self.PLAN):
                    b = self.banks(group)
                    if group >= 2:
                        pe.wait_ge(self.act_out, group - 1)
                        pe.wait_ge(self.dve_out, group - 1)
                    for j in range(2):
                        if kind == "f":
                            feat_unit(pe, n, b[j], ready=self.norm.ready if n == self.u0 else None)
                        else:
                            tok_unit(pe, n, j, b)
                        n += 1
                    if group == 0:
                        pe.wait_ge(self.wf_in, 32)
                        pe.wait_ge(self.t_ready, 1)
                        for k in range(KC):
                            m = pe.matmul(PS[0:8, 6, 0:S], wf[:, k, :], T[:, k, :], start=k == 0, stop=k == KC - 1)
                        m.then_inc(self.f_done, 1)
                    if group == 1:
                        pe.wait_ge(self.c_ready, 1)
                        for tb in range(TB):
                            m = pe.transpose(PS[:, 6, tb * 8:(tb + 1) * 8], f_c[:, tb * P:(tb + 1) * P],
                                             consts[0:8, C_IDENT:C_IDENT + 8])
                        m.then_inc(self.c_turned, 1)
                    if group == 2:
                        for pair in range(4):
                            bank = 4 + pair % 2
                            if pair >= 2:
                                pe.wait_ge(self.bias_done, pair - 1)
                            for a in range(2):
                                m = pe.matmul(PS[:, bank, a * S:(a + 1) * S], sel[:, 2 * pair + a, :], f_m,
                                              start=True, stop=True)
                            m.then_inc(self.c_wide, 1)

            def take(self, eng, mine, split, copy, out, extra):
                n = self.u0
                for group, (kind, _, dst) in enumerate(self.PLAN):
                    b = self.banks(group)[mine]
                    for j in range(2):
                        split(eng, n + LOOKAHEAD)
                        n += 1
                        if kind == "f" and j == mine:
                            eng.wait_ge(w_released, n)
                            copy(QKT[:, dst + 2 * j:dst + 2 * j + 2, :],
                                 PS[:, b, :].rearrange("p (a s) -> p a s", a=2), group).then_inc(out, 1)
                    if kind == "t":
                        eng.wait_ge(w_released, n)
                        o = (V[:, mine, 0:512], hg_gate[:, mine, :], V[:, mine, 512:1024])[dst]
                        copy(o, PS[:, b, :], group).then_inc(out, 1)
                    extra(group)

            def act(self, act):
                def extra(group):
                    if group == 0:
                        act.wait_ge(self.f_done, 1)
                        alink(act, act.activation(f_z, PS[0:8, 6, 0:S], ACT.Identity, bias=fbias[:, 0:1]))
                        alink(act, act.activation(f_a, f_z, ACT.Abs))
                        alink(act, act.activation(f_a, f_a, ACT.Exp, scale=-1.0))
                        act.activation(f_a, f_a, ACT.Ln, bias=1.0).then_inc(self.f_chain, 1)
                    if group == 6:
                        act.wait_ge(self.dve_out, 6)
                        act.wait_ge(self.act_out, 6)
                        alink(act, act.activation(hg_d[:, :, :], hg_f, ACT.Abs))
                        alink(act, act.activation(hg_d[:, :, :], hg_d[:, :, :], ACT.Exp, scale=-1.0))
                        act.activation(hg_d[:, :, :], hg_d[:, :, :], ACT.Ln, bias=1.0).then_inc(self.att.start, 1)

                def copy(o, i, group):
                    return act.activation(o, i, ACT.Copy)

                self.take(act, 0, split_hi, copy, self.act_out, extra)

            def dve(self, dve):
                def extra(group):
                    if group == 0:
                        dve.wait_ge(self.f_chain, 1)
                        dlink(dve, dve.tensor_scalar(f_m, f_z, 0.0, None, ALU.min))
                        dlink(dve, dve.tensor_tensor(f_m, f_m, f_a, ALU.subtract))
                        for c in range(4):
                            dlink(dve, dve.tensor_tensor_scan(f_c[:, c * 64:(c + 1) * 64], f_m[:, c * 64:(c + 1) * 64],
                                                              zeros[0:8, :], 0.0 if c == 0 else f_c[:, c * 64 - 1:c * 64],
                                                              ALU.add, ALU.add))
                        dlink(dve, dve.tensor_scalar(f_m, f_c, -8.0, None, ALU.mult))
                        dve.tensor_scalar(f_c, f_c, 8.0, None, ALU.mult).then_inc(self.c_ready, 1)
                    if group == 1:
                        dve.wait_ge(self.c_turned, 1)
                        dlink(dve, dve.tensor_copy(cq[:, :, :], PS[:, 6, 0:16].rearrange("p (t h) -> p t h", t=TB)))
                    if group == 2:
                        for pair in range(4):
                            dve.wait_ge(self.c_wide, pair + 1)
                            for a in range(2):
                                h = 2 * pair + a
                                for tb in range(TB):
                                    m = dve.scalar_tensor_tensor(
                                        fox_bias[:, h, tb, :], PS[:, 4 + pair % 2, a * S:(a + 1) * S],
                                        cq[:, tb, h:h + 1], causal_mask[:, tb, :], ALU.add, ALU.add)
                            m.then_inc(self.bias_done, 1)

                def copy(o, i, group):
                    return dve.tensor_copy(o, i)

                self.take(dve, 1, split_lo, copy, self.dve_out, extra)
                dve.wait_ge(self.bias_done, 4)
                dve.tensor_copy(cq[:, :, :], cq[:, :, :]).then_inc(self.att.start, 1)

        class Recurrence:

            def __init__(self, att):
                self.att = att
                self.k_arg = sem("hg_k_arg")
                self.k_ready = sem("hg_k_ready")
                self.b_ready = sem("hg_b_ready")
                self.d_ready = sem("hg_d_ready")
                self.e_ready = sem("hg_e_ready")
                self.kq_ready = sem("hg_kq_ready")
                self.st_zero = sem("hg_st_zero")
                self.mm_done = sem("hg_mm_done")
                self.read_done = sem("hg_read_done")
                self.o_done = sem("hg_o_done")
                self.q_ready = sem("hg_q_ready")
                self.gate_ready = sem("hg_gate_ready")

            def pool(self, pool):
                pool.wait_ge(self.att.out_ready, 8)
                pool.memset(hg_st[:, :, :], 0.0).then_inc(self.st_zero, 1)
                pool.wait_ge(self.b_ready, 1)
                for n, m in enumerate((64,) + LEVELS):
                    b = hg_b.rearrange("p h t -> p (h t)")
                    d = hg_d.rearrange("p h t -> p (h t)")
                    if n == 0:
                        w = 64
                        ref = b.rearrange("p (c w) -> p c w", w=w)[:, :, w - 1:w]
                    else:
                        w = 2 * m
                        ref = b.rearrange("p (c w) -> p c w", w=w)[:, :, m - 1:m]
                        pool.wait_ge(self.e_ready, n)
                    pool.tensor_tensor(d.rearrange("p (c w) -> p c w", w=w), b.rearrange("p (c w) -> p c w", w=w),
                                       ref.to_broadcast([P, 1024 // w, w]), ALU.subtract).then_inc(self.d_ready, 1)

            def act(self, act):
                act.wait_ge(self.k_arg, 1)
                act.activation(hg_k, hg_k, ACT.Exp).then_inc(self.k_ready, 1)
                act.wait_ge(self.d_ready, 1)
                act.wait_ge(self.st_zero, 1)
                act.activation(hg_f, hg_b, ACT.Exp)
                act.activation(hg_e, hg_d, ACT.Exp, scale=-1.0).then_inc(self.e_ready, 1)
                for n, m in enumerate(LEVELS):
                    act.wait_ge(self.d_ready, n + 2)
                    act.wait_ge(self.kq_ready, n + 2 if n else 1)
                    d = hg_d.rearrange("p h t -> p (h t)").rearrange("p (c w) -> p c w", w=2 * m)
                    e = hg_e.rearrange("p h t -> p (h t)").rearrange("p (c w) -> p c w", w=2 * m)
                    act.activation(e[:, :, 0:m], d[:, :, 0:m], ACT.Exp, scale=-1.0)
                    act.activation(e[:, :, m:2 * m], d[:, :, m:2 * m], ACT.Exp).then_inc(self.e_ready, 1)

            def act_silu(self, act):
                act.activation(hg_q, hg_q, ACT.Silu).then_inc(self.q_ready, 1)
                act.activation(hg_gate, hg_gate, ACT.Silu).then_inc(self.gate_ready, 1)

            def pe(self, pe):
                pe.wait_ge(self.k_ready, 1)
                pe.wait_ge(self.q_ready, 1)
                for tb in range(TB):
                    for h in range(4):
                        m = pe.matmul(PS[:, 6 + tb, h * P:(h + 1) * P], hg_k[:, h, tb * P:(tb + 1) * P],
                                      hg_q[:, h, tb * P:(tb + 1) * P], start=True, stop=True)
                m.then_inc(self.mm_done, 1)
                pe.wait_ge(self.kq_ready, 1)
                for h in range(4):
                    for tb in range(TB):
                        m = pe.matmul(PS[:, 0, (2 * h + tb) * 64:(2 * h + tb + 1) * 64],
                                      hg_kh[:, h, tb * P:(tb + 1) * P], hg_qh[:, h, tb * P + 64:(tb + 1) * P],
                                      start=True, stop=True)
                m.then_inc(self.mm_done, 1)
                pe.wait_ge(self.kq_ready, 2)
                for h in range(4):
                    m = pe.matmul(PS[:, 1, h * P:(h + 1) * P], hg_kh[:, h, 0:P], hg_qh[:, h, P:S], start=True, stop=True)
                m.then_inc(self.mm_done, 1)
                for n, mm in enumerate(LEVELS):
                    pe.wait_ge(self.kq_ready, n + 3)
                    bank = n % 2
                    pe.wait_ge(self.read_done, n + 2)
                    for h in range(4):
                        for tb in range(TB):
                            q = hg_qh[:, h, tb * P:(tb + 1) * P].rearrange("p (c w) -> p c w", w=2 * mm)[:, :, mm:2 * mm]
                            o = PS[:, bank, (2 * h + tb) * 64:(2 * h + tb + 1) * 64].rearrange("p (c w) -> p c w", w=mm)
                            m = pe.matmul(o, hg_kh[:, h, tb * P:(tb + 1) * P], q, start=True, stop=True)
                    m.then_inc(self.mm_done, 1)
                pe.wait_ge(self.read_done, 3 + len(LEVELS))
                for tb in range(TB):
                    for h in range(4):
                        o = PS[:, 2 + tb, h * P:(h + 1) * P]
                        m = pe.matmul(o, hg_st[:, 2 * h + tb, :], V[:, tb, 512 + h * P:512 + (h + 1) * P],
                                      start=True, stop=tb == 0)
                        if tb:
                            m = pe.matmul(o, hg_s2[:, h, :], V[:, 0, 512 + h * P:512 + (h + 1) * P],
                                          start=False, stop=True)
                m.then_inc(self.o_done, 1)

            def dve_gates(self, dve):
                dve.wait_ge(self.att.start, 2)
                dve.tensor_scalar(hg_b, hg_f, 0.0, None, ALU.min)
                dlink(dve, dve.tensor_scalar(hg_k, hg_f, 0.0, -1.0, ALU.max, ALU.mult))
                dve.tensor_tensor(hg_k, hg_k, hg_d, ALU.subtract).then_inc(self.k_arg, 1)
                dlink(dve, dve.tensor_tensor(hg_b, hg_b, hg_d, ALU.subtract))
                b = hg_b.rearrange("p h t -> p (h t)")
                for c in range(16):
                    m = dve.tensor_tensor_scan(b[:, c * 64:(c + 1) * 64], b[:, c * 64:(c + 1) * 64], zeros, 0.0,
                                               ALU.add, ALU.add)
                m.then_inc(self.b_ready, 1)

            def dve(self, dve):
                dve.wait_ge(self.e_ready, 1)
                dve.wait_ge(self.k_ready, 1)
                dve.wait_ge(self.q_ready, 1)
                dve.tensor_tensor(hg_kh, hg_k, hg_e, ALU.mult)
                dve.tensor_tensor(hg_qh, hg_q, hg_f, ALU.mult).then_inc(self.kq_ready, 1)
                dve.wait_ge(self.mm_done, 1)
                eye = ident.unsqueeze(1).to_broadcast([P, 4, P]).bitcast(U32)
                st = hg_st.rearrange("p (h t) x -> p t h x", t=TB)
                dve.wait_ge(self.st_zero, 1)
                for tb in range(TB):
                    m = dve.copy_predicated(st[:, tb], eye, PS[:, 6 + tb, :].rearrange("p (h x) -> p h x", h=4))
                m.then_inc(self.read_done, 1)
                dve.wait_ge(self.mm_done, 2)
                dve.wait_ge(self.read_done, 1)
                dve.tensor_copy(hg_st[0:64, :, 64:128], PS[0:64, 0, :].rearrange("p (b x) -> p b x", b=8))\
                   .then_inc(self.read_done, 1)
                dve.wait_ge(self.kq_ready, 1)
                dve.tensor_tensor(hg_kh[:, :, 0:64], hg_kh[:, :, 0:64], hg_f[:, :, 127:128].to_broadcast([P, 4, 64]),
                                  ALU.mult)
                dve.tensor_tensor(hg_qh[:, :, 192:256], hg_qh[:, :, 192:256],
                                  hg_f[:, :, 191:192].to_broadcast([P, 4, 64]), ALU.mult).then_inc(self.kq_ready, 1)
                dve.wait_ge(self.mm_done, 3)
                dve.tensor_copy(hg_s2, PS[:, 1, :].rearrange("p (h x) -> p h x", h=4)).then_inc(self.read_done, 1)

                def operands(n):
                    m = LEVELS[n]

                    def cut(x):
                        return x.rearrange("p h t -> p (h t)").rearrange("p (c w) -> p c w", w=2 * m)
                    dve.wait_ge(self.e_ready, n + 2)
                    dve.wait_ge(self.kq_ready, n + 2)
                    dve.tensor_tensor(cut(hg_kh)[:, :, 0:m], cut(hg_k)[:, :, 0:m], cut(hg_e)[:, :, 0:m], ALU.mult)
                    dve.tensor_tensor(cut(hg_qh)[:, :, m:2 * m], cut(hg_q)[:, :, m:2 * m], cut(hg_e)[:, :, m:2 * m],
                                      ALU.mult).then_inc(self.kq_ready, 1)

                for n, m in enumerate(LEVELS):
                    operands(n)
                    dve.wait_ge(self.mm_done, n + 4)
                    dve.wait_ge(self.read_done, n + 3)
                    mask = consts[:, C_LEVEL + 64 * n:C_LEVEL + 64 * (n + 1)].bitcast(U32)\
                        .rearrange("p (c w) -> p c w", w=m).unsqueeze(1).to_broadcast([P, 8, 64 // m, m])
                    o = hg_st.rearrange("p b (c w) -> p b c w", w=2 * m)[:, :, :, m:2 * m]
                    src = PS[:, n % 2, :].rearrange("p (b c w) -> p b c w", b=8, w=m)
                    dve.copy_predicated(o, mask, src).then_inc(self.read_done, 1)

        class RecOut:

            def __init__(self, att, rec, norm):
                self.att, self.rec, self.norm = att, rec, norm
                self.fox_read = sem("mix_fox_read")
                self.gained = sem("mix_gained")

            def dve_fox(self, dve):
                dve.wait_ge(self.att.out_ready, 8)
                for tb in range(TB):
                    dve.tensor_tensor(XN[:, tb, 0:512].rearrange("p (h d) -> p h d", d=HD),
                                      PS[:, 4 + tb, :].rearrange("p (h d) -> p h d", d=HD),
                                      rinv[:, 0:8, tb:tb + 1].to_broadcast([P, 8, HD]), ALU.mult)\
                       .then_inc(self.fox_read, 1)

            def pool(self, pool):
                pool.wait_ge(gain_in, 16 * 7 + 16)
                pool.wait_ge(self.rec.gate_ready, 1)
                for tb in range(TB):
                    m = pool.tensor_tensor(hg_gate[:, tb, :], hg_gate[:, tb, :], rowvec[:, 1, 512:1024], ALU.mult)
                m.then_inc(self.gained, 1)

            def dve(self, dve):
                dve.wait_ge(self.rec.o_done, 1)
                dve.wait_ge(self.fox_read, 2)
                for tb in range(TB):
                    m = dve.tensor_copy(XN[:, tb, 512:1024], PS[:, 2 + tb, :])
                dlink(dve, m)
                sq = arena[:, 4096:6144].rearrange("p (t n) -> p t n", t=TB)
                dlink(dve, dve.tensor_tensor(sq, XN[:, :, :], XN[:, :, :], ALU.mult))
                for tb in range(TB):
                    dve.tensor_reduce(ss[:, tb * 12:tb * 12 + 8], sq[:, tb, 0:512].rearrange("p (h d) -> p h d", d=HD),
                                      AX_X, ALU.add)
                    m = dve.tensor_reduce(ss[:, tb * 12 + 8:tb * 12 + 12],
                                          sq[:, tb, 512:1024].rearrange("p (h d) -> p h d", d=P), AX_X, ALU.add)
                dlink(dve, m)
                s3 = ss[:, 0:24].rearrange("p (t h) -> p t h", t=TB)
                dve.tensor_scalar(s3[:, :, 0:8], s3[:, :, 0:8], 1.0 / HD, EPS_RMS, ALU.mult, ALU.add)
                dlink(dve, dve.tensor_scalar(s3[:, :, 8:12], s3[:, :, 8:12], 1.0 / P, EPS_RMS, ALU.mult, ALU.add))
                rsqrt(dve, ss[:, 0:24], 24)
                dve.wait_ge(self.gained, 1)
                for tb in range(TB):
                    y = XN[:, tb, 0:512]
                    dlink(dve, dve.tensor_tensor(y.rearrange("p (h d) -> p h d", d=HD),
                                                 y.rearrange("p (h d) -> p h d", d=HD),
                                                 ss[:, tb * 12:tb * 12 + 8].unsqueeze(2).to_broadcast([P, 8, HD]),
                                                 ALU.mult))
                    dve.tensor_tensor(y, y, rowvec[:, 1, 0:512], ALU.mult).then_inc(self.norm.normed, 1)
                for tb in range(TB):
                    x = XN[:, tb, 512:1024]
                    dlink(dve, dve.tensor_tensor(x.rearrange("p (h d) -> p h d", d=P),
                                                 x.rearrange("p (h d) -> p h d", d=P),
                                                 ss[:, tb * 12 + 8:tb * 12 + 12].unsqueeze(2).to_broadcast([P, 4, P]),
                                                 ALU.mult))
                    dve.tensor_tensor(x, x, hg_gate[:, tb, :], ALU.mult).then_inc(self.norm.normed, 1)

        ffn_order = [(0, 0), (0, 1), (1, 0), (1, 1)]
        n_ffn1_0, n_mix_0, n_ffn2_0, n_ffn1_1, n_mix_1, n_ffn2_1 = (Norm(at) for at in range(6))
        n_emb, n_gated, n_conv = Norm(6, X), Norm(7, XN), Norm(8, X)
        for n in (n_ffn1_0, n_mix_0, n_ffn1_1, n_mix_1):
            n.order = ffn_order
        for n in (n_ffn2_0, n_ffn2_1):
            n.order = QUARTERS
        final_x = sem("final_x")
        mixed_x = sem("mixed_x")
        conv_x = sem("conv_x")
        out_x = sem("out_x")

        def even_q(g, tb):
            br, h = divmod(g, 8)
            base = (h // 4) * HD
            return QKT[base:base + HD, 5 * br + h % 4, tb * P:(tb + 1) * P]

        def even_k(g):
            br, h = divmod(g, 8)
            base = (h // 4) * HD
            return QKT[base:base + HD, 5 * br + 4, :]

        def even_v(g, kb):
            br, h = divmod(g, 8)
            at = 768 * br + 640 + (h // 4) * HD
            return PJ[:, kb, at:at + HD]

        att_even = Attention("att_even", 16, even_q, even_k, even_v, lambda g: None if g < 8 else win_mask,
                             lambda g: None if g < 8 else sink[:, g - 8:g - 7])
        att_odd = Attention("att_odd", 16,
                            lambda g, tb: QKT[(g % 2) * HD:(g % 2) * HD + HD, g // 2, tb * P:(tb + 1) * P],
                            lambda g: QKT[(g % 2) * HD:(g % 2) * HD + HD, 8 + g // 2, :],
                            lambda g, kb: V[:, kb, g * HD:(g + 1) * HD], lambda g: bias[:, g], rows_reversed=True)
        att_fox = Attention("att_fox", 8,
                            lambda g, tb: QKT[(g % 2) * HD:(g % 2) * HD + HD, g // 2, tb * P:(tb + 1) * P],
                            lambda g: QKT[(g % 2) * HD:(g % 2) * HD + HD, 4 + g // 2, :],
                            lambda g, kb: V[:, kb, g * HD:(g + 1) * HD], lambda g: fox_bias[:, g], token_out=True)
        even_in = EvenIn(n_mix_0, att_even)
        odd_in = OddIn(n_mix_1, att_odd)
        rec_in = RecIn(n_emb, att_fox)
        rec = Recurrence(att_fox)
        rec_out = RecOut(att_fox, rec, n_gated)
        ffn1_0 = Ffn(0, "ffn1_0", io["ffn1_w_gate"][0], io["ffn1_w_up"][0], io["ffn1_w_down"][0], n_ffn1_0, n_mix_0.x_ready)
        even_out = OutProj("even_out", io["even_w_out"][0], att_even.ready, n_ffn2_0.x_ready, 0)
        ffn2_0 = Ffn(1, "ffn2_0", io["ffn2_w_gate"][0], io["ffn2_w_up"][0], io["ffn2_w_down"][0], n_ffn2_0, n_ffn1_1.x_ready)
        ffn1_1 = Ffn(2, "ffn1_1", io["ffn1_w_gate"][1], io["ffn1_w_up"][1], io["ffn1_w_down"][1], n_ffn1_1, n_mix_1.x_ready)
        odd_out = OutProj("odd_out", io["odd_w_out"][0], att_odd.ready, n_ffn2_1.x_ready, 1)
        ffn2_1 = Ffn(3, "ffn2_1", io["ffn2_w_gate"][1], io["ffn2_w_up"][1], io["ffn2_w_down"][1], n_ffn2_1, final_x)
        rec_proj = OutProj("rec_out", io["w_o_2"][0], n_gated.ready, mixed_x, 2, alpha=ALPHA, bank=4)
        w_up = io["w_up_2"][0]
        conv_ffn = Ffn(4, "conv_ffn", w_up[:, 0:FF], w_up[:, FF:2 * FF], io["w_down_2"][0], n_conv, conv_x, conv=True)

        x_in = sem("x_in")
        consts_in = sem("consts_in")
        ident_in = sem("ident_in")
        rows_in = sem("rows_in")
        rows_turned = sem("rows_turned")
        cols_ready = sem("cols_ready")
        sink_in = sem("sink_in")
        bias_in = sem("bias_in")
        bias_masked = sem("bias_masked")
        even_done = sem("even_done")
        vec_in = sem("vec_in")
        vec2_in = sem("vec2_in")
        vec3_in = sem("vec3_in")
        vec_used = sem("vec_used")
        out_stored = sem("out_stored")

        conv_rows = pt_sb[0:44, 0, :, :].rearrange("p a b -> p (a b)").rearrange("p (a n) -> p a n", a=4)

        block = ctx.enter_context(nc.Block())

        @block.sync
        def _(sp):
            ffn1_0.sp(sp)
            even_in.sp(sp, io["even_w_in"][0])
            even_out.sp(sp)
            ffn2_0.sp(sp)
            ffn1_1.sp(sp)
            odd_in.sp(sp, io["odd_w_qkv"][0])
            odd_out.sp(sp)
            ffn2_1.sp(sp)
            rec_in.sp(sp, io["w_in_2"][0])
            rec_proj.sp(sp)
            conv_ffn.sp(sp)
            for q, (tb, half) in enumerate(QUARTERS):
                sp.wait_ge(out_x, q + 1)
                f = slice(half * 512, (half + 1) * 512)
                sp.dma_start(out[0, tb * P:(tb + 1) * P, f], X[:, tb, f]).then_inc(out_stored, 16)
            sp.wait_ge(out_stored, 16 * 4)

        @block.gpsimd
        def _(pool):
            def gain(at, name, layer):
                if at >= 2:
                    pool.wait_ge(Norm.normed, 4 * (at - 1))
                pool.wait_ge(gain_in, 16 * at) if at else None
                pool.dma_start(rowvec[:, at % 2, :], io[name][layer].partition_broadcast(P)).then_inc(gain_in, 16)

            gain(0, "ffn1_norm", 0)
            pool.wait_ge(w_lo_ready, 4)
            gain(1, "mix_norm", 0)
            pool.dma_start(consts[:, P:], io["consts"][:, P:C_SEL]).then_inc(consts_in, 16)
            pool.dma_start(conv_rows[:, 0:3, :], io["conv_w_2"][0].rearrange("a (k n) -> k a n", n=P)).then_inc(rows_in, 16)
            pool.dma_start(conv_rows[:, 3, :], io["conv_b_2"][0].rearrange("(k n) -> k n", n=P)).then_inc(rows_in, 16)
            pool.dma_start(sink[:, :], io["b_sink"][0].partition_broadcast(P)).then_inc(sink_in, 16)
            pool.dma_start(fbias[:, :], io["fox_f_bias_2"][0].rearrange("(h a) -> h a", a=1)).then_inc(sink_in, 16)
            q = bass.AP(tensor=io["a_q_norm"].tensor, offset=0, ap=[[0, P], [0, 8], [1, HD]])
            k = bass.AP(tensor=io["a_k_norm"].tensor, offset=0, ap=[[0, P], [0, 2], [1, HD]])
            pool.dma_start(qk_gain[:, 0:512].rearrange("p (h d) -> p h d", d=HD), q).then_inc(even_in.const, 16)
            pool.dma_start(qk_gain[:, 512:640].rearrange("p (h d) -> p h d", d=HD), k).then_inc(even_in.const, 16)
            gain(2, "ffn2_norm", 0)
            pool.wait_ge(consts_in, 16)
            even_in.pool(pool)
            gain(3, "ffn1_norm", 1)
            pool.wait_ge(even_done, 1)
            table = io["c_rel_bias"].tensor
            for h in range(16):
                for r in range(4):
                    tb, base = divmod(r * GRID_W, P)
                    src = bass.AP(tensor=table, offset=h * REL_H * REL_W + (7 - r) * REL_W - 48,
                                  ap=[[1, GRID_W], [REL_W, 4], [1, GRID_W]])
                    pool.dma_start(bias[base:base + GRID_W, h, tb, :].rearrange("p (a k) -> p a k", a=4), src)\
                        .then_inc(bias_in, 16)
            pool.wait_ge(bias_in, 16 * 64)
            for h in range(16):
                for tb in range(TB):
                    plink(pool, pool.tensor_scalar(bias[:, h, tb, :], bias[:, h, tb, :], 8.0, None, ALU.mult))
                    pool.tensor_tensor(bias[:, h, tb, :], bias[:, h, tb, :], nb_mask, ALU.add).then_inc(bias_masked, 1)
            gain(4, "mix_norm", 1)
            gain(5, "ffn2_norm", 1)
            pool.wait_ge(Norm.normed, 4 * 6)
            pool.dma_start(rowvec[:, 0, :], io["final_norm"].partition_broadcast(P)).then_inc(vec_in, 16)
            pool.dma_start(rowvec[:, 1, :], io["ln_emb_g_2"].partition_broadcast(P)).then_inc(vec_in, 16)
            pool.wait_ge(att_odd.lo, 8)
            pool.dma_start(V[:, 0, :], io["ln_emb_b_2"].partition_broadcast(P)).then_inc(vec_in, 16)
            pool.wait_ge(n_emb.normed, 7 * 4)
            pool.dma_start(wf, io["w_in_2"][0, :, FA:FA + 8].rearrange("(k p) n -> p k n", p=P)).then_inc(rec_in.wf_in, 16)
            pool.dma_start(sel, io["consts"][0:8, C_SEL:C_N].rearrange("p (h q) -> p h q", h=8)).then_inc(rec_in.wf_in, 16)
            pool.dma_start(rowvec[:, 1, 0:512], io["fox_norm_g_2"][0].partition_broadcast(P)).then_inc(gain_in, 16)
            pool.dma_start(rowvec[:, 1, 512:1024], io["hgrn_norm_g_2"][0].partition_broadcast(P)).then_inc(gain_in, 16)
            pool.dma_start(rowvec[:, 0, :], io["ln_mix_g_2"][0].partition_broadcast(P)).then_inc(vec2_in, 16)
            pool.wait_ge(n_emb.lo, 7 * 4)
            pool.tensor_tensor(T[:, :, :], h_hi[:, :, :].bitcast(F32), h_lo[:, :, :].bitcast(F32), ALU.add)\
                .then_inc(rec_in.t_ready, 1)
            rec.pool(pool)
            rec_out.pool(pool)
            pool.wait_ge(n_gated.normed, 8 * 4)
            pool.dma_start(rowvec[:, 1, :], io["ln_mix_b_2"][0].partition_broadcast(P)).then_inc(vec2_in, 16)
            pool.wait_ge(n_conv.normed, 9 * 4)
            pool.dma_start(rowvec[:, 0, :], io["ln_ffn_g_2"][0].partition_broadcast(P)).then_inc(vec3_in, 16)
            pool.dma_start(rowvec[:, 1, :], io["ln_ffn_b_2"][0].partition_broadcast(P)).then_inc(vec3_in, 16)
            pool.wait_ge(vec3_in, 32)

        @block.scalar
        def _(act):
            act.dma_start(X[:, :, :], io["x"][0].rearrange("(t p) n -> p t n", p=P)).then_inc(x_in, 16)
            act.dma_start(ident, io["consts"][:, 0:P]).then_inc(ident_in, 16)
            act.wait_ge(x_in, 16)
            n_ffn1_0.act(act, first=True)
            ffn1_0.act(act)
            n_mix_0.act(act)
            even_in.act(act)
            act.wait_ge(sink_in, 32)
            att_even.act(act)
            even_out.act(act)
            n_ffn2_0.act(act)
            ffn2_0.act(act)
            n_ffn1_1.act(act)
            ffn1_1.act(act)
            n_mix_1.act(act)
            odd_in.act(act)
            att_odd.act(act)
            odd_out.act(act)
            n_ffn2_1.act(act)
            ffn2_1.act(act)
            n_emb.act(act)
            rec_in.act(act)
            rec.act_silu(act)
            att_fox.act(act)
            rec.act(act)
            n_gated.act(act)
            rec_proj.act(act)
            n_conv.act(act)
            conv_ffn.act(act)

        @block.vector
        def _(dve):
            dve.wait_ge(x_in, 16)
            n_ffn1_0.dve(dve, first=True)
            ffn1_0.dve(dve)
            dve.wait_ge(rows_turned, 1)
            dve.tensor_copy(convc[:, :, :], PS[:, 2, 0:176].rearrange("p (a k) -> p a k", a=4)).then_inc(cols_ready, 1)
            n_mix_0.dve(dve)
            even_in.dve(dve)
            dve.wait_ge(sink_in, 32)
            att_even.dve(dve)
            dve.tensor_copy(mv[:, 0, 0:1], rinv[:, 15, 0:1]).then_inc(even_done, 1)
            even_out.dve(dve)
            n_ffn2_0.dve(dve)
            ffn2_0.dve(dve)
            n_ffn1_1.dve(dve)
            ffn1_1.dve(dve)
            n_mix_1.dve(dve)
            odd_in.dve(dve)
            dve.wait_ge(bias_masked, 32)
            att_odd.dve(dve)
            odd_out.dve(dve)
            n_ffn2_1.dve(dve)
            ffn2_1.dve(dve)
            dve.wait_ge(final_x, 4)
            for tb in range(TB):
                m = dve.tensor_tensor_reduce(XN[:, tb, :], X[:, tb, :], X[:, tb, :], 1.0 / DM, 0.0,
                                             ALU.mult, ALU.add, ss[:, tb:tb + 1])
            dlink(dve, m)
            dlink(dve, dve.tensor_scalar(ss[:, 0:2], ss[:, 0:2], EPS_RMS, None, ALU.add))
            rsqrt(dve, ss[:, 0:2], 2)
            dve.wait_ge(vec_in, 48)
            for tb in range(TB):
                m = dve.scalar_tensor_tensor(X[:, tb, :], X[:, tb, :], ss[:, tb:tb + 1], rowvec[:, 0, :],
                                             ALU.mult, ALU.mult)
            dlink(dve, m)
            layer_norm(dve, rowvec[:, 1, :], V[:, 0, :], n_emb.normed)
            n_emb.dve(dve)
            rec_in.dve(dve)
            rec.dve_gates(dve)
            att_fox.dve(dve)
            rec_out.dve_fox(dve)
            rec.dve(dve)
            rec_out.dve(dve)
            n_gated.dve(dve)
            rec_proj.dve(dve)
            dve.wait_ge(mixed_x, 4)
            dve.wait_ge(vec2_in, 32)
            layer_norm(dve, rowvec[:, 0, :], rowvec[:, 1, :], n_conv.normed)
            n_conv.dve(dve)
            conv_ffn.dve(dve)
            dve.wait_ge(conv_x, 4)
            dve.wait_ge(vec3_in, 32)
            layer_norm(dve, rowvec[:, 0, :], rowvec[:, 1, :], out_x)

        @block.tensor
        def _(pe):
            pe.wait_ge(ident_in, 16)
            n_ffn1_0.pe(pe)
            ffn1_0.pe(pe)
            pe.wait_ge(rows_in, 16 * 2)
            for a in range(4):
                m = pe.transpose(PS[:, 2, 44 * a:44 * (a + 1)], conv_rows[:, a, :],
                                 consts[0:44, C_IDENT:C_IDENT + 44])
            m.then_inc(rows_turned, 1)
            n_mix_0.pe(pe)
            even_in.pe(pe)
            att_even.pe(pe)
            even_out.pe(pe)
            n_ffn2_0.pe(pe)
            ffn2_0.pe(pe)
            n_ffn1_1.pe(pe)
            ffn1_1.pe(pe)
            n_mix_1.pe(pe)
            odd_in.pe(pe)
            att_odd.pe(pe)
            odd_out.pe(pe)
            n_ffn2_1.pe(pe)
            ffn2_1.pe(pe)
            n_emb.pe(pe)
            rec_in.pe(pe)
            att_fox.pe(pe)
            rec.pe(pe)
            n_gated.pe(pe)
            rec_proj.pe(pe)
            n_conv.pe(pe)
            conv_ffn.pe(pe)


_INS = ["x", "ffn1_norm", "ffn1_w_gate", "ffn1_w_up", "ffn1_w_down", "mix_norm", "ffn2_norm", "ffn2_w_gate",
        "ffn2_w_up", "ffn2_w_down", "even_w_in", "a_q_norm", "a_k_norm", "b_sink", "even_w_out", "odd_w_qkv",
        "c_rel_bias", "odd_w_out", "final_norm", "ln_emb_g_2", "ln_emb_b_2", "w_in_2", "fox_f_bias_2",
        "fox_norm_g_2", "hgrn_norm_g_2", "w_o_2", "ln_mix_g_2", "ln_mix_b_2", "w_up_2", "conv_w_2", "conv_b_2",
        "w_down_2", "ln_ffn_g_2", "ln_ffn_b_2"]


def kernel(**inputs):
    import numpy as _np
    import concourse.bacc as _bacc
    from concourse import mybir as _mybir
    from concourse.bass_utils import run_bass_kernel_spmd as _run

    nc = _bacc.Bacc("TRN2", target_bir_lowering=False, num_devices=1)
    arrays, io = {}, {}
    for name in _INS + ["consts"]:
        if name == "consts":
            a = constant_table()
        elif name == "c_rel_bias":
            a = _np.ascontiguousarray(inputs[name][..., ::-1])
        else:
            a = _np.ascontiguousarray(inputs[name])
        arrays[f"in_{name}_dram"] = a
        io[name] = nc.dram_tensor(f"in_{name}_dram", a.shape, _mybir.dt.from_np(a.dtype), kind="ExternalInput").ap()
    out = nc.dram_tensor("out_0_dram", (1, S, DM), F32, kind="ExternalOutput").ap()
    build(nc, io, out)
    r = _run(nc, [arrays], core_ids=[0])
    return r.results[0]["out_0_dram"]
```

```python
from contextlib import ExitStack

import numpy as np

import concourse.bass as bass
from concourse import mybir

F32 = mybir.dt.float32
F32R = mybir.dt.float32r
I32 = mybir.dt.int32
U32 = mybir.dt.uint32
ACT = mybir.ActivationFunctionType
ALU = mybir.AluOpType
AX_X = mybir.AxisListType.X

P = 128
S = 256
TB = S // P
DM = 1024
KC = DM // P
FF = 2816
UNIT = 2048
RING = 3
LOOKAHEAD = 2
FF_STEPS = FF // 256
EPS_RMS = 1e-6
EPS_LN = 1e-5
ALPHA = 2.0 ** 0.25
NEG = -1e30
HD = 64
SCALE = HD ** -0.5
GRID_W = 64
NA_KW = 16
REL_W = 2 * NA_KW - 1
REL_H = 15
LEVELS = (32, 16, 8, 4, 2, 1)
RSQRT_MAGIC = 1597463007.0

C_IDENT = 0
C_ROPE = C_IDENT + P
C_WIN = C_ROPE + 4 * TB * HD
C_NB = C_WIN + TB * S
C_CAUSAL = C_NB + S
C_LEVEL = C_CAUSAL + TB * S
C_ZERO = C_LEVEL + 64 * len(LEVELS)
C_SEL = C_ZERO + 64
C_N = C_SEL + 8 * P


def constant_table():
    t = np.zeros((P, C_N), np.float32)
    t[:, C_IDENT:C_IDENT + P] = np.eye(P, dtype=np.float32)
    pos = np.arange(S)

    def angles(at, dim):
        inv = (np.float32(10000.0) ** (-np.arange(0, dim, 2, dtype=np.float32) / np.float32(dim))).astype(np.float32)
        a = (at.astype(np.float32)[:, None] * inv[None, :]).astype(np.float32).astype(np.float64)
        return np.cos(a).astype(np.float32), np.sin(a).astype(np.float32)

    cr, sr = angles(pos // GRID_W, HD // 2)
    cc, sc = angles(pos % GRID_W, HD // 2)
    c1, s1 = angles(pos, HD)
    rope = [np.concatenate([cr, cr, cc, cc], 1), np.concatenate([-sr, sr, -sc, sc], 1),
            np.concatenate([c1, c1], 1), np.concatenate([-s1, s1], 1)]
    for n, r in enumerate(rope):
        for tb in range(TB):
            at = C_ROPE + (n * TB + tb) * HD
            t[:, at:at + HD] = r[tb * P:(tb + 1) * P]
    key = np.arange(S)[None, :]
    for tb in range(TB):
        q = tb * P + np.arange(P)[:, None]
        t[:, C_WIN + tb * S:C_WIN + (tb + 1) * S] = np.where(np.abs(q - key) <= 128, 0, 8 * NEG)
        t[:, C_CAUSAL + tb * S:C_CAUSAL + (tb + 1) * S] = np.where(key <= q, 0, 8 * NEG)
    c = np.arange(P)[:, None] % GRID_W
    first = np.clip(c - NA_KW // 2, 0, GRID_W - NA_KW)
    kc = key % GRID_W
    kc = GRID_W - 1 - kc
    t[:, C_NB:C_NB + S] = np.where((kc >= first) & (kc < first + NA_KW), 0, 8 * NEG)
    s = np.arange(P)[:, None]
    for n, m in enumerate(LEVELS):
        late = np.array([x for x in range(P) if x % (2 * m) >= m])[None, :]
        ok = (s // (2 * m) == late // (2 * m)) & (s % (2 * m) < m)
        t[:, C_LEVEL + 64 * n:C_LEVEL + 64 * (n + 1)] = ok
    for h in range(8):
        t[h, C_SEL + h * P:C_SEL + (h + 1) * P] = 1
    return t


def build(nc, io, out):
    ctx = ExitStack()
    with ctx:
        place = {}

        def sb(name, shape, dt=F32):
            place[name] = (nc.sbuf_base + 31) // 32 * 32
            return ctx.enter_context(nc.sbuf_tensor(name, shape, dt))

        def as_f32r(name, base, shape):
            return nc.alloc_sbuf_tensor_at(name, shape, F32R, offset=place[base])

        def sem(name):
            return ctx.enter_context(nc.semaphore(name))

        raw = [sb(f"raw{n}", [P, UNIT]) for n in range(RING)]
        w_hi = [sb(f"w_hi{n}", [P, UNIT], F32R) for n in range(RING)]
        w_lo = [sb(f"w_lo{n}", [P, UNIT], F32R) for n in range(RING)]
        X = sb("x_tok", [P, TB, DM])
        XN = sb("xn_tok", [P, TB, DM])
        T = sb("t_feat", [P, KC, S])
        h_hi = sb("h_hi", [P, KC, S], F32R)
        h_lo = sb("h_lo", [P, KC, S], F32R)
        gu_hi = sb("gu_hi", [P, 2, S], F32R)
        gu_lo = sb("gu_lo", [P, 2, S], F32R)
        consts = sb("consts", [P, C_SEL])
        rowvec = sb("rowvec", [P, 2, DM])
        QKT = sb("qk_feat", [P, 16, S])
        V = sb("v_tok", [P, TB, DM])
        s_sb = sb("s_sb", [P, 2, 512])
        p_sb = sb("p_sb", [P, 2, 512])
        pt_sb = sb("pt_sb", [P, 2, 2, S])
        fox_k_lo = sb("fox_k_lo", [P, 4, S], F32R)
        arena = sb("arena", [P, 8192])
        convc = sb("convc", [P, 4, 44])
        ss = sb("ss", [P, 24])
        nt = sb("nt", [P, 4, 24])
        mx = sb("mx", [P, 16, 2])
        negm = sb("negm", [P, 16, 2])
        rsum = sb("rsum", [P, 16, 2])
        rinv = sb("rinv", [P, 16, 2])
        esink = sb("esink", [P, 8, 2])
        sink = sb("sink", [P, 8])
        neg_sink = sb("neg_sink", [P, 8])
        fbias = sb("fbias", [8, 1])
        bn = sb("bn", [P, TB, 2, 6])
        mv = sb("mv", [P, TB, 2])
        cq = sb("cq", [P, TB, 8])
        PS = ctx.enter_context(nc.psum_tensor("ps", [P, 8, 512], F32))

        ident = consts[:, C_IDENT:C_IDENT + P]

        def rope_tab(n, tb):
            at = C_ROPE + (n * TB + tb) * HD
            return consts[:, at:at + HD]

        win_mask = consts[:, C_WIN:C_WIN + TB * S]
        nb_mask = consts[:, C_NB:C_NB + S]
        causal_mask = consts[:, C_CAUSAL:C_CAUSAL + TB * S].rearrange("p (t k) -> p t k", t=TB)
        zeros = consts[:, C_ZERO:C_ZERO + 64]

        ffn_act = s_sb[:, 0, :]
        ffn_up = s_sb[:, 1, :]
        ffn_gu = p_sb[:, 0, :]
        PJ = arena[:, 0:3072].rearrange("p (t n) -> p t n", t=TB)
        R = arena[:, 3072:5632].rearrange("p (t n) -> p t n", t=TB)
        rope_t1 = arena[:, 5632:6912].rearrange("p (b n) -> p b n", b=2)
        rope_t2 = arena[:, 6912:8192].rearrange("p (b n) -> p b n", b=2)
        qk_gain = QKT[:, 12, 0:2 * HD].rearrange("p (a d) -> p a d", d=HD)
        gain_cos = QKT[:, 10, :].rearrange("p (t a d) -> p t a d", t=TB, d=HD)
        gain_sin = QKT[:, 11, :].rearrange("p (t a d) -> p t a d", t=TB, d=HD)
        bias = arena[:, :].rearrange("p (h t k) -> p h t k", h=16, t=TB)
        bias_flat = arena[:, :].rearrange("p (h n) -> p h n", h=16)
        T_flat = T[:, :, :].rearrange("p k s -> p (k s)")
        fox_bias = [T_flat[:, 384 * h:384 * (h + 1)] for h in range(5)] + \
                   [XN[:, 0, 0:384], XN[:, 1, 0:384], XN[:, 1, 512:896]]
        hg_b = arena[:, 4096:5120].rearrange("p (h t) -> p h t", h=4)
        hg_k = arena[:, 5120:6144].rearrange("p (h t) -> p h t", h=4)
        hg_d = arena[:, 6144:7168].rearrange("p (h t) -> p h t", h=4)
        hg_gate = arena[:, 7168:8192].rearrange("p (t n) -> p t n", t=TB)
        hg_e = arena[:, 0:1024].rearrange("p (h t) -> p h t", h=4)
        hg_kh = arena[:, 1024:2048].rearrange("p (h t) -> p h t", h=4)
        hg_qh = arena[:, 2048:3072].rearrange("p (h t) -> p h t", h=4)
        hg_st = arena[:, 3072:4096].rearrange("p (b t) -> p b t", b=8)
        hg_s2 = XN[:, 0, 512:1024].rearrange("p (h t) -> p h t", h=4)
        hg_q = QKT[:, 8:12, :]
        hg_f = QKT[:, 12:16, :]
        QK_hi = as_f32r("qk_hi", "qk_feat", [P, 16, S])
        V_hi = as_f32r("v_hi", "v_tok", [P, TB, DM])
        T_r = as_f32r("t_r", "t_feat", [P, KC, S])
        XN_r = as_f32r("xn_r", "xn_tok", [P, KC, S])
        rowvec_r = as_f32r("rowvec_r", "rowvec", [P, 2, DM])
        pt_hi = as_f32r("pt_hi", "pt_sb", [P, 2, 2, S])
        pt_hi_flat = pt_hi[:, :, :, :].rearrange("p a k q -> p a (k q)")
        pt_lo_flat = [z[:, :, :].rearrange("p k q -> p (k q)") for z in (gu_hi, gu_lo)]

        def even_lo(at):
            return T_r[:, at, :] if at.start < 5 else XN_r[:, at.start - 5:at.stop - 5, :]

        even_v_hi, even_v_lo = (V_hi[:, a, :].rearrange("p (m h w d) -> p m h w d", h=2, w=2, d=HD) for a in range(2))
        even_v_src = PJ.rearrange("p t (b n) -> p (t b) n", b=2)[:, :, 640:768].rearrange("p m (h d) -> p m h d", d=HD)

        def odd_lo(at):
            return T_r[:, at, :] if at.start < 8 else XN_r[:, at.start - 8:at.stop - 8, :]

        odd_v_lo = rowvec_r[:, :, :]
        fox_v_lo = rowvec_r[:, 0, :].rearrange("p (t n) -> p t n", t=TB)
        fox_q_lo = rowvec_r[:, 1, :].rearrange("p (k s) -> p k s", s=S)
        wf = pt_sb[:, 0, 0, 0:64].rearrange("p (k n) -> p k n", k=KC)
        sel = s_sb[0:8, :, :].rearrange("p a b -> p (a b)").rearrange("p (h q) -> p h q", h=8)
        f_z = p_sb[0:8, 0, 0:256]
        f_a = p_sb[0:8, 0, 256:512]
        f_m = p_sb[0:8, 1, 0:256]
        f_c = p_sb[0:8, 1, 256:512]

        w_landed = [sem(f"w_landed{n}") for n in range(RING)]
        w_hi_ready = sem("w_hi_ready")
        w_lo_ready = sem("w_lo_ready")
        w_released = sem("w_released")
        bank_done = sem("bank_done")
        out_bank_done = sem("out_bank_done")
        gain_in = sem("gain_in")
        FFN_UNITS = 3 * FF_STEPS
        sizes = [("ffn1_0", FFN_UNITS), ("even_in", 6), ("even_out", 4), ("ffn2_0", FFN_UNITS),
                 ("ffn1_1", FFN_UNITS), ("odd_in", 12), ("odd_out", 4), ("ffn2_1", FFN_UNITS),
                 ("rec_in", 14), ("rec_out", 4), ("conv_ffn", FFN_UNITS)]
        first_unit, total = {}, 0
        for name, n in sizes:
            first_unit[name] = total
            total += n
        TOTAL_UNITS = total

        def split_hi(act, n, i=0):
            if isinstance(i, int) and n + 3 * i >= TOTAL_UNITS:
                return
            slot = n % RING
            act.wait_ge(w_landed[slot], 16 * i + 16 * (n // RING + 1))
            if n >= RING:
                act.wait_ge(w_released, 3 * i + (n - RING + 1))
            act.activation(w_hi[slot][:, :], raw[slot][:, :], ACT.Copy).then_inc(w_hi_ready, 1)

        def split_lo(dve, n, i=0):
            if isinstance(i, int) and n + 3 * i >= TOTAL_UNITS:
                return
            slot = n % RING
            dve.wait_ge(w_hi_ready, 3 * i + (n + 1))
            dve.tensor_tensor(w_lo[slot][:, :], raw[slot][:, :], w_hi[slot][:, :].bitcast(F32),
                              ALU.subtract).then_inc(w_lo_ready, 1)

        def load_unit(sp, n, src, view, i=0):
            slot = n % RING
            if n >= RING:
                sp.wait_ge(w_lo_ready, 3 * i + (n - RING + 1))
            sp.dma_start(view(raw[slot]), src).then_inc(w_landed[slot], 16)

        def feat_view(w):
            return w[:, :].rearrange("p (k n) -> p k n", k=KC)

        def tok_view(w):
            return w[:, :].rearrange("p (k n) -> p k n", k=4)

        def down_view(w):
            return w[:, :].rearrange("p (k n) -> p k n", k=2)

        def feat_src(w, col):
            return w[:, bass.ds(col, 256)].rearrange("(k p) n -> p k n", p=P)

        def tok_src(w, half, col):
            return w[half * 512:(half + 1) * 512, col:col + 512].rearrange("(k p) n -> p k n", p=P)

        def down_src(w, row):
            return w[bass.ds(row, 256), :].rearrange("(k p) n -> p k n", p=P)

        def three(mm, o, ahi, alo, bhi, blo, first, last):
            mm(o, ahi, bhi, start=first, stop=False)
            mm(o, alo, bhi, start=False, stop=False)
            return mm(o, ahi, blo, start=False, stop=last)

        def feat_unit(pe, n, bank, i=0, ready=None):
            slot = n % RING
            pe.wait_ge(w_lo_ready, 3 * i + (n + 1))
            for t in range(2):
                for k in range(KC):
                    if ready is not None and t == 0:
                        ready(pe, k)
                    a, b = feat_view(w_hi[slot]), feat_view(w_lo[slot])
                    last = three(pe.matmul, PS[:, bank, t * S:(t + 1) * S],
                                 a[:, k, t * P:(t + 1) * P], b[:, k, t * P:(t + 1) * P],
                                 h_hi[:, k, :], h_lo[:, k, :], k == 0, k == KC - 1)
            last.then_inc(w_released, 1)

        def tok_unit(pe, n, half, banks, ready=None, done=None):
            slot = n % RING
            pe.wait_ge(w_lo_ready, n + 1)
            a, b = tok_view(w_hi[slot]), tok_view(w_lo[slot])
            for tb in range(TB):
                for k in range(4):
                    kk = 4 * half + k
                    if ready is not None and tb == 0:
                        ready(pe, kk)
                    last = three(pe.matmul, PS[:, banks[tb], :],
                                 h_hi[:, kk, tb * P:(tb + 1) * P], h_lo[:, kk, tb * P:(tb + 1) * P],
                                 a[:, k, :], b[:, k, :], kk == 0, kk == KC - 1)
                if done is not None and tb == 0:
                    last.then_inc(done, 1)
            last.then_inc(w_released, 1)

        def down_unit(pe, n, first, last_unit, i=0):
            hi, lo = (h_hi, h_lo) if last_unit else (gu_hi, gu_lo)
            slot = n % RING
            pe.wait_ge(w_lo_ready, 3 * i + (n + 1))
            a, b = down_view(w_hi[slot]), down_view(w_lo[slot])
            for tb in range(TB):
                for half in range(2):
                    for k in range(2):
                        last = three(pe.matmul, PS[:, 4 + 2 * tb + half, :],
                                     hi[:, k, tb * P:(tb + 1) * P], lo[:, k, tb * P:(tb + 1) * P],
                                     a[:, k, half * 512:(half + 1) * 512], b[:, k, half * 512:(half + 1) * 512],
                                     first and k == 0, last_unit and k == 1)
                    if last_unit and (tb, half) != (1, 1):
                        last.then_inc(bank_done, 1)
            return last.then_inc(w_released, 1)

        def chain(name):
            step, count = sem(name), [0]

            def link(eng, ins):
                count[0] += 1
                ins.then_inc(step, 1)
                eng.wait_ge(step, count[0])
            return link

        dlink = chain("dve_step")
        alink = chain("act_step")
        plink = chain("pool_step")

        def rsqrt(dve, x, n):
            y, t, u = nt[:, 0, 0:n], nt[:, 1, 0:n], nt[:, 2, 0:n]
            dlink(dve, dve.tensor_scalar(y.bitcast(I32), x.bitcast(I32), -0.5, RSQRT_MAGIC, ALU.mult, ALU.add))
            for step in range(3):
                dlink(dve, dve.tensor_tensor(t, y, y, ALU.mult))
                dlink(dve, dve.scalar_tensor_tensor(u, t, -0.5, x, ALU.mult, ALU.mult))
                o = x if step == 2 else y
                dlink(dve, dve.scalar_tensor_tensor(o, u, 1.5, y, ALU.add, ALU.mult))

        QUARTERS = [(0, 0), (1, 0), (0, 1), (1, 1)]

        class Norm:

            x_ready = sem("norm_x_ready")
            square = sem("norm_square")
            normed = sem("norm_normed")
            turned = sem("norm_turned")
            hi = sem("norm_hi")
            lo = sem("norm_lo")

            def __init__(self, at, second_unit, src=None, banks=(0, 1, 2, 3)):
                self.at, self.rms, self.banks, self.second_unit = at, src is None, banks, second_unit
                self.src = XN if src is None else src
                self.gain = rowvec[:, at % 2, :]

            def quarters(self, half):
                return [(q, tb, h) for q, (tb, h) in enumerate(QUARTERS) if half is None or h == half]

            def pe(self, pe, half=None):
                for q, tb, half in self.quarters(half):
                    pe.wait_ge(self.normed, self.at * 4 + q + 1)
                    if self.banks[q] in self.banks[:q]:
                        pe.wait_ge(self.lo, self.at * 4 + q - 1)
                    for k in range(4):
                        kk = 4 * half + k
                        m = pe.transpose(PS[:, self.banks[q], k * P:(k + 1) * P], self.src[:, tb, kk * P:(kk + 1) * P], ident)
                    m.then_inc(self.turned, 1)

            def ready(self, pe, k):
                if k in (0, 4):
                    pe.wait_ge(self.lo, self.at * 4 + (2 if k == 0 else 4))

            def act(self, act, first=False, half=None):
                if self.rms:
                    for q, (tb, part) in enumerate(self.order):
                        if first:
                            act.wait_ge(x_in[tb], 16)
                        else:
                            act.wait_ge(self.x_ready, self.at * 4 - 4 + q + 1)
                        act.activation(XN[:, tb, part * 512:(part + 1) * 512], X[:, tb, part * 512:(part + 1) * 512],
                                       ACT.Square, scale=1.0 / 32.0, accum_out=ss[:, 2 * part + tb:2 * part + tb + 1])\
                           .then_inc(self.square, 1)
                if first:
                    split_hi(act, 0)
                    split_hi(act, 1)
                for q, tb, half in self.quarters(half):
                    act.wait_ge(self.turned, self.at * 4 + q + 1)
                    act.activation(h_hi[:, 4 * half:4 * half + 4, tb * P:(tb + 1) * P],
                                   PS[:, self.banks[q], :].rearrange("p (k t) -> p k t", k=4), ACT.Copy)\
                       .then_inc(self.hi, 1)

            def dve(self, dve, first=False, half=None):
                if self.rms:
                    dve.wait_ge(self.square, self.at * 4 + 4)
                    dlink(dve, dve.scalar_tensor_tensor(ss[:, 0:2], ss[:, 0:2], EPS_RMS, ss[:, 2:4], ALU.add, ALU.add))
                    rsqrt(dve, ss[:, 0:2], 2)
                    dve.wait_ge(gain_in, 16 * (self.at + 1))
                    for q, tb, part in self.quarters(None):
                        f = slice(part * 512, (part + 1) * 512)
                        dve.scalar_tensor_tensor(XN[:, tb, f], X[:, tb, f], ss[:, tb:tb + 1], self.gain[:, f],
                                                 ALU.mult, ALU.mult).then_inc(self.normed, 1)
                if first:
                    split_lo(dve, 0)
                for q, tb, half in self.quarters(half):
                    dve.wait_ge(self.hi, self.at * 4 + q + 1)
                    o = h_lo[:, 4 * half:4 * half + 4, tb * P:(tb + 1) * P]
                    h = h_hi[:, 4 * half:4 * half + 4, tb * P:(tb + 1) * P].bitcast(F32)
                    dve.tensor_tensor(o, PS[:, self.banks[q], :].rearrange("p (k t) -> p k t", k=4), h, ALU.subtract)\
                       .then_inc(self.lo, 1)
                if self.second_unit is not None:
                    split_lo(dve, self.second_unit)

        class Ffn:

            act_done = sem("ffn_act_done")
            gu_done = sem("ffn_gu_done")
            guhi_done = sem("ffn_guhi_done")
            gulo_done = sem("ffn_gulo_done")

            def __init__(self, at, name, wg, wu, wd, norm, after, conv=False):
                self.u0, self.b = first_unit[name], at * FF_STEPS
                self.wg, self.wu, self.wd, self.norm, self.conv = wg, wu, wd, norm, conv
                self.after, self.banks_before = after, 3 * at
                if conv:
                    self.tap2 = sem(name + "_tap2")
                    self.tap1 = sem(name + "_tap1")
                    self.a_conv = sem(name + "_a_conv")
                    self.u_conv = sem(name + "_u_conv")

            def sp(self, sp):
                u = self.u0
                load_unit(sp, u, feat_src(self.wg, 0), feat_view)
                load_unit(sp, u + 1, feat_src(self.wu, 0), feat_view)
                load_unit(sp, u + 2, feat_src(self.wg, 256), feat_view)
                load_unit(sp, u + 3, feat_src(self.wu, 256), feat_view)
                load_unit(sp, u + 4, down_src(self.wd, 0), down_view)
                with sp.Fori(0, FF_STEPS - 2) as i:
                    load_unit(sp, u + 5, feat_src(self.wg, i * 256 + 512), feat_view, i)
                    load_unit(sp, u + 6, feat_src(self.wu, i * 256 + 512), feat_view, i)
                    load_unit(sp, u + 7, down_src(self.wd, i * 256 + 256), down_view, i)
                load_unit(sp, u + 3 * FF_STEPS - 1, down_src(self.wd, FF - 256), down_view)

            def pe(self, pe):
                u = self.u0
                feat_unit(pe, u, 0, ready=self.norm.ready)
                self.up(pe, u + 1, 1, 0, None)
                self.up(pe, u + 2, 0, 0, 1)
                self.up(pe, u + 3, 1, 0, 1)
                pe.wait_ge(self.gulo_done, self.b + 1)
                down_unit(pe, u + 4, True, False)
                with pe.Fori(0, FF_STEPS - 2) as i:
                    self.up(pe, u + 5, 0, i, i + 2)
                    self.up(pe, u + 6, 1, i, i + 2)
                    pe.wait_ge(self.gulo_done, i + (self.b + 2))
                    down_unit(pe, u + 7, False, False, i)
                pe.wait_ge(self.gulo_done, self.b + FF_STEPS)
                down_unit(pe, u + 3 * FF_STEPS - 1, False, True)

            def up(self, pe, n, which, i, free):
                if free is not None:
                    if self.conv:
                        pe.wait_ge(self.a_conv if which == 0 else self.u_conv, free)
                    else:
                        pe.wait_ge(self.act_done if which == 0 else self.gu_done, free + self.b)
                feat_unit(pe, n, which, i)

            def conv_tap2(self, act, which, i, at):
                act.wait_ge(w_released, self.u0 + 1 + which + at)
                dst = ffn_act if which == 0 else ffn_up
                for t in range(2):
                    tile = i * 2 + (22 * which + t)
                    m = act.activation(dst[:, t * S:(t + 1) * S], PS[:, which, t * S:(t + 1) * S], ACT.Identity,
                                       bias=convc[:, 3, bass.ds(tile, 1)], scale=convc[:, 2, bass.ds(tile, 1)])
                m.then_inc(self.tap2, 1)

            def conv_taps(self, dve, which, i):
                dve.wait_ge(self.tap2, 2 * i + (which + 1))
                dst = ffn_act if which == 0 else ffn_up
                for t in range(2):
                    tile = i * 2 + (22 * which + t)
                    y = dst[:, t * S + 1:(t + 1) * S]
                    m = dve.scalar_tensor_tensor(y, PS[:, which, t * S:(t + 1) * S - 1],
                                                 convc[:, 1, bass.ds(tile, 1)], y, ALU.mult, ALU.add)
                m.then_inc(self.tap1, 1)
                dve.wait_ge(self.tap1, 2 * i + (which + 1))
                for t in range(2):
                    tile = i * 2 + (22 * which + t)
                    y = dst[:, t * S + 2:(t + 1) * S]
                    m = dve.scalar_tensor_tensor(y, PS[:, which, t * S:(t + 1) * S - 2],
                                                 convc[:, 0, bass.ds(tile, 1)], y, ALU.mult, ALU.add)
                m.then_inc(self.a_conv if which == 0 else self.u_conv, 1)

            def act_step(self, act, i, first):
                u, r = self.u0, (0 if first else i - 1)
                if first:
                    at_g, at_u = 0, 0
                    split_hi(act, u + 2)
                else:
                    at_g = 3 * r + 2
                    at_u = 3 * r + 2
                    split_hi(act, u + 4, i=r)
                if self.conv:
                    self.conv_tap2(act, 0, i, at_g)
                split_hi(act, u + 3 if first else u + 5, i=r)
                if self.conv:
                    self.conv_tap2(act, 1, i, at_u)
                    act.wait_ge(self.a_conv, i + 1)
                    act.activation(ffn_act, ffn_act, ACT.Gelu).then_inc(self.act_done, 1)
                else:
                    act.wait_ge(w_released, u + 1 + at_g)
                    act.activation(ffn_act, PS[:, 0, :], ACT.Silu).then_inc(self.act_done, 1)
                if not first:
                    split_hi(act, u + 6, i=r)
                act.wait_ge(self.gu_done, i + (self.b + 1))
                last = isinstance(i, int) and i == FF_STEPS - 1
                if last:
                    act.wait_ge(w_released, u + 3 * r + 4)
                elif not first:
                    act.wait_ge(w_released, u + 3 * r + 5)
                hi = h_hi[:, 0:2, :] if last else gu_hi[:, :, :]
                act.activation(hi, ffn_gu.rearrange("p (t s) -> p t s", t=2), ACT.Copy)\
                   .then_inc(self.guhi_done, 1)

            def act(self, act):
                self.act_step(act, 0, True)
                self.act_step(act, 1, False)
                with act.Fori(1, FF_STEPS - 2) as i:
                    self.act_step(act, i + 1, False)
                self.act_step(act, FF_STEPS - 1, False)
                split_hi(act, self.u0 + 3 * FF_STEPS + 1)

            def dve_step(self, dve, i, first):
                u, r = self.u0, (0 if first else i - 1)
                split_lo(dve, u + 2 if first else u + 4, i=r)
                if self.conv:
                    self.conv_taps(dve, 0, i)
                split_lo(dve, u + 3 if first else u + 5, i=r)
                if self.conv:
                    self.conv_taps(dve, 1, i)
                    dve.wait_ge(self.u_conv, i + 1)
                    dve.wait_ge(self.act_done, i + (self.b + 1))
                    if not first:
                        dve.wait_ge(self.gulo_done, i + self.b)
                    dve.tensor_tensor(ffn_gu, ffn_act, ffn_up, ALU.mult).then_inc(self.gu_done, 1)
                else:
                    dve.wait_ge(w_released, u + 2 if first else u + 3 * r + 4)
                    dve.wait_ge(self.act_done, i + (self.b + 1))
                    if not first:
                        dve.wait_ge(self.gulo_done, i + self.b)
                    dve.tensor_tensor(ffn_gu, PS[:, 1, :], ffn_act, ALU.mult).then_inc(self.gu_done, 1)
                if not first:
                    split_lo(dve, u + 6, i=r)
                dve.wait_ge(self.guhi_done, i + (self.b + 1))
                last = isinstance(i, int) and i == FF_STEPS - 1
                hi, lo = (h_hi[:, 0:2, :], h_lo[:, 0:2, :]) if last else (gu_hi[:, :, :], gu_lo[:, :, :])
                dve.tensor_tensor(lo, ffn_gu.rearrange("p (t s) -> p t s", t=2), hi.bitcast(F32), ALU.subtract)\
                   .then_inc(self.gulo_done, 1)

            def dve(self, dve, then=None):
                self.dve_step(dve, 0, True)
                with dve.Fori(0, FF_STEPS - 2) as i:
                    self.dve_step(dve, i + 1, False)
                self.dve_step(dve, FF_STEPS - 1, False)
                for tb in range(TB):
                    for half in range(2):
                        if (tb, half) == (1, 1):
                            dve.wait_ge(w_released, self.u0 + 3 * FF_STEPS)
                        else:
                            dve.wait_ge(bank_done, self.banks_before + 2 * tb + half + 1)
                        x = X[:, tb, half * 512:(half + 1) * 512]
                        y = PS[:, 4 + 2 * tb + half, :]
                        if self.conv:
                            m = dve.scalar_tensor_tensor(x, x, ALPHA, y, ALU.mult, ALU.add)
                        else:
                            m = dve.scalar_tensor_tensor(x, y, 0.5, x, ALU.mult, ALU.add)
                        m.then_inc(self.after, 1)
                        if then is not None:
                            then(2 * tb + half, tb, half)

        class OutProj:

            def __init__(self, name, w, ready, after, at, banks, alpha=None):
                self.u0, self.w, self.ready, self.after, self.alpha = first_unit[name], w, ready, after, alpha
                self.done_before, self.banks = 2 * at, banks

            def sp(self, sp):
                for j in range(4):
                    load_unit(sp, self.u0 + j, tok_src(self.w, j // 2, (j % 2) * 512), tok_view)

            def pe(self, pe, j):
                half, c = divmod(j, 2)
                tok_unit(pe, self.u0 + j, half, self.banks[c], ready=self.ready if c == 0 else None,
                         done=out_bank_done if half else None)

            def act(self, act, j):
                split_hi(act, self.u0 + j + LOOKAHEAD)

            def dve(self, dve, j, then=None):
                if j < 3:
                    split_lo(dve, self.u0 + j + LOOKAHEAD)
                half, c = divmod(j, 2)
                if half == 0:
                    return
                for tb in range(TB):
                    if tb == 0:
                        dve.wait_ge(out_bank_done, self.done_before + c + 1)
                    else:
                        dve.wait_ge(w_released, self.u0 + j + 1)
                    x = X[:, tb, c * 512:(c + 1) * 512]
                    y = PS[:, self.banks[c][tb], :]
                    if self.alpha is None:
                        m = dve.tensor_tensor(x, y, x, ALU.add)
                    else:
                        m = dve.scalar_tensor_tensor(x, x, self.alpha, y, ALU.mult, ALU.add)
                    m.then_inc(self.after, 1)
                    if then is not None:
                        then(2 * c + tb, tb, c)

        class Proj:

            class Feat:
                def __init__(self, col, bank, free, out, lo=None):
                    self.col, self.bank, self.free, self.out, self.lo = col, bank, free, out, lo

            class Tok:
                def __init__(self, col, bank, free, out, lo=None):
                    self.col, self.bank, self.free, self.out, self.lo = col, bank, free, out, lo

            def __init__(self, name, w, norm, chunks):
                self.u0, self.w, self.norm = first_unit[name], w, norm
                self.act_out = sem(name + "_act_out")
                self.dve_out = sem(name + "_dve_out")
                self.units = []
                for c, chunk in enumerate(chunks):
                    for j in range(1 if isinstance(chunk, Proj.Feat) else 2):
                        self.units.append((c, chunk, j))

            def sp(self, sp):
                for n, (_, chunk, j) in enumerate(self.units):
                    if isinstance(chunk, Proj.Feat):
                        load_unit(sp, self.u0 + n, feat_src(self.w, chunk.col), feat_view)
                    else:
                        load_unit(sp, self.u0 + n, tok_src(self.w, j, chunk.col), tok_view)

            def wait_read(self, eng, chunks):
                eng.wait_ge(self.act_out, chunks)
                eng.wait_ge(self.dve_out, chunks)

            def pe(self, pe, n):
                _, chunk, j = self.units[n]
                if j == 0 and chunk.free:
                    self.wait_read(pe, chunk.free)
                ready = self.norm.ready if n < 2 and j == n else None
                if isinstance(chunk, Proj.Feat):
                    feat_unit(pe, self.u0 + n, chunk.bank, ready=ready)
                else:
                    tok_unit(pe, self.u0 + n, j, (chunk.bank, chunk.bank + 1), ready=ready)

            def sums(self, chunk):
                if isinstance(chunk, Proj.Feat):
                    return PS[:, chunk.bank, :].rearrange("p (a s) -> p a s", a=2)
                return PS[:, chunk.bank:chunk.bank + 2, :]

            def act(self, act, n, split=True):
                if split:
                    split_hi(act, self.u0 + n + LOOKAHEAD)
                c, chunk, j = self.units[n]
                if isinstance(chunk, Proj.Tok) and j == 0:
                    return
                act.wait_ge(w_released, self.u0 + n + 1)
                src = self.sums(chunk)
                if chunk.lo is not None:
                    act.activation(chunk.out, src, ACT.Copy).then_inc(self.act_out, 1)
                else:
                    act.activation(chunk.out[:, 0, :], src[:, 0, :], ACT.Copy).then_inc(self.act_out, 1)

            def dve(self, dve, n, split=True):
                if split:
                    split_lo(dve, self.u0 + n + LOOKAHEAD)
                c, chunk, j = self.units[n]
                if isinstance(chunk, Proj.Tok) and j == 0:
                    return
                dve.wait_ge(w_released, self.u0 + n + 1)
                src = self.sums(chunk)
                dve.wait_ge(self.act_out, c + 1)
                if chunk.lo is not None:
                    dve.tensor_tensor(chunk.lo, src, chunk.out.bitcast(F32), ALU.subtract).then_inc(self.dve_out, 1)
                else:
                    dve.tensor_copy(chunk.out[:, 1, :], src[:, 1, :]).then_inc(self.dve_out, 1)

        class Attention:

            def __init__(self, name, heads, q, k, v, bias, pt_banks, out_step=7, sink_of=None, causal=False,
                         rows_reversed=False, inputs_free=None):
                self.n, self.q, self.k, self.v, self.bias = heads, q, k, v, bias
                self.pt_banks, self.out_step, self.sink_of = pt_banks, out_step, sink_of
                self.causal, self.rows_reversed, self.inputs_free = causal, rows_reversed, inputs_free
                self.scores = sem(name + "_scores")
                self.max_ready = sem(name + "_max")
                self.exp_done = sem(name + "_exp")
                self.inverse = sem(name + "_inverse")
                self.scaled = sem(name + "_scaled")
                self.turned = sem(name + "_turned")
                self.pt_hi_ready = sem(name + "_pt_hi")
                self.pt_lo_ready = sem(name + "_pt_lo")
                self.out_ready = sem(name + "_out")
                self.hi = sem(name + "_hi")
                self.lo = sem(name + "_lo")

            def spans(self):
                return [(0, P, 0), (S, S, P)] if self.causal else [(0, S, 0), (S, S, S)]

            def pt(self, g):
                return PS[:, self.pt_banks[g % 2], :], pt_hi_flat[:, g % 2], pt_lo_flat[g % 2], (3 if self.causal else 4) * P

            def pe_scores(self, pe, g):
                if g >= 2:
                    pe.wait_ge(self.exp_done, g - 1)
                k_hi, k_lo = self.k(g)
                for tb, (at, n, _) in enumerate(self.spans()):
                    m = three(pe.matmul, PS[:, g % 2, at:at + n], *self.q(g, tb), k_hi[:, 0:n], k_lo[:, 0:n],
                              True, True)
                m.then_inc(self.scores, 1)

            def pe_turn(self, pe, g):
                pe.wait_ge(self.exp_done if self.causal else self.scaled, g + 1)
                before = 2 if self.pt_banks[0] != self.pt_banks[1] else 1
                if g >= before:
                    pe.wait_ge(self.pt_lo_ready, g + 1 - before)
                bank, _, _, _ = self.pt(g)
                blocks = [(0, 0), (0, 1), (1, 1)] if self.causal else [(0, 0), (0, 1), (1, 0), (1, 1)]
                for n, (kb, tb) in enumerate(blocks):
                    m = pe.transpose(bank[:, n * P:(n + 1) * P],
                                     p_sb[:, g % 2, tb * S + kb * P:tb * S + (kb + 1) * P], ident)
                m.then_inc(self.turned, 1)

            def pe_values(self, pe, g):
                pe.wait_ge(self.pt_lo_ready, g + 1)
                _, hi, lo, _ = self.pt(g)
                if self.causal:
                    for tb in range(TB):
                        for kb in range(tb + 1):
                            at = (kb + tb) * P
                            m = three(pe.matmul, PS[:, 4 + tb, g * HD:(g + 1) * HD], hi[:, at:at + P],
                                      lo[:, at:at + P], *self.v(g, kb), kb == 0, kb == tb)
                else:
                    if g % 2 == 0 and g >= 4:
                        pe.wait_ge(self.lo, g // 2 - 1)
                    for kb in range(2):
                        m = three(pe.matmul, PS[:, 4 + (g // 2) % 2, (g % 2) * S:(g % 2 + 1) * S], *self.v(g, kb),
                                  hi[:, kb * S:(kb + 1) * S], lo[:, kb * S:(kb + 1) * S], kb == 0, kb == 1)
                m.then_inc(self.out_ready, 1)

            def pe(self, pe, s):
                if not self.causal and 3 <= s <= self.n + 2:
                    self.pe_turn(pe, s - 3)
                if s < self.n:
                    self.pe_scores(pe, s)
                if 5 <= s <= self.n + 4:
                    self.pe_values(pe, s - 5)
                if self.causal and 3 <= s <= self.n + 2:
                    self.pe_turn(pe, s - 3)

            def dve_max(self, dve, g):
                dve.wait_ge(self.scores, g + 1)
                b = self.bias(g)
                if b is None:
                    dlink(dve, dve.tensor_reduce(mx[:, g, :], PS[:, g % 2, :].rearrange("p (t k) -> p t k", t=TB),
                                                 AX_X, ALU.max))
                    dve.tensor_scalar(negm[:, g, :], mx[:, g, :], -SCALE, None, ALU.mult).then_inc(self.max_ready, 1)
                    return
                if g >= 2:
                    dve.wait_ge(self.exp_done, g - 1)
                for tb, (at, n, ab) in enumerate(self.spans()):
                    o, i, bb = s_sb[:, g % 2, at:at + n], PS[:, g % 2, at:at + n], b[:, ab:ab + n]
                    if self.rows_reversed:
                        bb = bass.AP(tensor=bb.tensor, offset=bb.offset + GRID_W - 1,
                                     ap=[list(bb.ap[0]), [GRID_W, 4], [-1, GRID_W]])
                        o, i = (z.rearrange("p (a k) -> p a k", k=GRID_W) for z in (o, i))
                    to = mx if self.has_sink(g) else negm
                    m = dve.tensor_tensor_reduce(o, i, bb, -SCALE, 3e38, ALU.add, ALU.min, to[:, g, tb:tb + 1])
                if self.has_sink(g):
                    dlink(dve, m)
                    m = dve.tensor_scalar(negm[:, g, :], mx[:, g, :], neg_sink[:, g - 8:g - 7], None, ALU.min)
                m.then_inc(self.max_ready, 1)

            def has_sink(self, g):
                return self.sink_of is not None and self.sink_of(g) is not None

            def act_exp(self, act, g):
                act.wait_ge(self.max_ready, g + 1)
                if g >= 2:
                    act.wait_ge(self.turned, g - 1)
                raw_scores = self.bias(g) is None
                if self.has_sink(g):
                    act.activation(esink[:, g % 8, :], negm[:, g, :], ACT.Exp, bias=self.sink_of(g))
                for tb, (at, n, _) in enumerate(self.spans()):
                    src = PS[:, g % 2, at:at + n] if raw_scores else s_sb[:, g % 2, at:at + n]
                    m = act.activation(p_sb[:, g % 2, at:at + n], src, ACT.Exp, bias=negm[:, g, tb:tb + 1],
                                       scale=SCALE if raw_scores else -1.0, accum_out=rsum[:, g, tb:tb + 1])
                m.then_inc(self.exp_done, 1)

            def dve_inverse(self, dve, g):
                dve.wait_ge(self.exp_done, g + 1)
                if self.has_sink(g):
                    dlink(dve, dve.tensor_tensor(rsum[:, g, :], rsum[:, g, :], esink[:, g % 8, :], ALU.add))
                dve.reciprocal(rinv[:, g, :], rsum[:, g, :]).then_inc(self.inverse, 1)

            def dve_scale(self, dve, g):
                dve.wait_ge(self.inverse, g + 1)
                for tb in range(TB):
                    p = p_sb[:, g % 2, tb * S:(tb + 1) * S]
                    m = dve.tensor_scalar(p, p, rinv[:, g, tb:tb + 1], None, ALU.mult)
                m.then_inc(self.scaled, 1)

            def act_turned(self, act, g):
                act.wait_ge(self.turned, g + 1)
                if g >= 2:
                    act.wait_ge(self.out_ready, g - 1)
                bank, hi, _, n = self.pt(g)
                act.activation(hi[:, 0:n], bank[:, 0:n], ACT.Copy).then_inc(self.pt_hi_ready, 1)

            def dve_turned(self, dve, g):
                dve.wait_ge(self.pt_hi_ready, g + 1)
                bank, hi, lo, n = self.pt(g)
                dve.tensor_tensor(lo[:, 0:n], bank[:, 0:n], hi[:, 0:n].bitcast(F32), ALU.subtract)\
                   .then_inc(self.pt_lo_ready, 1)

            def pair_of(self, s):
                p = s - self.out_step
                return None if self.causal or p < 0 or p % 2 else p // 2

            def halves(self, pair):
                for a in range(2):
                    rows = slice(a * HD, (a + 1) * HD)
                    yield rows, PS[rows, 4 + pair % 2, a * S:(a + 1) * S]

            def act(self, act, s):
                if 1 <= s <= self.n:
                    self.act_exp(act, s - 1)
                if 3 <= s <= self.n + 2:
                    self.act_turned(act, s - 3)
                pair = self.pair_of(s)
                if pair is not None:
                    if self.inputs_free is not None and pair == 0:
                        act.wait_ge(w_released, self.inputs_free)
                    act.wait_ge(self.out_ready, 2 * pair + 2)
                    for rows, src in self.halves(pair):
                        m = act.activation(h_hi[rows, pair, :], src, ACT.Copy)
                    m.then_inc(self.hi, 1)

            def dve(self, dve, s):
                if 2 <= s <= self.n + 1:
                    self.dve_inverse(dve, s - 2)
                    if not self.causal:
                        self.dve_scale(dve, s - 2)
                if 4 <= s <= self.n + 3:
                    self.dve_turned(dve, s - 4)
                if s < self.n:
                    self.dve_max(dve, s)
                pair = self.pair_of(s)
                if pair is not None:
                    dve.wait_ge(self.hi, pair + 1)
                    for rows, src in self.halves(pair):
                        m = dve.tensor_tensor(h_lo[rows, pair, :], src, h_hi[rows, pair, :].bitcast(F32), ALU.subtract)
                    m.then_inc(self.lo, 1)

            def ready(self, pe, k):
                pe.wait_ge(self.lo, k + 1)

        class EvenTurn:
            BANKS = ((0, 1, 3), (6, 7, 6))

            def __init__(self, proj):
                self.proj = proj
                self.rope = [sem("even_rope_a"), sem("even_rope_b")]
                self.turned = sem("even_turned")
                self.const = sem("even_const")
                self.tables_ready = sem("even_tables")
                self.squares = sem("even_squares")
                self.rotated = sem("even_rotated")
                self.v_hi = sem("even_v_hi")
                self.v_lo = sem("even_v_lo")
                self.act_read = sem("even_act_read")
                self.dve_read = sem("even_dve_read")

            def pe(self, pe, br):
                if br == 1:
                    self.proj.wait_read(pe, 3)
                pe.wait_ge(self.rope[br], TB)
                for slot in range(5):
                    bank = self.BANKS[br][slot // 2]
                    if br == 1 and slot == 4:
                        pe.wait_ge(self.dve_read, 3 + 1)
                    for tb in range(TB):
                        m = pe.transpose(PS[:, bank, (slot % 2) * S + tb * P:(slot % 2) * S + (tb + 1) * P],
                                         R[:, tb, br * 640 + slot * P:br * 640 + (slot + 1) * P], ident)
                    if slot % 2 or slot == 4:
                        m.then_inc(self.turned, 1)

            def ready(self, pe, br):
                pe.wait_ge(self.dve_read, 3 * br + 3)

            def evac(self, eng, br, j):
                w = 2 if j < 2 else 1
                src = PS[:, self.BANKS[br][j], 0:w * S].rearrange("p (a s) -> p a s", a=w)
                eng.wait_ge(self.turned, 3 * br + j + 1)
                at = slice(5 * br + 2 * j, 5 * br + 2 * j + w)
                return QK_hi[:, at, :], even_lo(at), src

            def act(self, act, br):
                for j in range(3):
                    hi, _, src = self.evac(act, br, j)
                    act.activation(hi, src, ACT.Copy).then_inc(self.act_read, 1)
                if br == 0:
                    self.proj.wait_read(act, 3)
                    for twin in range(2):
                        act.activation(even_v_hi[:, :, :, twin], even_v_src, ACT.Copy).then_inc(self.v_hi, 1)

            def products(self, eng, link, br, tb, buf):
                x = PJ[:, tb, 768 * br:768 * br + 640].rearrange("p (h d) -> p h d", d=HD)
                t1 = rope_t1[:, buf, :].rearrange("p (h d) -> p h d", d=HD)
                t2 = rope_t2[:, buf, :].rearrange("p (h d) -> p h d", d=HD)
                w = 16 if br == 0 else 32
                groups = HD // (2 * w)
                if br == 0:
                    parts = [(slice(0, 8), gain_cos[:, tb, 0], gain_sin[:, tb, 0]),
                             (slice(8, 10), gain_cos[:, tb, 1], gain_sin[:, tb, 1])]
                else:
                    parts = [(slice(0, 10), rope_tab(2, tb), rope_tab(3, tb))]
                for heads, cos, sin in parts:
                    n = heads.stop - heads.start
                    eng.tensor_tensor(t1[:, heads], x[:, heads], cos.unsqueeze(1).to_broadcast([P, n, HD]), ALU.mult)
                    for half in range(2):
                        o = t2[:, heads].rearrange("p h (g a w) -> p h g a w", a=2, w=w)[:, :, :, half, :]
                        i = x[:, heads].rearrange("p h (g a w) -> p h g a w", a=2, w=w)[:, :, :, 1 - half, :]
                        z = sin.rearrange("p (g a w) -> p g a w", a=2, w=w)[:, :, half, :].unsqueeze(1)\
                            .to_broadcast([P, n, groups, w])
                        m = eng.tensor_tensor(o, i, z, ALU.mult)
                link(eng, m)
                return t1, t2

            def tables(self, pool):
                pool.wait_ge(self.const, 32)
                for tb in range(TB):
                    for part in range(2):
                        pool.tensor_tensor(gain_cos[:, tb, part], rope_tab(0, tb), qk_gain[:, part], ALU.mult)
                        for half in range(2):
                            o, z = (y.rearrange("p (g a w) -> p g a w", a=2, w=16)[:, :, half, :]
                                    for y in (gain_sin[:, tb, part], rope_tab(1, tb)))
                            g = qk_gain[:, part].rearrange("p (g a w) -> p g a w", a=2, w=16)[:, :, 1 - half, :]
                            m = pool.tensor_tensor(o, z, g, ALU.mult)
                m.then_inc(self.tables_ready, 1)

            def act_squares(self, act):
                self.proj.wait_read(act, 2)
                act.activation(R[:, :, 0:640], PJ[:, :, 0:640], ACT.Square).then_inc(self.squares, 1)

            def dve_rotate(self, dve):
                self.proj.wait_read(dve, 2)
                dve.wait_ge(self.tables_ready, 1)
                t1, t2 = self.products(dve, dlink, 0, 0, 0)
                dlink(dve, dve.tensor_tensor(t1, t1, t2, ALU.add))
                dve.wait_ge(self.squares, 1)
                for tb in range(TB):
                    m = dve.tensor_reduce(ss[:, tb * 10:(tb + 1) * 10],
                                          R[:, tb, 0:640].rearrange("p (h d) -> p h d", d=HD), AX_X, ALU.add)
                dlink(dve, m)
                dlink(dve, dve.tensor_scalar(ss[:, 0:20], ss[:, 0:20], 1.0 / HD, EPS_RMS, ALU.mult, ALU.add))
                rsqrt(dve, ss[:, 0:20], 20)
                for tb in range(TB):
                    if tb:
                        dve.wait_ge(self.rotated, 1)
                    t1, r, rs = rope_t1[:, tb, :], R[:, tb, 0:640], ss[:, tb * 10:(tb + 1) * 10]
                    dve.tensor_tensor(r[:, 0:512].rearrange("p (s b d) -> p s b d", b=2, d=HD),
                                      t1[:, 0:512].rearrange("p (b s d) -> p s b d", b=2, d=HD),
                                      rs[:, 0:8].rearrange("p (b s) -> p s b", b=2).unsqueeze(3).to_broadcast([P, 4, 2, HD]),
                                      ALU.mult)
                    dve.tensor_tensor(r[:, 512:640].rearrange("p (h d) -> p h d", d=HD),
                                      t1[:, 512:640].rearrange("p (h d) -> p h d", d=HD),
                                      rs[:, 8:10].unsqueeze(2).to_broadcast([P, 2, HD]), ALU.mult)\
                       .then_inc(self.rope[0], 1)

            def pool(self, pool):
                self.proj.wait_read(pool, 2)
                pool.wait_ge(self.tables_ready, 1)
                t1, t2 = self.products(pool, plink, 0, 1, 1)
                pool.tensor_tensor(t1, t1, t2, ALU.add).then_inc(self.rotated, 1)
                self.proj.wait_read(pool, 3)
                pool.wait_ge(self.rope[0], TB)
                for tb in range(TB):
                    if tb:
                        pool.wait_ge(self.rope[1], tb)
                    self.products(pool, plink, 1, tb, 1)
                    t1, t2, r = rope_t1[:, 1, :], rope_t2[:, 1, :], R[:, tb, 640:1280]
                    pool.tensor_tensor(r[:, 0:512].rearrange("p (s b d) -> p b s d", b=2, d=HD),
                                       t1[:, 0:512].rearrange("p (b s d) -> p b s d", b=2, d=HD),
                                       t2[:, 0:512].rearrange("p (b s d) -> p b s d", b=2, d=HD), ALU.add)
                    pool.tensor_tensor(r[:, 512:640], t1[:, 512:640], t2[:, 512:640], ALU.add).then_inc(self.rope[1], 1)

            def dve(self, dve, br):
                for j in range(3):
                    hi, lo, src = self.evac(dve, br, j)
                    dve.wait_ge(self.act_read, 3 * br + j + 1)
                    dve.tensor_tensor(lo, src, hi.bitcast(F32), ALU.subtract).then_inc(self.dve_read, 1)
                if br == 0:
                    for twin in range(2):
                        dve.wait_ge(self.v_hi, twin + 1)
                        dve.tensor_tensor(even_v_lo[:, :, :, twin], even_v_src, even_v_hi[:, :, :, twin].bitcast(F32),
                                          ALU.subtract).then_inc(self.v_lo, 1)

        stats_done = sem("stats_done")

        def stats_of(dve, ready):
            def stats(q, tb, half):
                dve.wait_ge(ready, q + 1)
                dve.bn_stats(bn[:, tb, half, :], X[:, tb, half * 512:(half + 1) * 512]).then_inc(stats_done, 1)
            return stats

        def layer_norm(dve, at, g, b, rows_in, done):
            dve.wait_ge(stats_done, 4 * (at + 1))
            for tb in range(TB):
                m = dve.bn_aggr(mv[:, tb, :], bn[:, tb, :, :].rearrange("p a b -> p (a b)"))
            dlink(dve, m)
            dlink(dve, dve.tensor_scalar(ss[:, 0:2], mv[:, :, 1], EPS_LN, None, ALU.add))
            rsqrt(dve, ss[:, 0:2], 2)
            dve.wait_ge(rows_in, 32)
            for tb, half in QUARTERS:
                f = slice(half * 512, (half + 1) * 512)
                x = X[:, tb, f]
                dlink(dve, dve.scalar_tensor_tensor(x, x, mv[:, tb, 0:1], g[:, f], ALU.subtract, ALU.mult))
                dve.scalar_tensor_tensor(x, x, ss[:, tb:tb + 1], b[:, f], ALU.mult, ALU.add).then_inc(done, 1)

        class FinalNorms:

            def __init__(self):
                self.square = sem("final_square")

            def act(self, act):
                for q, (tb, half) in enumerate(ffn_order):
                    act.wait_ge(final_x, q + 1)
                    act.activation(T[:, 2 * q:2 * q + 2, :], X[:, tb, half * 512:(half + 1) * 512].rearrange(
                        "p (a s) -> p a s", a=2), ACT.Square, scale=1.0 / 32.0,
                        accum_out=ss[:, 2 * half + tb:2 * half + tb + 1]).then_inc(self.square, 1)

            def stats_of(self, dve, g_norm, rows_in):
                def stats(q, tb, half):
                    f = slice(half * 512, (half + 1) * 512)
                    if q == 0:
                        dve.wait_ge(rows_in, 48)
                    dve.wait_ge(final_x, q + 1)
                    dlink(dve, dve.tensor_tensor(XN[:, tb, f], X[:, tb, f], g_norm[:, f], ALU.mult))
                    dve.bn_stats(bn[:, tb, half, :], XN[:, tb, f]).then_inc(stats_done, 1)
                return stats

            def dve(self, dve, g, b, done):
                dve.wait_ge(stats_done, 4)
                for tb in range(TB):
                    m = dve.bn_aggr(mv[:, tb, :], bn[:, tb, :, :].rearrange("p a b -> p (a b)"))
                dlink(dve, m)
                dve.wait_ge(self.square, 4)
                dlink(dve, dve.scalar_tensor_tensor(ss[:, 0:2], ss[:, 0:2], EPS_RMS, ss[:, 2:4], ALU.add, ALU.add))
                dlink(dve, dve.scalar_tensor_tensor(ss[:, 0:2], ss[:, 0:2], EPS_LN, mv[:, :, 1], ALU.mult, ALU.add))
                rsqrt(dve, ss[:, 0:2], 2)
                for tb, half in QUARTERS:
                    f = slice(half * 512, (half + 1) * 512)
                    x = X[:, tb, f]
                    dlink(dve, dve.scalar_tensor_tensor(x, XN[:, tb, f], mv[:, tb, 0:1], g[:, f], ALU.subtract, ALU.mult))
                    dve.scalar_tensor_tensor(x, x, ss[:, tb:tb + 1], b[:, f], ALU.mult, ALU.add).then_inc(done, 1)

        QA, KA, VA, FA = 0, 512, 1024, 1536
        QR, FR, IR, GR = 1544, 2056, 2568, 3080

        class FoxGates:

            def __init__(self):
                self.wf_in = sem("fox_wf_in")
                self.t_ready = sem("fox_t_ready")
                self.f_done = sem("fox_f_done")
                self.f_chain = sem("fox_f_chain")
                self.c_ready = sem("fox_c_ready")
                self.c_turned = sem("fox_c_turned")
                self.cq_ready = sem("fox_cq_ready")
                self.c_wide = sem("fox_c_wide")
                self.bias_done = sem("fox_bias_done")

            def pe_gates(self, pe):
                pe.wait_ge(self.wf_in, 32)
                pe.wait_ge(self.t_ready, 1)
                for k in range(KC):
                    m = pe.matmul(PS[0:8, 2, 0:S], wf[:, k, :], T[:, k, :], start=k == 0, stop=k == KC - 1)
                m.then_inc(self.f_done, 1)

            def act_z(self, act):
                act.wait_ge(self.f_done, 1)
                alink(act, act.activation(f_z, PS[0:8, 2, 0:S], ACT.Identity, bias=fbias[:, 0:1]))

            def dve_chain(self, dve):
                dve.wait_ge(self.f_chain, 1)
                dlink(dve, dve.tensor_scalar(f_m, f_z, 0.0, None, ALU.min))
                dlink(dve, dve.tensor_tensor(f_m, f_m, f_a, ALU.subtract))
                for c in range(4):
                    dlink(dve, dve.tensor_tensor_scan(f_c[:, c * 64:(c + 1) * 64], f_m[:, c * 64:(c + 1) * 64],
                                                      zeros[0:8, :], 0.0 if c == 0 else f_c[:, c * 64 - 1:c * 64],
                                                      ALU.add, ALU.add))
                dlink(dve, dve.tensor_scalar(f_m, f_c, -8.0, None, ALU.mult))
                dve.tensor_scalar(f_c, f_c, 8.0, None, ALU.mult).then_inc(self.c_ready, 1)

            def pe_turn(self, pe):
                pe.wait_ge(self.c_ready, 1)
                for tb in range(TB):
                    m = pe.transpose(PS[:, 2, tb * 8:(tb + 1) * 8], f_c[:, tb * P:(tb + 1) * P],
                                     consts[0:8, C_IDENT:C_IDENT + 8])
                m.then_inc(self.c_turned, 1)

            def dve_turn(self, dve):
                dve.wait_ge(self.c_turned, 1)
                dve.tensor_copy(cq[:, :, :], PS[:, 2, 0:16].rearrange("p (t h) -> p t h", t=TB)).then_inc(self.cq_ready, 1)

            def pe_wide(self, pe, pair):
                if pair >= 2:
                    pe.wait_ge(self.bias_done, pair - 1)
                for a in range(2):
                    m = pe.matmul(PS[:, pair % 2, a * S:(a + 1) * S], sel[:, 2 * pair + a, :], f_m, start=True, stop=True)
                m.then_inc(self.c_wide, 1)

            def dve_wide(self, dve, pair):
                dve.wait_ge(self.cq_ready, 1)
                dve.wait_ge(self.c_wide, pair + 1)
                for a in range(2):
                    h = 2 * pair + a
                    for tb, (at, n) in enumerate(((0, P), (P, S))):
                        m = dve.scalar_tensor_tensor(fox_bias[h][:, at:at + n], PS[:, pair % 2, a * S:a * S + n],
                                                     cq[:, tb, h:h + 1], causal_mask[:, tb, 0:n], ALU.add, ALU.add)
                m.then_inc(self.bias_done, 1)

        class Recurrence:

            def __init__(self, proj):
                self.proj = proj
                self.q_ready = sem("hg_q_ready")
                self.gate_ready = sem("hg_gate_ready")
                self.l_ready = sem("hg_l_ready")
                self.k_arg = sem("hg_k_arg")
                self.k_ready = sem("hg_k_ready")
                self.b_ready = sem("hg_b_ready")
                self.d_ready = sem("hg_d_ready")
                self.e_ready = sem("hg_e_ready")
                self.kq_ready = sem("hg_kq_ready")
                self.st_zero = sem("hg_st_zero")
                self.mm_done = sem("hg_mm_done")
                self.read_done = sem("hg_read_done")
                self.o_done = sem("hg_o_done")

            def depth(self, n):
                return hg_f if n and n % 2 == 0 else hg_d

            def pool(self, pool):
                pool.memset(hg_st[:, :, :], 0.0).then_inc(self.st_zero, 1)
                pool.wait_ge(self.b_ready, 1)
                for n, m in enumerate((64,) + LEVELS):
                    b = hg_b.rearrange("p h t -> p (h t)")
                    d = self.depth(n).rearrange("p h t -> p (h t)")
                    if n == 0:
                        w = 64
                        ref = b.rearrange("p (c w) -> p c w", w=w)[:, :, w - 1:w]
                    else:
                        w = 2 * m
                        ref = b.rearrange("p (c w) -> p c w", w=w)[:, :, m - 1:m]
                        pool.wait_ge(self.e_ready, max(n - 1, 1))
                        if n == 2:
                            pool.wait_ge(self.kq_ready, 2)
                    pool.tensor_tensor(d.rearrange("p (c w) -> p c w", w=w), b.rearrange("p (c w) -> p c w", w=w),
                                       ref.to_broadcast([P, 1024 // w, w]), ALU.subtract).then_inc(self.d_ready, 1)

            def act_silu_q(self, act):
                self.proj.wait_read(act, 6)
                act.activation(hg_q, hg_q, ACT.Silu).then_inc(self.q_ready, 1)

            def act_silu_gate(self, act):
                self.proj.wait_read(act, 11)
                act.activation(hg_gate, hg_gate, ACT.Silu).then_inc(self.gate_ready, 1)

            def act_gates(self, act, fox):
                act.activation(f_a, f_z, ACT.Abs)
                self.proj.wait_read(act, 2)
                alink(act, act.activation(hg_d, hg_f, ACT.Abs))
                act.activation(f_a, f_a, ACT.Exp, scale=-1.0)
                alink(act, act.activation(hg_d, hg_d, ACT.Exp, scale=-1.0))
                act.activation(f_a, f_a, ACT.Ln, bias=1.0).then_inc(fox.f_chain, 1)
                act.activation(hg_d, hg_d, ACT.Ln, bias=1.0).then_inc(self.l_ready, 1)

            def dve_gates(self, dve):
                self.proj.wait_read(dve, 2)
                dve.tensor_scalar(hg_b, hg_f, 0.0, None, ALU.min)
                dlink(dve, dve.tensor_scalar(hg_k, hg_f, 0.0, -1.0, ALU.max, ALU.mult))
                dve.wait_ge(self.l_ready, 1)
                dve.tensor_tensor(hg_k, hg_k, hg_d, ALU.subtract).then_inc(self.k_arg, 1)
                dlink(dve, dve.tensor_tensor(hg_b, hg_b, hg_d, ALU.subtract))
                b = hg_b.rearrange("p h t -> p (h t)")
                for c in range(16):
                    m = dve.tensor_tensor_scan(b[:, c * 64:(c + 1) * 64], b[:, c * 64:(c + 1) * 64], zeros, 0.0,
                                               ALU.add, ALU.add)
                m.then_inc(self.b_ready, 1)

            def act_k(self, act):
                act.wait_ge(self.k_arg, 1)
                act.activation(hg_k, hg_k, ACT.Exp).then_inc(self.k_ready, 1)

            def pe_diag(self, pe):
                pe.wait_ge(self.k_ready, 1)
                pe.wait_ge(self.q_ready, 1)
                for tb in range(TB):
                    for h in range(4):
                        m = pe.matmul(PS[:, 4 + tb, h * P:(h + 1) * P], hg_k[:, h, tb * P:(tb + 1) * P],
                                      hg_q[:, h, tb * P:(tb + 1) * P], start=True, stop=True)
                m.then_inc(self.mm_done, 1)

            def dve_diag(self, dve):
                dve.wait_ge(self.mm_done, 1)
                dve.wait_ge(self.st_zero, 1)
                eye = ident.unsqueeze(1).to_broadcast([P, 4, P]).bitcast(U32)
                st = hg_st.rearrange("p (h t) x -> p t h x", t=TB)
                for tb in range(TB):
                    m = dve.copy_predicated(st[:, tb], eye, PS[:, 4 + tb, :].rearrange("p (h x) -> p h x", h=4))
                m.then_inc(self.read_done, 1)

            def act_chunks(self, act):
                act.wait_ge(self.d_ready, 1)
                act.activation(hg_f, hg_b, ACT.Exp)
                act.activation(hg_e, hg_d, ACT.Exp, scale=-1.0).then_inc(self.e_ready, 1)

            def dve_chunks(self, dve):
                dve.wait_ge(self.e_ready, 1)
                dve.wait_ge(self.k_ready, 1)
                dve.wait_ge(self.q_ready, 1)
                dve.tensor_tensor(hg_kh, hg_k, hg_e, ALU.mult)
                dve.tensor_tensor(hg_qh, hg_q, hg_f, ALU.mult).then_inc(self.kq_ready, 1)

            def pe_64(self, pe):
                pe.wait_ge(self.kq_ready, 1)
                for h in range(4):
                    for tb in range(TB):
                        m = pe.matmul(PS[:, 3, (2 * h + tb) * 64:(2 * h + tb + 1) * 64],
                                      hg_kh[:, h, tb * P:(tb + 1) * P], hg_qh[:, h, tb * P + 64:(tb + 1) * P],
                                      start=True, stop=True)
                m.then_inc(self.mm_done, 1)

            def dve_64(self, dve):
                dve.wait_ge(self.mm_done, 2)
                dve.wait_ge(self.read_done, 1)
                dve.tensor_copy(hg_st[0:64, :, 64:128], PS[0:64, 3, :].rearrange("p (b x) -> p b x", b=8))\
                   .then_inc(self.read_done, 1)
                dve.wait_ge(self.kq_ready, 1)
                dve.tensor_tensor(hg_kh[:, :, 0:64], hg_kh[:, :, 0:64], hg_f[:, :, 127:128].to_broadcast([P, 4, 64]),
                                  ALU.mult)
                dve.tensor_tensor(hg_qh[:, :, 192:256], hg_qh[:, :, 192:256],
                                  hg_f[:, :, 191:192].to_broadcast([P, 4, 64]), ALU.mult).then_inc(self.kq_ready, 1)

            def pe_128(self, pe):
                pe.wait_ge(self.kq_ready, 2)
                pe.wait_ge(self.read_done, 2)
                for h in range(4):
                    m = pe.matmul(PS[:, 3, h * P:(h + 1) * P], hg_kh[:, h, 0:P], hg_qh[:, h, P:S], start=True, stop=True)
                m.then_inc(self.mm_done, 1)

            def dve_128(self, dve):
                dve.wait_ge(self.mm_done, 3)
                dve.tensor_copy(hg_s2, PS[:, 3, :].rearrange("p (h x) -> p h x", h=4)).then_inc(self.read_done, 1)

            def cut(self, x, n):
                return x.rearrange("p h t -> p (h t)").rearrange("p (c w) -> p c w", w=2 * LEVELS[n])

            def act_level(self, act, n):
                m = LEVELS[n]
                act.wait_ge(self.d_ready, n + 2)
                act.wait_ge(self.kq_ready, n + 2 if n else 1)
                d, e = self.cut(self.depth(n + 1), n), self.cut(hg_e, n)
                act.activation(e[:, :, 0:m], d[:, :, 0:m], ACT.Exp, scale=-1.0)
                act.activation(e[:, :, m:2 * m], d[:, :, m:2 * m], ACT.Exp).then_inc(self.e_ready, 1)

            def dve_level(self, dve, n):
                m = LEVELS[n]
                dve.wait_ge(self.e_ready, n + 2)
                dve.wait_ge(self.kq_ready, n + 2)
                dve.wait_ge(self.mm_done, n + 3)
                k, q, e = self.cut(hg_k, n), self.cut(hg_q, n), self.cut(hg_e, n)
                dve.tensor_tensor(self.cut(hg_kh, n)[:, :, 0:m], k[:, :, 0:m], e[:, :, 0:m], ALU.mult)
                dve.tensor_tensor(self.cut(hg_qh, n)[:, :, m:2 * m], q[:, :, m:2 * m], e[:, :, m:2 * m],
                                  ALU.mult).then_inc(self.kq_ready, 1)

            def pe_level(self, pe, n):
                w = LEVELS[n]
                pe.wait_ge(self.kq_ready, n + 3)
                pe.wait_ge(self.read_done, n + 3)
                for h in range(4):
                    for tb in range(TB):
                        q = hg_qh[:, h, tb * P:(tb + 1) * P].rearrange("p (c w) -> p c w", w=2 * w)[:, :, w:2 * w]
                        o = PS[:, 3, (2 * h + tb) * 64:(2 * h + tb + 1) * 64].rearrange("p (c w) -> p c w", w=w)
                        m = pe.matmul(o, hg_kh[:, h, tb * P:(tb + 1) * P], q, start=True, stop=True)
                m.then_inc(self.mm_done, 1)

            def dve_level_read(self, dve, n):
                m = LEVELS[n]
                dve.wait_ge(self.mm_done, n + 4)
                dve.wait_ge(self.read_done, n + 3)
                mask = consts[:, C_LEVEL + 64 * n:C_LEVEL + 64 * (n + 1)].bitcast(U32)\
                    .rearrange("p (c w) -> p c w", w=m).unsqueeze(1).to_broadcast([P, 8, 64 // m, m])
                o = hg_st.rearrange("p b (c w) -> p b c w", w=2 * m)[:, :, :, m:2 * m]
                src = PS[:, 3, :].rearrange("p (b c w) -> p b c w", b=8, w=m)
                dve.copy_predicated(o, mask, src).then_inc(self.read_done, 1)

            def pe_out(self, pe):
                pe.wait_ge(att_fox.exp_done, 8)
                self.proj.wait_read(pe, 10)
                pe.wait_ge(self.read_done, 3 + len(LEVELS))
                for tb in range(TB):
                    for h in range(4):
                        o = PS[:, tb, h * P:(h + 1) * P]
                        m = pe.matmul(o, hg_st[:, 2 * h + tb, :], V[:, tb, 512 + h * P:512 + (h + 1) * P],
                                      start=True, stop=tb == 0)
                        if tb:
                            m = pe.matmul(o, hg_s2[:, h, :], V[:, 0, 512 + h * P:512 + (h + 1) * P],
                                          start=False, stop=True)
                    m.then_inc(self.o_done, 1)

        class RecOut:

            def __init__(self, att, rec, norm):
                self.att, self.rec, self.norm = att, rec, norm
                self.fox_read = sem("mix_fox_read")
                self.gained = sem("mix_gained")
                self.rec_square = sem("mix_rec_square")

            def pool(self, pool):
                pool.wait_ge(gain_in, 16 * 8)
                pool.wait_ge(self.rec.gate_ready, 1)
                for tb in range(TB):
                    m = pool.tensor_tensor(hg_gate[:, tb, :], hg_gate[:, tb, :], rowvec[:, 1, 512:1024], ALU.mult)
                m.then_inc(self.gained, 1)

            def dve_fox(self, dve):
                dve.wait_ge(self.att.out_ready, 8)
                dve.wait_ge(self.att.inverse, 8)
                for tb in range(TB):
                    m = dve.tensor_tensor(XN[:, tb, 0:512].rearrange("p (h d) -> p h d", d=HD),
                                          PS[:, 4 + tb, :].rearrange("p (h d) -> p h d", d=HD),
                                          rinv[:, 0:8, tb:tb + 1].to_broadcast([P, 8, HD]), ALU.mult)
                dlink(dve, m)
                dve.wait_ge(self.rec.d_ready, 1 + len(LEVELS))
                sq = arena[:, 4096:5120].rearrange("p (t n) -> p t n", t=TB)
                dlink(dve, dve.tensor_tensor(sq, XN[:, :, 0:512], XN[:, :, 0:512], ALU.mult))
                dlink(dve, dve.tensor_reduce(ss[:, 0:16].rearrange("p (t h) -> p t h", t=TB),
                                             sq.rearrange("p t (h d) -> p t h d", d=HD), AX_X, ALU.add))
                dlink(dve, dve.tensor_scalar(ss[:, 0:16], ss[:, 0:16], 1.0 / HD, EPS_RMS, ALU.mult, ALU.add))
                rsqrt(dve, ss[:, 0:16], 16)
                dve.wait_ge(gain_in, 16 * 8)
                for tb in range(TB):
                    y = XN[:, tb, 0:512]
                    dlink(dve, dve.tensor_tensor(y.rearrange("p (h d) -> p h d", d=HD),
                                                 y.rearrange("p (h d) -> p h d", d=HD),
                                                 ss[:, tb * 8:tb * 8 + 8].unsqueeze(2).to_broadcast([P, 8, HD]),
                                                 ALU.mult))
                    dve.tensor_tensor(y, y, rowvec[:, 1, 0:512], ALU.mult).then_inc(self.norm.normed, 1)

            def act(self, act):
                sq = arena[:, 5120:6144].rearrange("p (t n) -> p t n", t=TB)
                for tb in range(TB):
                    act.wait_ge(self.rec.o_done, tb + 1)
                    act.activation(sq[:, tb, :], PS[:, tb, :], ACT.Square).then_inc(self.rec_square, 1)

            def dve_sums(self, dve):
                sq = arena[:, 5120:6144].rearrange("p (t n) -> p t n", t=TB)
                for tb in range(TB):
                    dve.wait_ge(self.rec_square, tb + 1)
                    m = dve.tensor_reduce(ss[:, 16 + tb * 4:20 + tb * 4], sq[:, tb, :].rearrange("p (h d) -> p h d", d=P),
                                          AX_X, ALU.add)
                dlink(dve, m)
                dlink(dve, dve.tensor_scalar(ss[:, 16:24], ss[:, 16:24], 1.0 / P, EPS_RMS, ALU.mult, ALU.add))
                rsqrt(dve, ss[:, 16:24], 8)

            def dve(self, dve):
                dve.wait_ge(self.gained, 1)
                for tb in range(TB):
                    x = XN[:, tb, 512:1024]
                    dlink(dve, dve.tensor_tensor(x.rearrange("p (h d) -> p h d", d=P),
                                                 PS[:, tb, :].rearrange("p (h d) -> p h d", d=P),
                                                 ss[:, 16 + tb * 4:20 + tb * 4].unsqueeze(2).to_broadcast([P, 4, P]),
                                                 ALU.mult))
                    dve.tensor_tensor(x, x, hg_gate[:, tb, :], ALU.mult).then_inc(self.norm.normed, 1)

        ffn_order = [(0, 0), (0, 1), (1, 0), (1, 1)]
        n_ffn1_0, n_mix_0, n_ffn2_0, n_ffn1_1, n_mix_1, n_ffn2_1 = (
            Norm(at, first_unit[name] + 1)
            for at, name in enumerate(("ffn1_0", "even_in", "ffn2_0", "ffn1_1", "odd_in", "ffn2_1")))
        n_emb, n_conv = Norm(6, first_unit["rec_in"] + 1, X), Norm(8, first_unit["conv_ffn"] + 1, X)
        n_gated = Norm(7, None, XN, (2, 3, 2, 3))
        for n in (n_ffn1_0, n_mix_0, n_ffn1_1, n_mix_1):
            n.order = ffn_order
        for n in (n_ffn2_0, n_ffn2_1):
            n.order = QUARTERS
        final_x = sem("final_x")
        mixed_x = sem("mixed_x")
        conv_x = sem("conv_x")
        out_x = sem("out_x")
        final_norms = FinalNorms()

        def even_slot(g, slot, tokens):
            base = ((g % 8) // 4) * HD
            return (QK_hi[base:base + HD, slot, tokens],
                    even_lo(slice(slot, slot + 1))[base:base + HD, 0, tokens])

        def even_q(g, tb):
            return even_slot(g, 5 * (g // 8) + g % 4, slice(tb * P, (tb + 1) * P))

        def even_k(g):
            return even_slot(g, 5 * (g // 8) + 4, slice(0, S))

        def even_v(g, kb):
            br, h = divmod(g, 8)
            return [z[:, 2 * kb + br, h // 4].rearrange("p w d -> p (w d)") for z in (even_v_hi, even_v_lo)]

        def odd_slot(g, slot, tokens):
            rows = slice((g % 2) * HD, (g % 2 + 1) * HD)
            return QK_hi[rows, slot, tokens], odd_lo(slice(slot, slot + 1))[rows, 0, tokens]

        def fox_part(g, slot, lo, tokens):
            rows = slice((g % 2) * HD, (g % 2 + 1) * HD)
            return QK_hi[rows, slot + g // 2, tokens], lo[rows, g // 2, tokens]

        att_even = Attention("att_even", 16, even_q, even_k, even_v, lambda g: None if g < 8 else win_mask,
                             (2, 3),
                             sink_of=lambda g: None if g < 8 else sink[:, g - 8:g - 7])
        att_odd = Attention("att_odd", 16,
                            lambda g, tb: odd_slot(g, g // 2, slice(tb * P, (tb + 1) * P)),
                            lambda g: odd_slot(g, 8 + g // 2, slice(0, S)),
                            lambda g, kb: [z[:, kb, g // 2 * P:(g // 2 + 1) * P] for z in (V_hi, odd_v_lo)],
                            lambda g: bias_flat[:, g], (2, 3), out_step=8,
                            rows_reversed=True, inputs_free=first_unit["odd_in"] + 12)
        att_fox = Attention("att_fox", 8,
                            lambda g, tb: fox_part(g, 0, fox_q_lo, slice(tb * P, (tb + 1) * P)),
                            lambda g: fox_part(g, 4, fox_k_lo, slice(0, S)),
                            lambda g, kb: (V_hi[:, kb, g * HD:(g + 1) * HD], fox_v_lo[:, kb, g * HD:(g + 1) * HD]),
                            lambda g: fox_bias[g], (2, 2), causal=True)
        Feat, Tok = Proj.Feat, Proj.Tok
        even_in = Proj("even_in", io["even_w_in"][0], n_mix_0,
                       [Tok(0, 6, 0, PJ[:, :, 0:512]), Tok(512, 4, 0, PJ[:, :, 512:1024]),
                        Tok(1024, 6, 1, PJ[:, :, 1024:1536])])
        even_turn = EvenTurn(even_in)

        def odd_qk(first, j, bank, free):
            at = slice(first + 2 * j, first + 2 * j + 2)
            return Feat((first // 8) * DM + j * 256, bank, free, QK_hi[:, at, :], odd_lo(at))

        def odd_v(c, free):
            f = slice(c * 512, (c + 1) * 512)
            return Tok(2 * DM + c * 512, 6, free, V_hi[:, :, f], odd_v_lo[:, :, f])

        odd_in = Proj("odd_in", io["odd_w_qkv"][0], n_mix_1,
                      [odd_v(0, 0), odd_qk(0, 0, 6, 1), odd_qk(8, 0, 7, 1), odd_qk(0, 1, 6, 2), odd_qk(8, 1, 7, 3),
                       odd_qk(0, 2, 6, 4), odd_qk(8, 2, 7, 5), odd_v(1, 7), odd_qk(0, 3, 6, 8), odd_qk(8, 3, 7, 8)])

        def rec_feat(col, j, bank, free, slot, lo=None):
            at = slice(slot + 2 * j, slot + 2 * j + 2)
            if lo is None:
                return Feat(col + 256 * j, bank, free, QKT[:, at, :])
            return Feat(col + 256 * j, bank, free, QK_hi[:, at, :], lo[:, 2 * j:2 * j + 2, :])

        rec_in = Proj("rec_in", io["w_in_2"][0], n_emb,
                      [rec_feat(FR, 0, 6, 0, 12), rec_feat(FR, 1, 7, 0, 12),
                       rec_feat(QA, 0, 6, 1, 0, fox_q_lo), rec_feat(KA, 0, 7, 2, 4, fox_k_lo),
                       rec_feat(QR, 0, 6, 3, 8), rec_feat(QR, 1, 7, 4, 8),
                       Tok(VA, 6, 6, V_hi[:, :, 0:512], fox_v_lo),
                       rec_feat(QA, 1, 6, 7, 0, fox_q_lo), rec_feat(KA, 1, 7, 7, 4, fox_k_lo), Tok(IR, 6, 9, V[:, :, 512:1024]),
                       Tok(GR, 6, 10, hg_gate)])
        fox = FoxGates()
        rec = Recurrence(rec_in)
        rec_out = RecOut(att_fox, rec, n_gated)
        ffn1_0 = Ffn(0, "ffn1_0", io["ffn1_w_gate"][0], io["ffn1_w_up"][0], io["ffn1_w_down"][0], n_ffn1_0, n_mix_0.x_ready)
        even_out = OutProj("even_out", io["even_w_out"][0], att_even.ready, n_ffn2_0.x_ready, 0, ((6, 7), (0, 1)))
        ffn2_0 = Ffn(1, "ffn2_0", io["ffn2_w_gate"][0], io["ffn2_w_up"][0], io["ffn2_w_down"][0], n_ffn2_0, n_ffn1_1.x_ready)
        ffn1_1 = Ffn(2, "ffn1_1", io["ffn1_w_gate"][1], io["ffn1_w_up"][1], io["ffn1_w_down"][1], n_ffn1_1, n_mix_1.x_ready)
        odd_out = OutProj("odd_out", io["odd_w_out"][0], att_odd.ready, n_ffn2_1.x_ready, 1, ((6, 7), (0, 1)))
        ffn2_1 = Ffn(3, "ffn2_1", io["ffn2_w_gate"][1], io["ffn2_w_up"][1], io["ffn2_w_down"][1], n_ffn2_1, final_x)
        rec_proj = OutProj("rec_out", io["w_o_2"][0], n_gated.ready, mixed_x, 2, ((4, 5), (6, 7)), alpha=ALPHA)
        w_up = io["w_up_2"][0]
        conv_ffn = Ffn(4, "conv_ffn", w_up[:, 0:FF], w_up[:, FF:2 * FF], io["w_down_2"][0], n_conv, conv_x, conv=True)

        def att(first, end):
            return [("att", s) for s in range(first, end)]

        EVEN = [("unit", n) for n in range(4)] + [("rotate", 0), ("unit", 4), ("unit", 5), ("turn", 0)] \
            + att(0, 7) + [("turn", 1)] + att(7, 8) + [("split", 0)] + att(8, 9) + [("split", 1)] + att(9, 16) \
            + [("out", 0)] + att(16, 19) + [("out", 1)] + att(19, 22) + [("out", 2), ("out", 3)]
        ODD = [("unit", n) for n in range(4)]
        for s in range(8):
            ODD += [("att", s), ("unit", 4 + s)]
        ODD += att(8, 16) + [("out", 0)] + att(16, 19) + [("out", 1)] + att(19, 23) + [("out", 2), ("out", 3)]
        ODD_NEEDS = {0: 3, 4: 5, 8: 8, 12: 10}
        REC = [("unit", 0), ("unit", 1), ("unit", 2), ("fox_gates", 0), ("fox_z", 0), ("fox_chain", 0), ("gates", 0),
               ("unit", 3), ("k", 0), ("fox_turn", 0), ("unit", 4), ("fox_wide", 0), ("fox_wide", 1),
               ("unit", 5), ("fox_wide", 2), ("fox_wide", 3), ("silu_q", 0), ("chunks", 0),
               ("unit", 6), ("diag", 0), ("fox", 0), ("unit", 7), ("mm64", 0), ("read64", 0), ("fox", 1),
               ("unit", 8), ("mm128", 0), ("read128", 0), ("level", 0), ("fox", 2), ("fox", 3),
               ("unit", 9), ("level_mm", 0), ("level_read", 0), ("level", 1), ("fox", 4),
               ("unit", 10), ("level_mm", 1), ("level_read", 1), ("level", 2), ("fox", 5), ("level_mm", 2), ("level_read", 2), ("level", 3), ("fox", 6), ("unit", 11), ("fox", 7), ("level_mm", 3),
               ("level_read", 3), ("level", 4), ("fox", 8), ("fox", 9), ("level_mm", 4), ("level_read", 4),
               ("level", 5), ("unit", 12), ("fox", 10), ("fox", 11), ("level_mm", 5), ("level_read", 5), ("fox", 12),
               ("fox_out", 0), ("rec_mm", 0), ("unit", 13), ("gated", 0), ("silu_gate", 0), ("rec_sums", 0), ("split", 1),
               ("rec_out", 0), ("rec_proj", 0), ("rec_proj", 1), ("gated", 1), ("rec_proj", 2),
               ("rec_proj", 3)]

        x_in = [sem(f"x_in{tb}") for tb in range(TB)]
        consts_in = sem("consts_in")
        ident_in = sem("ident_in")
        rows_in = sem("rows_in")
        rows_turned = sem("rows_turned")
        cols_ready = sem("cols_ready")
        sink_in = sem("sink_in")
        bias_in = sem("bias_in")
        bias_masked = sem("bias_masked")
        vec_in = sem("vec_in")
        vec2_in = sem("vec2_in")
        vec3_in = sem("vec3_in")
        out_stored = sem("out_stored")

        conv_rows = pt_sb[0:44, 0, :, :].rearrange("p a b -> p (a b)").rearrange("p (a n) -> p a n", a=4)

        block = ctx.enter_context(nc.Block())

        @block.sync
        def _(sp):
            for tb in range(TB):
                sp.dma_start(X[:, tb, :], io["x"][0, tb * P:(tb + 1) * P, :]).then_inc(x_in[tb], 16)
            sp.dma_start(ident, io["consts"][:, 0:P]).then_inc(ident_in, 16)
            ffn1_0.sp(sp)
            even_in.sp(sp)
            even_out.sp(sp)
            ffn2_0.sp(sp)
            ffn1_1.sp(sp)
            odd_in.sp(sp)
            odd_out.sp(sp)
            ffn2_1.sp(sp)
            rec_in.sp(sp)
            rec_proj.sp(sp)
            conv_ffn.sp(sp)
            for q, (tb, half) in enumerate(QUARTERS):
                sp.wait_ge(out_x, q + 1)
                f = slice(half * 512, (half + 1) * 512)
                sp.dma_start(out[0, tb * P:(tb + 1) * P, f], X[:, tb, f]).then_inc(out_stored, 16)
            sp.wait_ge(out_stored, 16 * 4)

        @block.gpsimd
        def _(pool):
            def gain(at, name, layer):
                if at >= 2:
                    pool.wait_ge(Norm.normed, 4 * (at - 1))
                if at:
                    pool.wait_ge(gain_in, 16 * at)
                pool.dma_start(rowvec[:, at % 2, :], io[name][layer].partition_broadcast(P)).then_inc(gain_in, 16)

            gain(0, "ffn1_norm", 0)
            pool.wait_ge(w_lo_ready, 4)
            gain(1, "mix_norm", 0)
            pool.dma_start(consts[:, P:], io["consts"][:, P:C_SEL]).then_inc(consts_in, 16)
            pool.dma_start(conv_rows[:, 0:3, :], io["conv_w_2"][0].rearrange("a (k n) -> k a n", n=P)).then_inc(rows_in, 16)
            pool.dma_start(conv_rows[:, 3, :], io["conv_b_2"][0].rearrange("(k n) -> k n", n=P)).then_inc(rows_in, 16)
            pool.dma_start(sink[:, :], io["b_sink"][0].partition_broadcast(P)).then_inc(sink_in, 16)
            pool.dma_start(fbias[:, :], io["fox_f_bias_2"][0].rearrange("(h a) -> h a", a=1)).then_inc(sink_in, 16)
            pool.dma_start(qk_gain[:, 0], io["a_q_norm"][0].partition_broadcast(P)).then_inc(even_turn.const, 16)
            pool.dma_start(qk_gain[:, 1], io["a_k_norm"][0].partition_broadcast(P)).then_inc(even_turn.const, 16)
            gain(2, "ffn2_norm", 0)
            pool.wait_ge(consts_in, 16)
            even_turn.tables(pool)
            even_turn.pool(pool)
            gain(3, "ffn1_norm", 1)
            pool.wait_ge(att_even.out_ready, 16)
            table = io["c_rel_bias"].tensor
            for h in range(16):
                for r in range(4):
                    tb, base = divmod(r * GRID_W, P)
                    src = bass.AP(tensor=table, offset=h * REL_H * REL_W + (7 - r) * REL_W - 48,
                                  ap=[[1, GRID_W], [REL_W, 4], [1, GRID_W]])
                    pool.dma_start(bias[base:base + GRID_W, h, tb, :].rearrange("p (a k) -> p a k", a=4), src)\
                        .then_inc(bias_in, 16)
            pool.wait_ge(bias_in, 16 * 64)
            for h in range(16):
                for tb in range(TB):
                    plink(pool, pool.tensor_scalar(bias[:, h, tb, :], bias[:, h, tb, :], 8.0, None, ALU.mult))
                    pool.tensor_tensor(bias[:, h, tb, :], bias[:, h, tb, :], nb_mask, ALU.add).then_inc(bias_masked, 1)
            gain(4, "mix_norm", 1)
            pool.wait_ge(att_odd.out_ready, 16)
            gain(5, "ffn2_norm", 1)
            pool.wait_ge(Norm.normed, 4 * 6)
            pool.dma_start(rowvec[:, 0, :], io["final_norm"].partition_broadcast(P)).then_inc(vec_in, 16)
            pool.dma_start(rowvec[:, 1, :], io["ln_emb_g_2"].partition_broadcast(P)).then_inc(vec_in, 16)
            pool.wait_ge(att_odd.out_ready, 16)
            pool.dma_start(V[:, 0, :], io["ln_emb_b_2"].partition_broadcast(P)).then_inc(vec_in, 16)
            pool.wait_ge(n_emb.normed, 7 * 4)
            pool.dma_start(wf, io["w_in_2"][0, :, FA:FA + 8].rearrange("(k p) n -> p k n", p=P)).then_inc(fox.wf_in, 16)
            pool.dma_start(sel, io["consts"][0:8, C_SEL:C_N].rearrange("p (h q) -> p h q", h=8)).then_inc(fox.wf_in, 16)
            pool.wait_ge(n_emb.lo, 7 * 4)
            pool.tensor_tensor(T[:, :, :], h_hi[:, :, :].bitcast(F32), h_lo[:, :, :].bitcast(F32), ALU.add)\
                .then_inc(fox.t_ready, 1)
            rec.pool(pool)
            pool.wait_ge(att_fox.scores, 8)
            pool.dma_start(rowvec[:, 1, 0:512], io["fox_norm_g_2"][0].partition_broadcast(P)).then_inc(gain_in, 16)
            pool.dma_start(rowvec[:, 1, 512:1024], io["hgrn_norm_g_2"][0].partition_broadcast(P)).then_inc(gain_in, 16)
            rec_out.pool(pool)
            pool.wait_ge(att_fox.out_ready, 8)
            pool.dma_start(rowvec[:, 0, :], io["ln_mix_g_2"][0].partition_broadcast(P)).then_inc(vec2_in, 16)
            pool.wait_ge(n_gated.normed, 8 * 4)
            pool.dma_start(rowvec[:, 1, :], io["ln_mix_b_2"][0].partition_broadcast(P)).then_inc(vec2_in, 16)
            pool.wait_ge(n_conv.normed, 9 * 4)
            pool.dma_start(rowvec[:, 0, :], io["ln_ffn_g_2"][0].partition_broadcast(P)).then_inc(vec3_in, 16)
            pool.dma_start(rowvec[:, 1, :], io["ln_ffn_b_2"][0].partition_broadcast(P)).then_inc(vec3_in, 16)
            pool.wait_ge(vec3_in, 32)

        @block.scalar
        def _(act):
            n_ffn1_0.act(act, first=True)
            ffn1_0.act(act)
            n_mix_0.act(act)
            act.wait_ge(sink_in, 32)
            for what, n in EVEN:
                if what == "unit":
                    even_in.act(act, n, split=n < 4)
                elif what == "split":
                    split_hi(act, even_out.u0 + n)
                elif what == "rotate":
                    even_turn.act_squares(act)
                elif what == "turn":
                    even_turn.act(act, n)
                elif what == "att":
                    att_even.act(act, n)
                elif what == "out":
                    even_out.act(act, n)
            n_ffn2_0.act(act)
            ffn2_0.act(act)
            n_ffn1_1.act(act)
            ffn1_1.act(act)
            n_mix_1.act(act)
            for what, n in ODD:
                if what == "unit":
                    odd_in.act(act, n)
                elif what == "att":
                    att_odd.act(act, n)
                elif what == "out":
                    odd_out.act(act, n)
            n_ffn2_1.act(act)
            ffn2_1.act(act)
            final_norms.act(act)
            n_emb.act(act)
            for what, n in REC:
                if what == "unit":
                    rec_in.act(act, n, split=n < 13)
                elif what == "split":
                    split_hi(act, rec_proj.u0 + n)
                elif what == "silu_q":
                    rec.act_silu_q(act)
                elif what == "fox_z":
                    fox.act_z(act)
                elif what == "gates":
                    rec.act_gates(act, fox)
                elif what == "k":
                    rec.act_k(act)
                elif what == "chunks":
                    rec.act_chunks(act)
                elif what == "level":
                    rec.act_level(act, n)
                elif what == "fox":
                    att_fox.act(act, n)
                elif what == "silu_gate":
                    rec.act_silu_gate(act)
                elif what == "rec_sums":
                    rec_out.act(act)
                elif what == "gated":
                    n_gated.act(act, half=n)
                elif what == "rec_proj":
                    rec_proj.act(act, n)
            n_conv.act(act)
            conv_ffn.act(act)

        @block.vector
        def _(dve):
            dve.wait_ge(x_in[0], 16)
            dve.wait_ge(x_in[1], 16)
            n_ffn1_0.dve(dve, first=True)
            ffn1_0.dve(dve)
            dve.wait_ge(rows_turned, 1)
            dve.tensor_copy(convc[:, :, :], PS[:, 2, 0:176].rearrange("p (a k) -> p a k", a=4)).then_inc(cols_ready, 1)
            n_mix_0.dve(dve)
            dve.wait_ge(sink_in, 32)
            dlink(dve, dve.tensor_scalar(neg_sink[:, :], sink[:, :], -1.0, None, ALU.mult))
            for what, n in EVEN:
                if what == "unit":
                    even_in.dve(dve, n, split=n < 4)
                elif what == "split":
                    split_lo(dve, even_out.u0 + n)
                elif what == "rotate":
                    even_turn.dve_rotate(dve)
                elif what == "turn":
                    even_turn.dve(dve, n)
                elif what == "att":
                    att_even.dve(dve, n)
                elif what == "out":
                    even_out.dve(dve, n)
            n_ffn2_0.dve(dve)
            ffn2_0.dve(dve)
            n_ffn1_1.dve(dve)
            ffn1_1.dve(dve)
            n_mix_1.dve(dve)
            for what, n in ODD:
                if what == "unit":
                    odd_in.dve(dve, n)
                elif what == "att":
                    if n == 0:
                        dve.wait_ge(bias_masked, 32)
                    att_odd.dve(dve, n)
                elif what == "out":
                    odd_out.dve(dve, n)
            n_ffn2_1.dve(dve)
            ffn2_1.dve(dve, final_norms.stats_of(dve, rowvec[:, 0, :], vec_in))
            final_norms.dve(dve, rowvec[:, 1, :], V[:, 0, :], n_emb.normed)
            n_emb.dve(dve)
            for what, n in REC:
                if what == "unit":
                    rec_in.dve(dve, n, split=n < 13)
                elif what == "split":
                    split_lo(dve, rec_proj.u0 + n)
                elif what == "fox_chain":
                    fox.dve_chain(dve)
                elif what == "gates":
                    rec.dve_gates(dve)
                elif what == "fox_turn":
                    fox.dve_turn(dve)
                elif what == "fox_wide":
                    fox.dve_wide(dve, n)
                elif what == "diag":
                    rec.dve_diag(dve)
                elif what == "chunks":
                    rec.dve_chunks(dve)
                elif what == "read64":
                    rec.dve_64(dve)
                elif what == "read128":
                    rec.dve_128(dve)
                elif what == "level":
                    rec.dve_level(dve, n)
                elif what == "level_read":
                    rec.dve_level_read(dve, n)
                elif what == "fox":
                    att_fox.dve(dve, n)
                elif what == "fox_out":
                    rec_out.dve_fox(dve)
                elif what == "rec_sums":
                    rec_out.dve_sums(dve)
                elif what == "rec_out":
                    rec_out.dve(dve)
                elif what == "gated":
                    n_gated.dve(dve, half=n)
                elif what == "rec_proj":
                    rec_proj.dve(dve, n, stats_of(dve, mixed_x))
            layer_norm(dve, 1, rowvec[:, 0, :], rowvec[:, 1, :], vec2_in, n_conv.normed)
            n_conv.dve(dve)
            conv_ffn.dve(dve, stats_of(dve, conv_x))
            layer_norm(dve, 2, rowvec[:, 0, :], rowvec[:, 1, :], vec3_in, out_x)

        @block.tensor
        def _(pe):
            pe.wait_ge(ident_in, 16)
            n_ffn1_0.pe(pe)
            ffn1_0.pe(pe)
            pe.wait_ge(rows_in, 16 * 2)
            for a in range(4):
                m = pe.transpose(PS[:, 2, 44 * a:44 * (a + 1)], conv_rows[:, a, :],
                                 consts[0:44, C_IDENT:C_IDENT + 44])
            m.then_inc(rows_turned, 1)
            n_mix_0.pe(pe)
            for what, n in EVEN:
                if what == "unit":
                    even_in.pe(pe, n)
                elif what == "turn":
                    even_turn.pe(pe, n)
                elif what == "att":
                    if n in (0, 8):
                        even_turn.ready(pe, n // 8)
                    if n == 5:
                        pe.wait_ge(even_turn.v_lo, 2)
                    att_even.pe(pe, n)
                elif what == "out":
                    even_out.pe(pe, n)
            n_ffn2_0.pe(pe)
            ffn2_0.pe(pe)
            n_ffn1_1.pe(pe)
            ffn1_1.pe(pe)
            n_mix_1.pe(pe)
            for what, n in ODD:
                if what == "unit":
                    odd_in.pe(pe, n)
                elif what == "att":
                    if n in ODD_NEEDS:
                        odd_in.wait_read(pe, ODD_NEEDS[n])
                    att_odd.pe(pe, n)
                elif what == "out":
                    odd_out.pe(pe, n)
            n_ffn2_1.pe(pe)
            ffn2_1.pe(pe)
            n_emb.pe(pe)
            for what, n in REC:
                if what == "unit":
                    rec_in.pe(pe, n)
                elif what == "fox_gates":
                    fox.pe_gates(pe)
                elif what == "fox_turn":
                    fox.pe_turn(pe)
                elif what == "fox_wide":
                    fox.pe_wide(pe, n)
                elif what == "diag":
                    rec.pe_diag(pe)
                elif what == "mm64":
                    rec.pe_64(pe)
                elif what == "mm128":
                    rec.pe_128(pe)
                elif what == "level_mm":
                    rec.pe_level(pe, n)
                elif what == "fox":
                    if n == 0:
                        rec_in.wait_read(pe, 4)
                        pe.wait_ge(fox.bias_done, 4)
                    if n == 4:
                        rec_in.wait_read(pe, 9)
                        pe.wait_ge(rec.read_done, 1)
                    att_fox.pe(pe, n)
                elif what == "rec_mm":
                    rec.pe_out(pe)
                elif what == "gated":
                    n_gated.pe(pe, half=n)
                elif what == "rec_proj":
                    if n == 1:
                        rec_in.wait_read(pe, 11)
                    rec_proj.pe(pe, n)
            n_conv.pe(pe)
            conv_ffn.pe(pe)


_INS = ["x", "ffn1_norm", "ffn1_w_gate", "ffn1_w_up", "ffn1_w_down", "mix_norm", "ffn2_norm", "ffn2_w_gate",
        "ffn2_w_up", "ffn2_w_down", "even_w_in", "a_q_norm", "a_k_norm", "b_sink", "even_w_out", "odd_w_qkv",
        "c_rel_bias", "odd_w_out", "final_norm", "ln_emb_g_2", "ln_emb_b_2", "w_in_2", "fox_f_bias_2",
        "fox_norm_g_2", "hgrn_norm_g_2", "w_o_2", "ln_mix_g_2", "ln_mix_b_2", "w_up_2", "conv_w_2", "conv_b_2",
        "w_down_2", "ln_ffn_g_2", "ln_ffn_b_2"]


def kernel(**inputs):
    import numpy as _np
    import concourse.bacc as _bacc
    from concourse import mybir as _mybir
    from concourse.bass_utils import run_bass_kernel_spmd as _run

    nc = _bacc.Bacc("TRN2", target_bir_lowering=False, num_devices=1)
    arrays, io = {}, {}
    for name in _INS + ["consts"]:
        if name == "consts":
            a = constant_table()
        elif name == "c_rel_bias":
            a = _np.ascontiguousarray(inputs[name][..., ::-1])
        else:
            a = _np.ascontiguousarray(inputs[name])
        arrays[f"in_{name}_dram"] = a
        io[name] = nc.dram_tensor(f"in_{name}_dram", a.shape, _mybir.dt.from_np(a.dtype), kind="ExternalInput").ap()
    out = nc.dram_tensor("out_0_dram", (1, S, DM), F32, kind="ExternalOutput").ap()
    build(nc, io, out)
    r = _run(nc, [arrays], core_ids=[0])
    return r.results[0]["out_0_dram"]
```
